# Optimizing a Trainium2 kernel written in Bass

```python
import math
import jax
import jax.numpy as jnp
from jax import lax
import numpy as np

D_MODEL = 1024
BATCH = 1
SEQ = 512
DEPTH = 1

A_HEADS = 16
A_HEAD_DIM = 64
A_WIDTH = A_HEADS * A_HEAD_DIM
DILATED_PATTERNS = ((128, 1), (512, 4), (2048, 16))
N_BUCKETS = 32
MAX_EXACT = N_BUCKETS // 2
MAX_DISTANCE = 2048
M_HEADS = 4
M_WIDTH = 2 * D_MODEL
M_HEAD_DIM = M_WIDTH // M_HEADS
CONV_K = 4
QKV_BLOCK = 4
CHUNK = 64
EPS = 1e-6
N_IN = 4 * A_WIDTH + 3 * M_WIDTH + 2 * D_MODEL
SPLIT_POINTS = (A_WIDTH, 2 * A_WIDTH, 3 * A_WIDTH, 4 * A_WIDTH, 4 * A_WIDTH + M_WIDTH, 4 * A_WIDTH + 2 * M_WIDTH, 4 * A_WIDTH + 3 * M_WIDTH)


def rmsnorm(x, g):
    xf = x.astype(jnp.float32)
    y = xf * lax.rsqrt(jnp.mean(xf * xf, axis=-1, keepdims=True) + EPS)
    return (y * g.astype(jnp.float32)).astype(x.dtype)

def t5_bucket(dist):
    large = MAX_EXACT + (jnp.log(jnp.maximum(dist, MAX_EXACT).astype(jnp.float32) / MAX_EXACT)
                         / math.log(MAX_DISTANCE / MAX_EXACT) * (N_BUCKETS - MAX_EXACT)).astype(jnp.int32)
    return jnp.where(dist < MAX_EXACT, dist, jnp.minimum(large, N_BUCKETS - 1))

def dilated_band_attention(q, k, v, rel_bias, window, dilation):
    B, S, H, dh = q.shape
    band = window // dilation
    span = band * dilation
    s_pad = -(-S // span) * span
    L = s_pad // dilation
    nb = L // band

    def to_blocks(t):
        t = jnp.pad(t, ((0, 0), (0, s_pad - S), (0, 0), (0, 0)))
        t = t.reshape(B, L, dilation, H, dh).transpose(0, 2, 3, 1, 4)
        return t.reshape(B, dilation, H, nb, band, dh)

    def with_prev(t):
        prev = jnp.pad(t, ((0, 0), (0, 0), (0, 0), (1, 0), (0, 0), (0, 0)))[:, :, :, :-1]
        return jnp.concatenate([prev, t], axis=4)

    qb = to_blocks(q)
    kc = with_prev(to_blocks(k))
    vc = with_prev(to_blocks(v))
    logits = jnp.einsum('brhnqc,brhnkc->brhnqk', qb, kc, preferred_element_type=jnp.float32) * (dh ** -0.5)
    qi = jnp.arange(band)[:, None]
    kj = jnp.arange(2 * band)[None, :]
    delta = qi + band - kj
    bias = rel_bias.astype(jnp.float32)[t5_bucket(jnp.clip(delta, 0, band) * dilation)]
    bias = jnp.transpose(bias, (2, 0, 1))[:, None]
    key_pos = jnp.arange(nb)[:, None, None] * band + kj[None] - band
    valid = (delta >= 0) & (delta <= band) & (key_pos >= 0)
    logits = jnp.where(valid, logits + bias, -jnp.inf)
    m = jnp.max(logits, axis=-1)
    p = jnp.exp(logits - m[..., None])
    s = jnp.sum(p, axis=-1)
    o = jnp.einsum('brhnqk,brhnkc->brhnqc', p, vc.astype(jnp.float32)) / s[..., None]

    def from_blocks(t):
        t = t.reshape((B, dilation, H, L) + t.shape[5:])
        t = jnp.moveaxis(t, 3, 1)
        return t.reshape((B, s_pad, H) + t.shape[4:])[:, :S]

    return from_blocks(o), from_blocks(m), from_blocks(s)

def dilated_attention(q, k, v, rel_bias):
    B, S, H, dh = q.shape
    outs = [dilated_band_attention(q, k, v, rel_bias, w, d) for (w, d) in DILATED_PATTERNS]
    o = jnp.stack([t[0] for t in outs])
    m = jnp.stack([t[1] for t in outs])
    s = jnp.stack([t[2] for t in outs])
    wgt = jnp.exp(m - jnp.max(m, axis=0, keepdims=True)) * s
    out = jnp.sum(wgt[..., None] * o, axis=0) / jnp.sum(wgt, axis=0)[..., None]
    return out.reshape(B, S, H * dh)

def causal_depthwise_conv(x, w, b):
    S = x.shape[1]
    xp = jnp.pad(x, ((0, 0), (CONV_K - 1, 0), (0, 0)))
    y = b
    for tap in range(CONV_K):
        y = y + xp[:, tap:tap + S] * w[tap]
    return y

def block_diag_proj(x, w):
    B, S, C = x.shape
    return jnp.einsum('bsgi,gio->bsgo', x.reshape(B, S, C // QKV_BLOCK, QKV_BLOCK), w).reshape(B, S, C)

def mlstm_chunkwise(q, k, v, li, lf):
    B, S, H, dh = q.shape
    nc = S // CHUNK

    def chunks(t):
        t = t.astype(jnp.float32).reshape((B, nc, CHUNK, H) + t.shape[3:])
        return jnp.moveaxis(jnp.moveaxis(t, 1, 0), 3, 2)

    qc, kc, vc = chunks(q), chunks(k) * (dh ** -0.5), chunks(v)
    lic, lfc = chunks(li), chunks(lf)
    tril = jnp.tril(jnp.ones((CHUNK, CHUNK), dtype=bool))

    def step(carry, xs):
        C, n, m = carry
        qt, kt, vt, it, ft = xs
        b = jnp.cumsum(ft, axis=-1)
        g = b[..., -1]
        D = jnp.where(tril, b[..., :, None] - b[..., None, :] + it[..., None, :], -jnp.inf)
        inter = b + m[..., None]
        m_t = jnp.maximum(inter, jnp.max(D, axis=-1))
        qk = jnp.einsum('bhtd,bhsd->bhts', qt, kt) * jnp.exp(D - m_t[..., None])
        w_inter = jnp.exp(inter - m_t)
        num = w_inter[..., None] * jnp.einsum('bhtd,bhde->bhte', qt, C) + jnp.einsum('bhts,bhse->bhte', qk, vt)
        den = w_inter * jnp.einsum('bhtd,bhd->bht', qt, n) + jnp.sum(qk, axis=-1)
        h = num / jnp.maximum(jnp.abs(den), jnp.exp(-m_t))[..., None]
        to_end = g[..., None] - b + it
        m_new = jnp.maximum(g + m, jnp.max(to_end, axis=-1))
        w_s = jnp.exp(to_end - m_new[..., None])
        decay = jnp.exp(g + m - m_new)
        C_new = decay[..., None, None] * C + jnp.einsum('bhsd,bhse->bhde', kt * w_s[..., None], vt)
        n_new = decay[..., None] * n + jnp.einsum('bhs,bhsd->bhd', w_s, kt)
        return (C_new, n_new, m_new), h

    init = (jnp.zeros((B, H, dh, dh), jnp.float32), jnp.zeros((B, H, dh), jnp.float32), jnp.zeros((B, H), jnp.float32))
    _, h = lax.scan(step, init, (qc, kc, vc, lic, lfc))
    return jnp.transpose(h, (1, 0, 3, 2, 4)).reshape(B, S, H, dh)

def mlstm_branch(x_m, z_m, o_m, conv_w, conv_b, wq, wk, wv, w_if, b_if, head_norm_g, skip):
    B, S, _ = x_m.shape
    x_c = jax.nn.silu(causal_depthwise_conv(x_m, conv_w, conv_b))
    q = block_diag_proj(x_c, wq)
    k = block_diag_proj(x_c, wk)
    v = block_diag_proj(x_m, wv)
    gate_pre = (jnp.concatenate([q, k, v], axis=-1) @ w_if + b_if).astype(jnp.float32)
    li = gate_pre[..., :M_HEADS]
    lf = jax.nn.log_sigmoid(gate_pre[..., M_HEADS:])
    heads = lambda t: t.reshape(B, S, M_HEADS, M_HEAD_DIM)
    h = mlstm_chunkwise(heads(q), heads(k), heads(v), li, lf)
    h = jax.nn.sigmoid(heads(o_m).astype(jnp.float32)) * h
    mu = jnp.mean(h, axis=-1, keepdims=True)
    var = jnp.mean(jnp.square(h - mu), axis=-1, keepdims=True)
    h = (h - mu) * lax.rsqrt(var + EPS) * head_norm_g.astype(jnp.float32).reshape(M_HEADS, M_HEAD_DIM)
    h = h.reshape(B, S, M_WIDTH) + skip * x_c
    return h * jax.nn.silu(z_m)

def first_inputs(seed: int = 0) -> dict:
    key = jax.random.key(seed)
    ks = jax.random.split(key, 20)
    nrm = lambda k, shape, scale: jax.random.normal(k, shape, jnp.float32) * scale
    n_blocks = M_WIDTH // QKV_BLOCK
    x = nrm(ks[0], (BATCH, SEQ, D_MODEL), 1.0)
    norm_in_g = 1.0 + nrm(ks[1], (DEPTH, D_MODEL), 0.02)
    w_in = nrm(ks[2], (DEPTH, D_MODEL, N_IN), D_MODEL ** -0.5)
    gate_b = nrm(ks[3], (DEPTH, 2 * D_MODEL), 0.01)
    conv_w = nrm(ks[4], (DEPTH, CONV_K, M_WIDTH), CONV_K ** -0.5)
    conv_b = nrm(ks[5], (DEPTH, M_WIDTH), 0.01)
    wq_m = nrm(ks[6], (DEPTH, n_blocks, QKV_BLOCK, QKV_BLOCK), QKV_BLOCK ** -0.5)
    wk_m = nrm(ks[7], (DEPTH, n_blocks, QKV_BLOCK, QKV_BLOCK), QKV_BLOCK ** -0.5)
    wv_m = nrm(ks[8], (DEPTH, n_blocks, QKV_BLOCK, QKV_BLOCK), QKV_BLOCK ** -0.5)
    w_if = nrm(ks[9], (DEPTH, 3 * M_WIDTH, 2 * M_HEADS), (3 * M_WIDTH) ** -0.5)
    b_if = jnp.concatenate([nrm(ks[10], (DEPTH, M_HEADS), 0.1),
                            jnp.linspace(3.0, 6.0, M_HEADS)[None] + nrm(ks[11], (DEPTH, M_HEADS), 0.01)], axis=-1)
    head_norm_g = 1.0 + nrm(ks[12], (DEPTH, M_WIDTH), 0.02)
    skip_m = 1.0 + nrm(ks[13], (DEPTH, M_WIDTH), 0.02)
    w_pa = nrm(ks[14], (DEPTH, A_WIDTH, D_MODEL), A_WIDTH ** -0.5)
    w_pb = nrm(ks[15], (DEPTH, M_WIDTH, D_MODEL), M_WIDTH ** -0.5)
    w_out = nrm(ks[16], (DEPTH, D_MODEL, D_MODEL), D_MODEL ** -0.5)
    rel_bias = nrm(ks[17], (N_BUCKETS, A_HEADS), 0.3)
    norm_out_g = 1.0 + nrm(ks[18], (D_MODEL,), 0.02)
    return {'x': x, 'norm_in_g': norm_in_g, 'w_in': w_in, 'gate_b': gate_b, 'conv_w': conv_w, 'conv_b': conv_b,
            'wq_m': wq_m, 'wk_m': wk_m, 'wv_m': wv_m, 'w_if': w_if, 'b_if': b_if, 'head_norm_g': head_norm_g,
            'skip_m': skip_m, 'w_pa': w_pa, 'w_pb': w_pb, 'w_out': w_out, 'rel_bias': rel_bias, 'norm_out_g': norm_out_g}

def first_block(x, norm_in_g, w_in, gate_b, conv_w, conv_b, wq_m, wk_m, wv_m, w_if, b_if, head_norm_g,
              skip_m, w_pa, w_pb, w_out, rel_bias, norm_out_g):
    B, S, _ = x.shape
    h = x
    for layer in range(DEPTH):
        xn = rmsnorm(h, norm_in_g[layer])
        proj = xn @ w_in[layer]
        q_a, k_a, v_a, z_a, x_m, z_m, o_m, gates = jnp.split(proj, SPLIT_POINTS, axis=-1)
        to_heads = lambda t: t.reshape(B, S, A_HEADS, A_HEAD_DIM)
        y_a = dilated_attention(to_heads(q_a), to_heads(k_a), to_heads(v_a), rel_bias)
        y_a = (y_a * jax.nn.silu(z_a)) @ w_pa[layer]
        y_m = mlstm_branch(x_m, z_m, o_m, conv_w[layer], conv_b[layer], wq_m[layer], wk_m[layer], wv_m[layer],
                           w_if[layer], b_if[layer], head_norm_g[layer], skip_m[layer]) @ w_pb[layer]
        g = jax.nn.sigmoid(gates.astype(jnp.float32) + gate_b[layer])
        g_a, g_m = jnp.split(g, 2, axis=-1)
        merged = g_a * y_a + g_m * y_m
        h = h + (merged @ w_out[layer]).astype(h.dtype)
    return rmsnorm(h, norm_out_g)


_first_inputs = first_inputs


def first_inputs(seed=0):
    import zlib

    import numpy as np

    out = dict(_first_inputs(seed))
    spreads = {}
    factors = {'norm_in_g': 3.524,
     'gate_b': 8.0,
     'conv_b': 8.0,
     'head_norm_g': 8.0,
     'skip_m': 8.0,
     'rel_bias': 4.517,
     'norm_out_g': 2.91}
    for name, (base, spread) in spreads.items():
        noise = np.random.default_rng([zlib.crc32(name.encode()), seed]).standard_normal(out[name].shape)
        drawn = base * np.exp(spread * noise) if base else spread * noise
        out[name] = jnp.asarray(drawn.astype(out[name].dtype))
    for name, factor in factors.items():
        out[name] = (out[name] * factor).astype(out[name].dtype)
    return out


_narrow_inputs = first_inputs


def first_inputs(seed=0):

    out = dict(_narrow_inputs(seed))
    wider = {'gate_b': 3.94, 'head_norm_g': 8.89, 'skip_m': 3.4, 'norm_out_g': 3.27}
    for name, times in wider.items():
        mean = out[name].mean()
        out[name] = (mean + times * (out[name] - mean)).astype(out[name].dtype)
    return out


DEPTH_2 = 2

CTX_LEN = 256
GRID_W = 64
N_EVEN = (DEPTH_2 + 1) // 2
N_ODD = DEPTH_2 // 2

RET_HEADS = 4
RET_HEAD_DIM = D_MODEL // 8
RET_W = RET_HEADS * RET_HEAD_DIM
RET_CHUNK = 128
ROPE_BASE = 10000.0
ROPE_PAIRS = (RET_HEAD_DIM // 8, 3 * RET_HEAD_DIM // 16, 3 * RET_HEAD_DIM // 16)
CONV_CH = D_MODEL // 2
CONV_K_2 = 31
EVEN_IN = 4 * RET_W + 2 * CONV_CH
EVEN_MIX = RET_W + CONV_CH
POOL_CH = D_MODEL // 2
POOL_WINDOWS = (2, 4, 8, 16)
POOL_GROUPS = len(POOL_WINDOWS)
POOL_GC = POOL_CH // POOL_GROUPS
SG_CH = D_MODEL // 2
SG_GROUPS = 4
SG_GC = SG_CH // SG_GROUPS
SG_CHUNK = 128
ODD_IN = POOL_CH + 2 * SG_CH
ODD_MIX = POOL_CH + SG_CH
D_FF = ((8 * D_MODEL // 3 + 255) // 256) * 256


def rms_norm(x, w):
    x32 = x.astype(jnp.float32)
    y = x32 * lax.rsqrt(jnp.mean(x32 * x32, axis=-1, keepdims=True) + EPS)
    return (y * w.astype(jnp.float32)).astype(x.dtype)

def layer_norm(x, w, b):
    x32 = x.astype(jnp.float32)
    mu = jnp.mean(x32, axis=-1, keepdims=True)
    xc = x32 - mu
    y = xc * lax.rsqrt(jnp.mean(xc * xc, axis=-1, keepdims=True) + EPS)
    return (y * w.astype(jnp.float32) + b.astype(jnp.float32)).astype(x.dtype)

def modulate(h, shift, scale):
    return h * (1.0 + scale) + shift

def swiglu(h, w_gate, w_up, w_down):
    return (jax.nn.silu(h @ w_gate) * (h @ w_up)) @ w_down

def rope_angles(p_seq, p_row, p_col):
    parts = []
    for p, n in zip((p_seq, p_row, p_col), ROPE_PAIRS):
        freq = ROPE_BASE ** (-jnp.arange(n, dtype=jnp.float32) / n)
        parts.append(p[:, None] * freq[None, :])
    return jnp.concatenate(parts, axis=-1)

def apply_rope(t, ang):
    t32 = t.astype(jnp.float32)
    half = t32.shape[-1] // 2
    t1, t2 = t32[..., :half], t32[..., half:]
    cos, sin = jnp.cos(ang), jnp.sin(ang)
    return jnp.concatenate([t1 * cos - t2 * sin, t1 * sin + t2 * cos], axis=-1)

def split_heads(t):
    b, l, _ = t.shape
    return t.reshape(b, l, RET_HEADS, RET_HEAD_DIM).transpose(0, 2, 1, 3)

def retention_chunkwise(q, k, v, log_g, s0, inclusive):
    b, h, l, dk = q.shape
    dv = v.shape[-1]
    n = l // RET_CHUNK
    qc = q.reshape(b, h, n, RET_CHUNK, dk)
    kc = k.reshape(b, h, n, RET_CHUNK, dk)
    vc = v.reshape(b, h, n, RET_CHUNK, dv)
    pos = jnp.arange(RET_CHUNK, dtype=jnp.float32)
    diff = pos[:, None] - pos[None, :]
    if inclusive:
        mask = diff >= 0
        expo = diff
        xi_exp = pos + 1.0
    else:
        mask = diff > 0
        expo = diff - 1.0
        xi_exp = pos
    lg = log_g[:, None, None]
    dmat = jnp.where(mask[None], jnp.exp(lg * jnp.where(mask, expo, 0.0)[None]), 0.0)
    xi = jnp.exp(log_g[:, None] * xi_exp[None, :])
    zeta = jnp.exp(log_g[:, None] * (RET_CHUNK - 1.0 - pos)[None, :])
    chunk_decay = jnp.exp(log_g * RET_CHUNK)[None, :, None, None]
    scores = jnp.einsum('bhncd,bhnmd->bhncm', qc, kc) * dmat[None, :, None]
    intra = jnp.einsum('bhncm,bhnme->bhnce', scores, vc)
    kv = jnp.einsum('bhnmd,hm,bhnme->bhnde', kc, zeta, vc)

    def step(s, kv_n):
        return s * chunk_decay + kv_n, s

    _, s_prev = lax.scan(step, s0, jnp.moveaxis(kv, 2, 0))
    inter = jnp.einsum('bhncd,hc,nbhde->bhnce', qc, xi, s_prev)
    return (intra + inter).reshape(b, h, l, dv)

def retention_final_states(k, v, log_g2):
    l = k.shape[2]
    pos = jnp.arange(l, dtype=jnp.float32)
    w_f = jnp.exp(log_g2[0][:, None] * (l - 1.0 - pos)[None, :])
    w_b = jnp.exp(log_g2[1][:, None] * pos[None, :])
    s_f = jnp.einsum('bhld,hl,bhle->bhde', k, w_f, v)
    s_b = jnp.einsum('bhld,hl,bhle->bhde', k, w_b, v)
    return s_f, s_b

def bidir_retention(q, k, v, log_g2, s_f, s_b):
    flip = lambda t: jnp.flip(t, axis=2)
    fwd = retention_chunkwise(q, k, v, log_g2[0], s_f, True)
    bwd = flip(retention_chunkwise(flip(q), flip(k), flip(v), log_g2[1], s_b, False))
    return fwd + bwd

def retention_kv(h, w_in, ang):
    k = apply_rope(split_heads(h @ w_in[:, RET_W:2 * RET_W]), ang)
    v = split_heads(h @ w_in[:, 2 * RET_W:3 * RET_W]).astype(jnp.float32)
    return k, v

def even_project(h, w_in, ang):
    p = h @ w_in
    q, k, v, g, a, gb = jnp.split(p, [RET_W, 2 * RET_W, 3 * RET_W, 4 * RET_W, 4 * RET_W + CONV_CH], axis=-1)
    q = apply_rope(split_heads(q), ang) * (RET_HEAD_DIM ** -0.5)
    k = apply_rope(split_heads(k), ang)
    v = split_heads(v).astype(jnp.float32)
    return q, k, v, g, a * jax.nn.sigmoid(gb)

def depthwise_conv(u, w):
    return lax.conv_general_dilated(
        u, w.astype(u.dtype)[:, None, :], window_strides=(1,),
        padding=[(CONV_K_2 // 2, CONV_K_2 // 2)],
        dimension_numbers=('NWC', 'WIO', 'NWC'), feature_group_count=u.shape[-1])

def even_mix(q, k, v, g, u, s_f, s_b, log_g2, conv_w, ln_w, ln_b, w_out):
    b, _, l, _ = q.shape
    y = bidir_retention(q, k, v, log_g2, s_f, s_b)
    y = y * lax.rsqrt(jnp.mean(y * y, axis=-1, keepdims=True) + EPS)
    y = y.transpose(0, 2, 1, 3).reshape(b, l, RET_W).astype(g.dtype)
    ret_out = jax.nn.silu(g) * y
    conv_out = jax.nn.silu(layer_norm(depthwise_conv(u, conv_w), ln_w, ln_b))
    return jnp.concatenate([ret_out, conv_out], axis=-1) @ w_out

def pool_minus_token(h32):
    b, l, _ = h32.shape
    cs = jnp.concatenate([jnp.zeros((b, 1, POOL_CH), jnp.float32), lax.cumsum(h32, axis=1)], axis=1)
    t = jnp.arange(l)
    outs = []
    for gi, w in enumerate(POOL_WINDOWS):
        left = w // 2
        right = w - 1 - left
        lo = jnp.clip(t - left, 0, l - 1)
        hi = jnp.clip(t + right, 0, l - 1)
        csg = cs[..., gi * POOL_GC:(gi + 1) * POOL_GC]
        mean = (csg[:, hi + 1] - csg[:, lo]) / (hi - lo + 1).astype(jnp.float32)[None, :, None]
        outs.append(mean - h32[..., gi * POOL_GC:(gi + 1) * POOL_GC])
    return jnp.stack(outs, axis=2)

def odd_stream(h, w_in, w_out, pool_w, pool_scale, sg_ln_w, sg_ln_b, sg_w, sg_b):
    b, l, _ = h.shape
    p = h @ w_in
    pc, pd = p[..., :POOL_CH], p[..., POOL_CH:]
    m = pool_minus_token(pc.astype(jnp.float32))
    pool_out = jnp.einsum('blgc,gcd->blgd', m, pool_w.astype(jnp.float32)).reshape(b, l, POOL_CH)
    pool_out = pool_out.astype(h.dtype) * pool_scale
    z = jax.nn.gelu(pd, approximate=False)
    u, v = jnp.split(z, 2, axis=-1)
    v = layer_norm(v, sg_ln_w, sg_ln_b).reshape(b, l // SG_CHUNK, SG_CHUNK, SG_GROUPS, SG_GC)
    s = jnp.einsum('bnpgc,gqp->bnqgc', v, sg_w) + sg_b.T[None, None, :, :, None]
    sg_out = u * s.reshape(b, l, SG_CH)
    return jnp.concatenate([pool_out, sg_out], axis=-1) @ w_out

def second_inputs(seed: int = 0) -> dict:
    key = jax.random.key(seed)
    ks = jax.random.split(key, 25)
    f32 = jnp.float32
    nrm = lambda k, shape, s: jax.random.normal(k, shape, f32) * s
    gamma0 = 1.0 - 2.0 ** (-5.0 - np.arange(RET_HEADS))
    decay_base = jnp.asarray(np.log(gamma0 / (1.0 - gamma0)), f32)
    return {
        'x': nrm(ks[0], (BATCH, SEQ, D_MODEL), 1.0),
        'c': nrm(ks[1], (BATCH, D_MODEL), 1.0),
        'ctx': nrm(ks[2], (BATCH, CTX_LEN, D_MODEL), 1.0),
        'c_ctx': nrm(ks[3], (D_MODEL,), 1.0),
        'ada_w': nrm(ks[4], (DEPTH_2, D_MODEL, 6 * D_MODEL), 0.5 * D_MODEL ** -0.5),
        'ada_b': nrm(ks[5], (DEPTH_2, 6 * D_MODEL), 0.02),
        'norm_w': 1.0 + nrm(ks[6], (DEPTH_2, 2, D_MODEL), 0.02),
        'even_w_in': nrm(ks[7], (N_EVEN, D_MODEL, EVEN_IN), D_MODEL ** -0.5),
        'even_w_out': nrm(ks[8], (N_EVEN, EVEN_MIX, D_MODEL), EVEN_MIX ** -0.5),
        'ret_decay_logit': decay_base + nrm(ks[9], (N_EVEN, 2, RET_HEADS), 0.1),
        'conv_dw_w': nrm(ks[10], (N_EVEN, CONV_K_2, CONV_CH), CONV_K_2 ** -0.5),
        'conv_ln_w': 1.0 + nrm(ks[11], (N_EVEN, CONV_CH), 0.02),
        'conv_ln_b': nrm(ks[12], (N_EVEN, CONV_CH), 0.02),
        'odd_w_in': nrm(ks[13], (N_ODD, D_MODEL, ODD_IN), D_MODEL ** -0.5),
        'odd_w_out': nrm(ks[14], (N_ODD, ODD_MIX, D_MODEL), ODD_MIX ** -0.5),
        'pool_w': nrm(ks[15], (N_ODD, POOL_GROUPS, POOL_GC, POOL_GC), POOL_GC ** -0.5),
        'pool_scale': 1.0 + nrm(ks[16], (N_ODD, POOL_CH), 0.02),
        'sg_ln_w': 1.0 + nrm(ks[17], (N_ODD, SG_CH), 0.02),
        'sg_ln_b': nrm(ks[18], (N_ODD, SG_CH), 0.02),
        'sg_w': nrm(ks[19], (N_ODD, SG_GROUPS, SG_CHUNK, SG_CHUNK), 0.5 * SG_CHUNK ** -0.5),
        'sg_b': 1.0 + nrm(ks[20], (N_ODD, SG_GROUPS, SG_CHUNK), 0.02),
        'ffn_w_gate': nrm(ks[21], (DEPTH_2, D_MODEL, D_FF), D_MODEL ** -0.5),
        'ffn_w_up': nrm(ks[22], (DEPTH_2, D_MODEL, D_FF), D_MODEL ** -0.5),
        'ffn_w_down': nrm(ks[23], (DEPTH_2, D_FF, D_MODEL), D_FF ** -0.5),
        'final_norm_w': 1.0 + nrm(ks[24], (D_MODEL,), 0.02),
    }

def second_block(x, c, ctx, c_ctx, ada_w, ada_b, norm_w, even_w_in, even_w_out, ret_decay_logit,
              conv_dw_w, conv_ln_w, conv_ln_b, odd_w_in, odd_w_out, pool_w, pool_scale,
              sg_ln_w, sg_ln_b, sg_w, sg_b, ffn_w_gate, ffn_w_up, ffn_w_down, final_norm_w):
    b, l, d = x.shape
    lc = ctx.shape[1]
    rows = l // GRID_W
    grid_r = jnp.broadcast_to(jnp.arange(rows, dtype=jnp.float32)[:, None], (rows, GRID_W)).reshape(-1)
    grid_c = jnp.broadcast_to(jnp.arange(GRID_W, dtype=jnp.float32)[None, :], (rows, GRID_W)).reshape(-1)
    ang_x = rope_angles(jnp.full((l,), lc, jnp.float32), grid_r, grid_c)
    zeros_c = jnp.zeros((lc,), jnp.float32)
    ang_c = rope_angles(jnp.arange(lc, dtype=jnp.float32), zeros_c, zeros_c)
    silu_c = jax.nn.silu(c)
    silu_cc = jax.nn.silu(c_ctx)

    for i in range(DEPTH_2):
        j = i // 2
        even = i % 2 == 0
        ctx_after = any(m % 2 == 0 for m in range(i + 1, DEPTH_2))
        use_ctx = even or ctx_after
        mod_x = (silu_c @ ada_w[i] + ada_b[i]).reshape(b, 6, 1, d)
        hx = modulate(rms_norm(x, norm_w[i, 0]), mod_x[:, 0], mod_x[:, 1])
        if use_ctx:
            mod_c = (silu_cc @ ada_w[i] + ada_b[i]).reshape(6, 1, d)
            hc = modulate(rms_norm(ctx, norm_w[i, 0]), mod_c[0], mod_c[1])
        if even:
            log_g2 = jax.nn.log_sigmoid(ret_decay_logit[j].astype(jnp.float32))
            if ctx_after:
                parts_c = even_project(hc, even_w_in[j], ang_c)
                kc, vc = parts_c[1], parts_c[2]
            else:
                kc, vc = retention_kv(hc, even_w_in[j], ang_c)
            s_f, s_b = retention_final_states(kc, vc, log_g2)
            yx = even_mix(*even_project(hx, even_w_in[j], ang_x), s_f, s_b, log_g2,
                          conv_dw_w[j], conv_ln_w[j], conv_ln_b[j], even_w_out[j])
            if ctx_after:
                s_zero = jnp.zeros_like(s_f)
                yc = even_mix(*parts_c, s_zero, s_zero, log_g2,
                              conv_dw_w[j], conv_ln_w[j], conv_ln_b[j], even_w_out[j])
        else:
            yx = odd_stream(hx, odd_w_in[j], odd_w_out[j], pool_w[j], pool_scale[j],
                            sg_ln_w[j], sg_ln_b[j], sg_w[j], sg_b[j])
            if ctx_after:
                yc = odd_stream(hc, odd_w_in[j], odd_w_out[j], pool_w[j], pool_scale[j],
                                sg_ln_w[j], sg_ln_b[j], sg_w[j], sg_b[j])
        x = x + mod_x[:, 2] * yx
        x = x + mod_x[:, 5] * swiglu(modulate(rms_norm(x, norm_w[i, 1]), mod_x[:, 3], mod_x[:, 4]),
                                     ffn_w_gate[i], ffn_w_up[i], ffn_w_down[i])
        if ctx_after:
            ctx = ctx + mod_c[2] * yc
            ctx = ctx + mod_c[5] * swiglu(modulate(rms_norm(ctx, norm_w[i, 1]), mod_c[3], mod_c[4]),
                                          ffn_w_gate[i], ffn_w_up[i], ffn_w_down[i])
    return rms_norm(x, final_norm_w)


_first_inputs_2 = second_inputs


def second_inputs(seed=0):
    import zlib

    import numpy as np

    out = dict(_first_inputs_2(seed))
    spreads = {}
    factors = {'norm_w': 4.832,
     'conv_ln_w': 8.0,
     'conv_ln_b': 8.0,
     'pool_scale': 8.0,
     'sg_ln_w': 8.0,
     'sg_ln_b': 8.0,
     'sg_b': 8.0,
     'final_norm_w': 2.859}
    for name, (base, spread) in spreads.items():
        noise = np.random.default_rng([zlib.crc32(name.encode()), seed]).standard_normal(out[name].shape)
        drawn = base * np.exp(spread * noise) if base else spread * noise
        out[name] = jnp.asarray(drawn.astype(out[name].dtype))
    for name, factor in factors.items():
        out[name] = (out[name] * factor).astype(out[name].dtype)
    return out


_narrow_inputs_2 = second_inputs


def second_inputs(seed=0):

    out = dict(_narrow_inputs_2(seed))
    wider = {'pool_scale': 4.55, 'sg_ln_w': 11.4, 'sg_ln_b': 11.77, 'sg_b': 6.0, 'final_norm_w': 3.24}
    for name, times in wider.items():
        mean = out[name].mean()
        out[name] = (mean + times * (out[name] - mean)).astype(out[name].dtype)
    return out


def setup_inputs(seed=0):
    out = dict(first_inputs(seed))
    for name, value in second_inputs(seed + 1).items():
        if name != "x":
            out[name + "_2"] = value
    return out


def reference(
    x, norm_in_g, w_in, gate_b, conv_w, conv_b, wq_m, wk_m, wv_m, w_if, b_if, head_norm_g,
    skip_m, w_pa, w_pb, w_out, rel_bias, norm_out_g, c_2, ctx_2, c_ctx_2, ada_w_2, ada_b_2,
    norm_w_2, even_w_in_2, even_w_out_2, ret_decay_logit_2, conv_dw_w_2, conv_ln_w_2,
    conv_ln_b_2, odd_w_in_2, odd_w_out_2, pool_w_2, pool_scale_2, sg_ln_w_2, sg_ln_b_2, sg_w_2,
    sg_b_2, ffn_w_gate_2, ffn_w_up_2, ffn_w_down_2, final_norm_w_2,
):
    x = first_block(
        x, norm_in_g, w_in, gate_b, conv_w, conv_b, wq_m, wk_m, wv_m, w_if, b_if, head_norm_g,
        skip_m, w_pa, w_pb, w_out, rel_bias, norm_out_g,
    )
    return second_block(
        x, c_2, ctx_2, c_ctx_2, ada_w_2, ada_b_2, norm_w_2, even_w_in_2, even_w_out_2,
        ret_decay_logit_2, conv_dw_w_2, conv_ln_w_2, conv_ln_b_2, odd_w_in_2, odd_w_out_2,
        pool_w_2, pool_scale_2, sg_ln_w_2, sg_ln_b_2, sg_w_2, sg_b_2, ffn_w_gate_2, ffn_w_up_2,
        ffn_w_down_2, final_norm_w_2,
    )


_drawn_inputs = setup_inputs


def setup_inputs(seed=0):
    import zlib

    import numpy as np

    out = dict(_drawn_inputs(seed))
    spreads = {}
    factors = {'conv_ln_w_2': 4.791, 'conv_ln_b_2': 4.601, 'c_ctx_2': 2.884}
    for name, (base, spread) in spreads.items():
        noise = np.random.default_rng([zlib.crc32(name.encode()), seed]).standard_normal(out[name].shape)
        drawn = base * np.exp(spread * noise) if base else spread * noise
        out[name] = jnp.asarray(drawn.astype(out[name].dtype))
    for name, factor in factors.items():
        out[name] = (out[name] * factor).astype(out[name].dtype)
    return out
```

```python
import math
from contextlib import ExitStack

import concourse.bass as bass
import numpy as np
from concourse import mybir

P = 128
S = 512
CTX = 256
D = 1024
KT = D // P
EPS = 1e-6
HB = (4, 5, 7, 6)
ROPE_PAIRS = (16, 24, 24)
TOEP = 2 * S - P
TRI = 10 * P
TRI_AT = (0, P, 3 * P, 6 * P)
PC_AT = (0, 4 * P, 7 * P, 9 * P)
SB, SO = (2, 2, 1, 0), (256, 0, 0, 0)
FF = 22
CW = S + 30
PW = S + 16
F32 = mybir.dt.float32
F32R = mybir.dt.float32r
ALU = mybir.AluOpType
ACT = mybir.ActivationFunctionType
AX = mybir.AxisListType
ds = bass.ds

WIDTHS = dict(g_in=8, g_out=8, gate_b=16, conv_w=64, conv_b=16, g_head=16, skip=16, b_if=8, c=16, ada_b=96,
              norm_w=32, decay=8, conv2_w=124, ln_w=4, ln_b=4, pool_scale=4, g_final=8)
COL, at = {}, 0
for name, width in WIDTHS.items():
    COL[name] = at
    at += width
NCOL = at

STAGES = [("x_m", 8, 2)]
for h in range(4):
    STAGES += [(f"o_m{h}", 2, 2), (f"z_m{h}", 2, 2), (f"w_pb{h}", 2, 4)]
STAGES += [("q_a", 4, 2), ("k_a", 4, 2), ("v_a", 4, 4), ("z_a", 4, 2), ("gate_a", 4, 2), ("w_pa", 4, 2), ("gate_m", 4, 2),
           ("w_out", 4, 2), ("a_e", 2, 2), ("b_e", 2, 2), ("q_r", 2, 2), ("k_r", 2, 4), ("v_r", 2, 6), ("g_r", 2, 2), ("even_out", 4, 2),
           ("up0", 22, 2), ("down0", 16, 1), ("pool", 2, 2), ("u_s", 2, 2), ("v_s", 2, 4), ("odd_out", 4, 2),
           ("up1", 22, 2), ("down1", 16, 1)]
FIRST, GROUP0, PER = {}, {}, {}
nb = ng = 0
for name, blocks, groups in STAGES:
    FIRST[name], GROUP0[name], PER[name] = nb, ng, groups
    nb += blocks
    ng += blocks * groups
COUNT = {name: blocks for name, blocks, _ in STAGES}


class Tally:

    def __init__(self, engine, sem):
        self.engine, self.sem, self.n = engine, sem, 0

    def __call__(self, instruction):
        instruction.then_inc(self.sem, 1)
        self.n = self.n + 1
        self.engine.wait_ge(self.sem, self.n)


def program(nc, xt, ctxt, cols, blocks, bd_qk, bd_v, bd_back, w_if, rel, ada, pool_w, sg_w, sg_rows, square, hot,
            diff, rope_x, rope_c, inv, out):
    ctx = ExitStack()
    with ctx:
        body(nc, ctx, xt, ctxt, cols, blocks, bd_qk, bd_v, bd_back, w_if, rel, ada, pool_w, sg_w, sg_rows, square, hot,
             diff, rope_x, rope_c, inv, out)


def body(nc, ctx, xt, ctxt, cols, blocks, bd_qk, bd_v, bd_back, w_if, rel, ada, pool_w, sg_w, sg_rows, square, hot,
         diff, rope_x, rope_c, inv, out):
    def sb(name, shape, dt=F32, stack=ctx):
        return stack.enter_context(nc.sbuf_tensor(name, shape, dt))

    sems = {}

    def sem(name):
        if name not in sems:
            sems[name] = ctx.enter_context(nc.semaphore(name))
        return sems[name]

    raw = sb("raw", [P, 2, 2048])
    w_hi = sb("w_hi", [P, 2, 2048], F32R)
    w_lo = sb("w_lo", [P, 2, 2048], F32R)
    x_hi = sb("x_hi", [P, KT, S], F32R)
    x_lo = sb("x_lo", [P, KT, S], F32R)
    col = sb("col", [P, NCOL])
    sq_c = sb("sq_c", [P, 3, P])
    ones = sb("ones", [P, P])
    sq = sb("sq", [P, 2, S])
    tt = sb("tt", [P, 2, S])
    var = sb("var", [P, S])
    root = sb("root", [P, S])
    low = sb("low", [P, KT * S])
    def c1(name, j):
        return col[:, COL[name] + j:COL[name] + j + 1]

    def stat(h, what):
        o = 16 * (h % 2) + 4 * what
        return sq[:, 0, o:o + 4]

    def backward(b):
        a = bank[b][:, :]
        return bass.AP(a.tensor, a.offset + P - 1, [list(a.ap[0]), [P, 4], [-1, P]])

    ident, tri, neg = sq_c[:, 0, :], sq_c[:, 1, :], sq_c[:, 2, :]

    m1, m2, m3 = ExitStack(), ExitStack(), ExitStack()
    pb = sb("pb", [P, KT, S], stack=m1)
    bd_b = sb("bd_b", [P, 16, 3, P], stack=m2)
    m2.close()
    m2 = ExitStack()
    v_m = sb("v_m", [P, 4, 2048], stack=m2)
    x_c = sb("x_c", [P, 16, S], stack=m2)
    k_t = sb("k_t", [P, 4, S], stack=m3)
    p_t = sb("p_t", [P, 4, S], stack=m3)
    m3.close()
    m3 = ExitStack()
    y_hi = sb("y_hi", [P, 4, S], F32R, stack=m3)
    y_lo = sb("y_lo", [P, 4, S], F32R, stack=m3)
    m3.close()
    m2.close()

    a1, a2 = ExitStack(), ExitStack()
    k_a = sb("k_a", [P, KT, S], stack=a1)
    v_a = sb("v_a", [P, 4, D], stack=a1)
    y_a = sb("y_a", [P, 4, D], stack=a1)
    s_r = sb("s_r", [P, TRI], stack=a2)
    p_r = sb("p_r", [P, TRI], stack=a2)
    p_c = sb("p_c", [P, TRI], stack=a2)
    strip = sb("strip", [P, 2, S], stack=a2)
    a2.close()
    hot_sb = sb("hot_sb", [33, S + P], stack=a2)
    rel_sb = sb("rel_sb", [33, 16], stack=a2)
    bias_v = sb("bias_v", [16, S + P], stack=a2)
    a2.close()
    a1.close()
    a1 = ExitStack()
    yz_lo = sb("yz_lo", [P, KT, S], F32R, stack=a1)
    sb("gap", [P, 2 * KT * S], stack=a1)
    yz_hi = sb("yz_hi", [P, KT, S], F32R, stack=a1)
    a1.close()
    m1.close()
    q_a = low[:, :].rearrange("p (k n) -> p k n", n=S)
    z_a = res = q_a
    gate = v_a[:, :, :].rearrange("p t (a n) -> p (t a) n", n=S)
    merged = y_a[:, :, :].rearrange("p t (a n) -> p (t a) n", n=S)
    skew = nc.dram_tensor("skew", (16, S + P), F32, kind="Internal").ap()

    e0 = ExitStack()
    mod = sb("mod", [P, 96, 2], stack=e0)
    coef = sb("coef", [P, 5, 8], stack=e0)
    silu_c = sb("silu_c", [P, 8, 2], stack=e0)
    e1 = ExitStack()
    ada_w = sb("ada_w", [P, 4, 2048], stack=e1)
    e1.close()
    e1 = ExitStack()
    conv_c = sb("conv_c", [P, 4, S], stack=e1)
    conv_u = sb("conv_u", [P, 4, CW], stack=e1)
    q_r = sb("q_r", [P, 4, S], stack=e1)
    k_r = sb("k_r", [P, 4, S], stack=e1)
    v_r = sb("v_r", [P, 4, S], stack=e1)
    g_r = sb("g_r", [P, 4, S], stack=e1)
    k_x = sb("k_x", [P, 4, CTX], stack=e1)
    v_x = sb("v_x", [P, 2, S], stack=e1)
    rope_t = sb("rope_t", [P, 2, S], stack=e1)
    rope_u = sb("rope_u", [P, 2, CTX], stack=e1)
    diff_t = sb("diff_t", [P, TOEP], stack=e1)
    ahead = sb("ahead", [P, TOEP], stack=e1)
    behind = sb("behind", [P, TOEP], stack=e1)
    lg = sb("lg", [P, 48], stack=e1)
    e2 = ExitStack()
    c_hi = sb("c_hi", [P, KT, CTX], F32R, stack=e2)
    c_lo = sb("c_lo", [P, KT, CTX], F32R, stack=e2)
    e2.close()
    e2 = ExitStack()
    w_r = sb("w_r", [P, 6, S], stack=e2)
    decay = sb("decay", [P, TOEP], stack=e2)
    decay_x = sb("decay_x", [P, 2, S], stack=e2)
    e2.close()
    e1.close()
    c_in = g_r[:, :, :].rearrange("p a (b n) -> p (a b) n", n=CTX)
    f1 = ExitStack()
    hid_hi = sb("hid_hi", [P, FF, S], F32R, stack=f1)
    hid_lo = sb("hid_lo", [P, FF, S], F32R, stack=f1)
    f1.close()
    o1 = ExitStack()
    pc = sb("pc", [P, 4, PW], stack=o1)
    pool_a = sb("pool_a", [P, 4, PW], stack=o1)
    pool_b = sb("pool_b", [P, 4, PW], stack=o1)
    u_s = sb("u_s", [P, 4, S], stack=o1)
    v_s = sb("v_s", [P, 4, S], stack=o1)
    inv_t = sb("inv_t", [P, 4, S], stack=o1)
    sg_r = sb("sg_r", [P, 3, S], stack=o1)
    pool_ws = sb("pool_ws", [P, 4, P], stack=o1)
    sg_ws = sb("sg_ws", [P, 4, P], stack=o1)
    bn = sb("bn", [P, 4, 16], stack=o1)
    o1.close()
    e0.close()
    conv_out = k_t
    conv_in = pb[:, 0:5, :].rearrange("p a b -> p (a b)")[:, 0:4 * 516].rearrange("p (b n) -> p b n", n=516)
    q_t = low[:, 0:2048].rearrange("p (c n) -> p c n", n=S)
    bd = low[:, 2048:3072].rearrange("p (c w n) -> p c w n", w=2, n=P)
    v_w = low[:, 0:2176].rearrange("p (k n) -> p k n", n=136)
    wif = low[:, 2176:2560].rearrange("p (k g) -> p k g", g=8)
    small = low[:, 3072:4096]
    g_tok = small[:, 0:32].rearrange("p (t g) -> p t g", g=8)
    w_g = small[:, 32:160].rearrange("p (k g) -> p k g", g=8)
    lf = small[:, 160:176].rearrange("p (t g) -> p t g", g=4)
    u_c = small[:, 176:192].rearrange("p (t g) -> p t g", g=4)
    b_c = small[:, 192:208].rearrange("p (t g) -> p t g", g=4)
    gs = small[:, 208:240].rearrange("p (t g) -> p t g", g=8)
    ga = small[:, 240:256].rearrange("p (t g) -> p t g", g=4)
    gb = small[:, 256:272].rearrange("p (t g) -> p t g", g=4)
    rows = small[0:64, 272:784]

    bank = [ctx.enter_context(nc.psum_tensor(f"bank{i}", [P, S], F32)) for i in range(8)]

    raw_in = [sem("raw_in0"), sem("raw_in1")]
    hi_done, lo_done, mm_done = sem("hi_done"), sem("lo_done"), sem("mm_done")
    ev_act, ev_dve = sem("ev_act"), sem("ev_dve")
    LEAD = 4
    evs = {"act": 0, "dve": 0}
    EV = {}
    for name, blocks_, groups in STAGES:
        base = name.rstrip("0123")
        if base == "up":
            EV[name] = ("both", dict(evs))
            evs["act"] += blocks_
            evs["dve"] += blocks_
            continue
        by = "act" if base in ("x_m", "o_m", "z_m", "z_a", "gate_a", "q_a", "k_a", "gate_m", "a_e", "b_e", "q_r", "k_r", "v_r", "g_r", "pool", "u_s", "v_s") else "dve"
        EV[name] = (by, dict(evs))
        n = blocks_ * groups // (2 if base == "down" else 1)
        evs[by] += n
    block = ctx.enter_context(nc.Block())
    LAST = STAGES[-1][0]
    BLOCKS = FIRST[LAST] + COUNT[LAST]

    @block.sync
    def _(sp):
        def stream(lo, hi):
            with sp.Fori((lo - 2) // 2, (hi - 2) // 2) as i:
                for s in range(2):
                    sp.wait_ge(lo_done, 2 * i + s + 1)
                    sp.dma_start(raw[:, s, :], blocks[ds(2 * i + s + 2, 1)].rearrange("a p n -> p (a n)"))\
                      .then_inc(raw_in[s], 16)

        for s in range(2):
            sp.dma_start(raw[:, s, :], blocks[s]).then_inc(raw_in[s], 16)
        first = FIRST["a_e"] + 2
        stream(2, first)
        for n in range(4):
            if n == 0:
                sp.wait_ge(sem("merge_over"), 1)
            sp.dma_start(ada_w[:, n, :], ada[n]).then_inc(sem(f"ada_in{n}"), 16)
        with sp.Fori(0, 11) as i:
            for n in range(4):
                sp.wait_ge(sem("ada_mm"), 4 * i + n + 1)
                sp.dma_start(ada_w[:, n, :], ada[ds(4 * i + n + 4, 1)].rearrange("a p n -> p (a n)"))\
                  .then_inc(sem(f"ada_in{n}"), 16)
        stream(first, BLOCKS)
        sp.wait_ge(sem("out_ready"), 1)
        sp.dma_start(out.rearrange("(k p) n -> p k n", p=P), low[:, :].rearrange("p (k n) -> p k n", n=S))\
          .then_inc(sem("out_sent"), 16)
        sp.wait_ge(sem("out_sent"), 16)

    @block.gpsimd
    def _(pool):
        with pool.Fori(0, BLOCKS // 2) as i:
            for s in range(2):
                pool.wait_ge(hi_done, 2 * i + s + 1)
                pool.tensor_tensor(w_lo[:, s, :], raw[:, s, :], w_hi[:, s, :].bitcast(F32), ALU.subtract)\
                    .then_inc(lo_done, 1)

    @block.scalar
    def _(act):
        own = Tally(act, sem("act_own"))

        def split(n, s, after):
            act.wait_ge(raw_in[s], 16 * n + 16)
            act.wait_ge(mm_done, after)
            act.activation(w_hi[:, s, :], raw[:, s, :], ACT.Copy).then_inc(hi_done, 1)

        def stage(name, free, between=None):
            n0, g0, per = FIRST[name], GROUP0[name], PER[name]
            blocks_ = COUNT[name]

            def pair(i, last=False):
                for s in range(2):
                    if not (last and s == 1):
                        split(n0 // 2 + i + (s + 1) // 2, 1 - s, 1 + g0 + per * (2 * i + s))
                    if free:
                        for m in range(per):
                            act.wait_ge(mm_done, 2 + g0 + per * (2 * i + s) + m)
                            free(per * (2 * i + s) + m, (per * s + m) % 4, i)
                if between:
                    between(i)

            pairs = blocks_ // 2
            whole = pairs - 1 if name == LAST else pairs
            if whole > 1:
                with act.Fori(0, whole) as i:
                    pair(i)
            elif whole == 1:
                pair(0)
            if name == LAST:
                pair(whole, last=True)

        act.sem_inc(ev_act, LEAD)
        act.sem_inc(sem("xc_ready"), 4)
        act.dma_start(col[:, :], cols).then_inc(sem("consts"), 16)
        act.dma_start(sq_c[:, :, :], square).then_inc(sem("consts"), 16)
        act.dma_start(pb[:, :, :], xt).then_inc(sem("x_in"), 16)
        act.dma_start(wif, w_if).then_inc(sem("bd_in"), 16)
        act.dma_start(v_w[:, :, 0:P], bd_v).then_inc(sem("bd_in"), 16)
        act.dma_start(bd_b[:, :, :, :].rearrange("p a b c -> p (a b c)"), bd_back).then_inc(sem("bd_in"), 16)
        act.wait_ge(raw_in[0], 16)
        act.activation(w_hi[:, 0, :], raw[:, 0, :], ACT.Copy).then_inc(hi_done, 1)

        norms = [0, 0]

        def norm(src, n=S, shift=None, dst=x_hi, after=None):
            v, w = norms
            for k in range(KT):
                if v or k >= 2:
                    act.wait_ge(sem("sq_used"), 8 * v + k - 1)
                if after:
                    act.wait_ge(ev_dve, LEAD + EV[after][1]["dve"] + k + 1)
                act.activation(sq[:, k % 2, :n], src(k), ACT.Square).then_inc(sem("sq_ready"), 1)
            act.wait_ge(sem("var_ready"), v + 1)
            act.activation(root[:, :n], var[:, :n], ACT.Sqrt).then_inc(sem("root_ready"), 1)
            norms[0] += 1
            if dst is None:
                return
            for k in range(KT):
                act.wait_ge(sem("t_ready"), 8 * w + k + 1)
                if shift is None:
                    act.activation(dst[:, k, :n], tt[:, k % 2, :n], ACT.Copy).then_inc(sem("xh_ready"), 1)
                else:
                    act.activation(dst[:, k, :n], tt[:, k % 2, :n], ACT.Identity, bias=shift(k)).then_inc(sem("xh_ready"), 1)
            norms[1] += 1

        act.wait_ge(sem("x_in"), 16)
        norm(lambda k: pb[:, k, :])

        def x_m_free(g, b, i):
            act.wait_ge(sem("conv_done"), 4 * i + b + 1)
            act.wait_ge(sem("vg_mm"), 4 * i + b + 1)
            act.activation(conv_in[:, b, 3:3 + S], bank[b][:, :], ACT.Copy).then_inc(ev_act, 1)

        def x_m_silu(i):
            for b in range(4):
                act.wait_ge(sem("conv_done"), 4 + 4 * i + b + 1)
                act.activation(x_c[:, ds(4 * i + b, 1), :], conv_out[:, b, :], ACT.Silu).then_inc(sem("xc_ready"), 1)

        act.wait_ge(sem("pad_ready"), 1)
        stage("x_m", x_m_free, x_m_silu)

        act.wait_ge(sem("g_ready"), 1)
        own(act.activation(ga, gs[:, :, 4:8], ACT.Abs))
        own(act.activation(gb, ga, ACT.Exp, scale=-1.0))
        act.activation(ga, gb, ACT.Ln, bias=1.0).then_inc(sem("ln_ready"), 1)
        act.wait_ge(sem("bm_ready"), 1)
        act.activation(rows[32:36, :], root[32:36, :], ACT.Exp, scale=-1.0).then_inc(sem("rows_ready"), 1)

        for h in range(4):
            before = 1 + GROUP0[f"o_m{h}"]
            if h:
                act.wait_ge(sem("qk_used"), h)
            else:
                act.wait_ge(sem("gates_mm"), 1)
                act.wait_ge(sem("vg_mm"), 4 + 16)
            act.dma_start(bd, bd_qk[:, h, :].rearrange("p (c w n) -> p c w n", w=2, n=P)).then_inc(sem("bd_ready"), 16)
            act.wait_ge(mm_done, before)
            if h:
                act.wait_ge(sem("y_done"), 4 * h)
            for j in range(8):
                act.wait_ge(sem("qk_mm"), 8 * h + j + 1)
                dst = (q_t, k_t)[j // 4][:, j % 4, :]
                act.activation(dst, bank[4 + j % 2][:, :], ACT.Copy, scale=1.0 if j < 4 else 512 ** -0.5)\
                   .then_inc(sem("qk_ev"), 1)
            act.wait_ge(sem("nm_ready"), h + 1)
            for j in range(4):
                last = act.activation(p_t[:, j, 0:P], tt[:, 1, P * j:P * j + P], ACT.Exp, bias=u_c[:, j, h:h + 1])
                if j < 3:
                    last = act.activation(p_t[:, j, P:S - P * j], tt[:, 0, P * j + P:S], ACT.Exp, bias=u_c[:, j, h:h + 1])
                last.then_inc(sem("e_done"), 1)
            act.wait_ge(sem("s_mm"), 4 * h + 4)
            stage(f"o_m{h}", lambda g, b, i: act.activation(q_t[:, b, :], bank[b][:, :], ACT.Sigmoid).then_inc(ev_act, 1))
            act.wait_ge(sem("den_mm"), h + 1)
            act.activation(root[:, :], bank[6][:, :], ACT.Abs).then_inc(sem("abs_done"), 1)
            for e in range(4):
                act.wait_ge(sem("h_done"), 4 * h + e + 1)
                if e >= 2:
                    act.wait_ge(sem("hs_mm"), 4 * h + e - 1)
                act.activation(sq[:, e % 2, :], q_t[:, e, :], ACT.Square).then_inc(sem("hsq_ready"), 1)
            act.wait_ge(sem("hvar_ready"), h + 1)
            act.activation(var[:, :], root[:, :], ACT.Sqrt).then_inc(sem("hroot_ready"), 1)
            act.wait_ge(sem("hs_mm"), 4 * h + 4)

            def z_free(g, b, i):
                if b >= 2:
                    act.wait_ge(sem("prod_done"), 4 * h + b - 1)
                act.activation(sq[:, b % 2, :], bank[b][:, :], ACT.Silu).then_inc(ev_act, 1)
                act.wait_ge(sem("prod_done"), 4 * h + b + 1)
                act.activation(y_hi[:, b, :], q_t[:, b, :], ACT.Copy).then_inc(sem("yh_done"), 1)
            stage(f"z_m{h}", z_free)
            stage(f"w_pb{h}", None)

        act.wait_ge(mm_done, 1 + GROUP0["w_pb3"])
        act.dma_start(rel_sb[0:32, :], rel).then_inc(sem("rel_in"), 16)
        act.dma_start(hot_sb[:, :], hot).then_inc(sem("rel_in"), 16)
        act.wait_ge(sem("bias_mm"), 1)
        act.activation(bias_v[:, 0:S], bank[4][0:16, :], ACT.Copy)
        act.activation(bias_v[:, S:], bank[5][0:16, 0:P], ACT.Copy).then_inc(sem("bias_ready"), 1)
        act.wait_ge(sem("bias_ready"), 1)
        act.dma_start(skew, bias_v[:, :]).then_inc(sem("skew_out"), 16)
        act.wait_ge(sem("skew_out"), 16)

        def load_strip(h):
            src = bass.AP(skew.tensor, h * (S + P), [[1, P], [1, S]])
            act.dma_start(strip[:, h % 2, :], src).then_inc(sem(f"strip_in{h % 2}"), 16)
        load_strip(0)
        load_strip(1)
        act.wait_ge(sem("y_done"), 16)
        stage("q_a", lambda g, b, i: act.activation(q_a[:, ds(g, 1), :].rearrange("p a (t n) -> p (a t) n", n=P), backward(b), ACT.Copy, scale=0.125)
              .then_inc(ev_act, 1))
        stage("k_a", lambda g, b, i: act.activation(k_a[:, ds(g, 1), :], bank[b][:, :], ACT.Copy).then_inc(ev_act, 1))
        stage("v_a", None)
        for h in range(16):
            act.wait_ge(sem("max_ready"), h + 1)
            if h:
                act.wait_ge(sem("t_mm"), 3 * h)
            for i in range(4):
                o = TRI_AT[i]
                last = act.activation(p_r[:, o:o + P * (i + 1)], s_r[:, o:o + P * (i + 1)], ACT.Exp,
                                      bias=stat(h, 1)[:, i:i + 1], accum_out=stat(h, 2)[:, i:i + 1])
            last.then_inc(sem("p_done"), 1)
            act.wait_ge(sem("t_mm"), 3 * h + 1)
            if h:
                act.wait_ge(sem("pv_mm"), h)
            act.activation(p_c[:, 0:S], bank[4][:, :], ACT.Copy).then_inc(sem("pc_act"), 1)
            if h >= 1 and h < 15:
                load_strip(h + 1)
        act.wait_ge(sem("qk_a_mm"), 16)
        stage("z_a", lambda g, b, i: act.activation(z_a[:, ds(g, 1), :], bank[b][:, :], ACT.Silu).then_inc(ev_act, 1))
        for c in range(8):
            act.wait_ge(sem("yz_f"), c + 1)
            act.activation(yz_hi[:, c, :], tt[:, c % 2, :], ACT.Copy).then_inc(sem("yz_h"), 1)
        act.wait_ge(sem("yz_l"), 8)
        act.dma_start(res, xt).then_inc(sem("res_in"), 16)

        def gate_b(g, more=0):
            return col[:, ds(g + (COL["gate_b"] + more), 1)]
        stage("gate_a", lambda g, b, i: act.activation(gate[:, ds(g, 1), :], bank[b][:, :], ACT.Sigmoid, bias=gate_b(g)).then_inc(ev_act, 1))
        stage("w_pa", None)
        act.wait_ge(ev_dve, LEAD + EV["gate_m"][1]["dve"])

        def merged_hi(i):
            for b in range(4):
                act.wait_ge(sem("mrg"), 4 * i + b + 1)
                act.activation(yz_hi[:, ds(4 * i + b, 1), :], merged[:, ds(4 * i + b, 1), :], ACT.Copy).then_inc(sem("mrg_hi"), 1)
        stage("gate_m", lambda g, b, i: act.activation(gate[:, ds(g, 1), :], bank[b][:, :], ACT.Sigmoid, bias=gate_b(g, 8)).then_inc(ev_act, 1),
              merged_hi)
        stage("w_out", None)
        norm(lambda k: res[:, k, :], dst=None, after="w_out")
        act.activation(silu_c[:, :, :], col[:, COL["c"]:COL["c"] + 16].rearrange("p (k n) -> p k n", n=2), ACT.Silu)\
           .then_inc(sem("silu_c"), 1)
        act.wait_ge(sem("mod_ready"), 1)
        act.dma_start(c_in, ctxt).then_inc(sem("ctx_in"), 16)
        act.dma_start(rope_t[:, :, :], rope_x).then_inc(sem("rope_in"), 16)
        act.dma_start(rope_u[:, :, :], rope_c).then_inc(sem("rope_in"), 16)
        act.dma_start(diff_t[:, :], diff).then_inc(sem("diff_in"), 16)

        def shift(m0, who=0):
            return lambda k: mod[:, m0 + k, who:who + 1]
        act.wait_ge(sem("ctx_in"), 16)
        norm(lambda k: c_in[:, k, :], n=CTX, shift=shift(0, 1), dst=c_hi)
        act.wait_ge(sem("x1_ready"), 1)
        norm(lambda k: res[:, k, :], shift=shift(0))
        act.wait_ge(sem("pad2_ready"), 1)
        stage("a_e", lambda g, b, i: act.activation(conv_u[:, b, 15:15 + S], bank[b][:, :], ACT.Copy).then_inc(ev_act, 1))

        def b_free(g, b, i):
            if b >= 2:
                act.wait_ge(sem("u_made"), b - 1)
            act.activation(sq[:, b % 2, :], bank[b][:, :], ACT.Sigmoid).then_inc(ev_act, 1)
        stage("b_e", b_free)

        def swapped(scale):
            def free(src, to, other):
                act.activation(to, src, ACT.Copy, scale=scale)
                act.activation(other[0:64], src[64:P], ACT.Copy, scale=scale)
                return act.activation(other[64:P], src[0:64], ACT.Copy, scale=scale)
            return free
        q_swap = swapped(P ** -0.5)
        stage("q_r", lambda g, b, i: q_swap(bank[b][:, :], q_r[:, g, :], g_r[:, g, :]).then_inc(ev_act, 1))
        k_swap = swapped(1.0)

        def k_free(g, b, i):
            h = g // 2
            if g % 2 == 0:
                k_swap(bank[b][:, :], k_r[:, h, :], v_r[:, h, :]).then_inc(ev_act, 1)
            else:
                swap = v_x[:, :, :].rearrange("p a (b n) -> p (a b) n", n=CTX)[:, h, :]
                k_swap(bank[b][:, :CTX], k_x[:, h, :], swap).then_inc(ev_act, 1)
        stage("k_r", k_free)

        def v_free(g, b, i):
            if g == 0:
                act.wait_ge(sem("roped"), 12)
            s, t = g // 6, g % 6
            dst = v_r[:, t, 256 * s:256 * s + 256] if t < 4 else v_x[:, t - 4, 256 * s:256 * s + 256]
            act.activation(dst, bank[b][:, 0:256], ACT.Copy).then_inc(ev_act, 1)
        stage("v_r", v_free)
        own(act.activation(lg[:, 8:16], col[:, COL["decay"]:COL["decay"] + 8], ACT.Abs))
        own(act.activation(lg[:, 16:24], lg[:, 8:16], ACT.Exp, scale=-1.0))
        act.activation(lg[:, 8:16], lg[:, 16:24], ACT.Ln, bias=1.0).then_inc(sem("lg_ln"), 1)
        stage("g_r", lambda g, b, i: act.activation(g_r[:, g, :], bank[b][:, :], ACT.Silu).then_inc(ev_act, 1))
        for h in range(4):
            act.wait_ge(sem("decay_arg"), h + 1)
            own(act.activation(decay[:, :], decay[:, :], ACT.Exp))
            for j in range(2):
                own(act.activation(decay_x[:, j, :], diff_t[:, S - P:], ACT.Exp, scale=lg[:, h:h + 1], bias=lg[:, 24 + 4 * j + h:25 + 4 * j + h]))
                if h or j:
                    act.wait_ge(sem("dx_used"), 2 * h + j)
                act.activation(tt[:, 0, :], diff_t[:, S - P:], ACT.Exp, scale=lg[:, 40 + h:41 + h], bias=lg[:, 32 + 4 * j + h:33 + 4 * j + h])\
                   .then_inc(sem("dx_ready"), 1)
        for h in range(4):
            act.wait_ge(sem("y_out"), h + 1)
            if h:
                act.wait_ge(sem("mix_lo"), h)
            act.activation(sq[:, h % 2, :], q_r[:, h, :], ACT.Square).then_inc(sem("ysq"), 1)
            act.wait_ge(sem("yvar"), h + 1)
            act.activation(root[:, :], var[:, :], ACT.Sqrt).then_inc(sem("yroot"), 1)
            act.wait_ge(sem("mix_f"), h + 1)
            act.activation(x_hi[:, h, :], tt[:, 0, :], ACT.Copy).then_inc(sem("mix_hi"), 1)
        for c in range(4):
            act.wait_ge(sem("conv_made"), 2 * (c // 2) + 2)
            if c >= 2:
                act.wait_ge(sem("csq_mm"), c - 1)
            act.activation(sq[:, c % 2, :], conv_c[:, c, :], ACT.Square).then_inc(sem("csq"), 1)
        act.wait_ge(sem("cvar"), 1)
        act.activation(root[:, :], var[:, :], ACT.Sqrt).then_inc(sem("croot"), 1)
        for c in range(4):
            act.wait_ge(sem("c_norm"), c + 1)
            own(act.activation(conv_c[:, c, :], conv_c[:, c, :], ACT.Silu, bias=c1("ln_b", c)))
            act.activation(x_hi[:, 4 + c, :], conv_c[:, c, :], ACT.Copy).then_inc(sem("mix_hi"), 1)
        stage("even_out", None)

        def ffn(i):
            norm(lambda k: res[:, k, :], shift=shift(48 * i + 24), after=("even_out", "odd_out")[i])
            before = EV[f"up{i}"][1]["dve"]

            n0, g0 = FIRST[f"up{i}"], GROUP0[f"up{i}"]
            with act.Fori(0, FF // 2) as j:
                for s in range(2):
                    n = 2 * j + s
                    split(n0 // 2 + j + (s + 1) // 2, 1 - s, 1 + g0 + 2 * n)
                    act.wait_ge(mm_done, 2 + g0 + 2 * n)
                    act.wait_ge(ev_dve, LEAD + before + n - 1)
                    act.activation(sq[:, s, :], bank[2 * s][:, :], ACT.Silu).then_inc(ev_act, 1)
                    act.wait_ge(ev_dve, LEAD + before + n + 1)
                    act.activation(hid_hi[:, ds(n, 1), :], tt[:, s, :], ACT.Copy).then_inc(sem("hid_h"), 1)
            stage(f"down{i}", None)
        ffn(0)

        act.wait_ge(mm_done, 1 + GROUP0["pool"])
        act.dma_start(inv_t[:, :, :], inv).then_inc(sem("odd_in"), 16)
        act.dma_start(sg_r[:, :, :], sg_rows).then_inc(sem("odd_in"), 16)
        act.dma_start(pool_ws[:, :, :], pool_w).then_inc(sem("odd_in"), 16)
        act.dma_start(sg_ws[:, :, :], sg_w).then_inc(sem("odd_in"), 16)
        norm(lambda k: res[:, k, :], shift=shift(48), after="down0")
        act.wait_ge(sem("pad3_ready"), 1)
        stage("pool", lambda g, b, i: act.activation(pc[:, g, 8:8 + S], bank[b][:, :], ACT.Copy).then_inc(ev_act, 1))
        stage("u_s", lambda g, b, i: act.activation(u_s[:, g, :], bank[b][:, :], ACT.Gelu).then_inc(ev_act, 1))
        stage("v_s", lambda g, b, i: act.activation(v_s[:, b, 256 * (g // 4):256 * (g // 4) + 256], bank[b][:, 0:256], ACT.Gelu)
              .then_inc(ev_act, 1))
        for g in range(4):
            act.wait_ge(sem("pool_mm"), g + 1)
            act.activation(x_hi[:, g, :], bank[4 + g % 2][:, :], ACT.Copy, scale=c1("pool_scale", g)).then_inc(sem("omix_hi"), 1)
        act.wait_ge(sem("sg_var"), 1)
        act.activation(bn[:, :, 8:9], bn[:, :, 7:8], ACT.Sqrt).then_inc(sem("sg_root"), 1)
        for g in range(4):
            act.wait_ge(sem("omix_f"), g + 1)
            act.activation(x_hi[:, 4 + g, :], tt[:, g % 2, :], ACT.Copy).then_inc(sem("omix_hi"), 1)
        stage("odd_out", None)
        ffn(1)
        norm(lambda k: res[:, k, :], dst=None, after="down1")

    @block.vector
    def _(dve):
        own = Tally(dve, sem("dve_own"))
        norms = [0, 0]

        def stage(name, free):
            g0, per = GROUP0[name], PER[name]
            blocks_ = COUNT[name]

            def pair(i):
                for s in range(2):
                    for m in range(per):
                        dve.wait_ge(mm_done, 2 + g0 + per * (2 * i + s) + m)
                        free(per * (2 * i + s) + m, (per * s + m) % 4, i)

            if blocks_ > 2:
                n0 = own.n
                with dve.Fori(0, blocks_ // 2) as i:
                    pair(i)
                assert own.n == n0, "no own waits in this loop"
            else:
                pair(0)

        def norm(src, scale, width=D, n=S, shift=None, dst=(x_hi, x_lo), into=None):
            v, w = norms
            dve.wait_ge(sem("sq_used"), 8 * v + 8)
            dve.tensor_scalar(var[:, :n], bank[4][:, :n], 1.0 / width, EPS, ALU.mult, ALU.add).then_inc(sem("var_ready"), 1)
            dve.wait_ge(sem("root_ready"), v + 1)
            own(dve.reciprocal(root[:, :n], root[:, :n]))
            norms[0] += 1
            for k in range(KT + 1):
                if k < KT:
                    if into is not None:
                        last = dve.scalar_tensor_tensor(into(k), src(k), scale(k), root[:, :n], ALU.mult, ALU.mult)
                        continue
                    if w or k >= 2:
                        dve.wait_ge(sem("xl_ready"), 8 * w + k - 1)
                    dve.scalar_tensor_tensor(tt[:, k % 2, :n], src(k), scale(k), root[:, :n], ALU.mult, ALU.mult)\
                       .then_inc(sem("t_ready"), 1)
                if k and into is None:
                    dve.wait_ge(sem("xh_ready"), 8 * w + k)
                    if shift is None:
                        dve.tensor_tensor(dst[1][:, k - 1, :n], tt[:, (k - 1) % 2, :n], dst[0][:, k - 1, :n].bitcast(F32), ALU.subtract)\
                           .then_inc(sem("xl_ready"), 1)
                    else:
                        dve.scalar_tensor_tensor(dst[1][:, k - 1, :n], tt[:, (k - 1) % 2, :n], shift(k - 1),
                                                 dst[0][:, k - 1, :n].bitcast(F32), ALU.add, ALU.subtract)\
                           .then_inc(sem("xl_ready"), 1)
            if into is not None:
                own(last)
            else:
                norms[1] += 1

        dve.sem_inc(ev_dve, LEAD)
        dve.sem_inc(sem("conv_done"), 4)
        dve.memset(ones[:, :], 1.0).then_inc(sem("ones_ready"), 1)
        dve.wait_ge(sem("consts"), 32)
        norm(lambda k: pb[:, k, :], lambda k: c1("g_in", k))
        dve.wait_ge(sem("fold_mm"), 1)
        own(dve.tensor_copy(w_g, bank[5][:, 0:128].rearrange("p (k g) -> p k g", g=8)))
        dve.tensor_copy(v_w[:, :, P:136], bank[5][:, 128:256].rearrange("p (k g) -> p k g", g=8)).then_inc(sem("fold_ready"), 1)
        own(dve.memset(g_tok, 0.0))
        dve.memset(conv_in[:, :, 0:3], 0.0).then_inc(sem("pad_ready"), 1)

        def cw(g, tap):
            return col[:, ds(g * 4 + (COL["conv_w"] + tap), 1)]

        n0 = own.n
        with dve.Fori(0, 4) as i:
            own.n = n0 + 20 * i
            for b in range(4):
                g = 4 * i + b
                dve.wait_ge(ev_act, LEAD + g + 1)
                dve.wait_ge(sem("xc_ready"), g + 1)
                y = conv_out[:, b, :]
                own(dve.tensor_scalar(y, conv_in[:, b, 0:S], cw(g, 0), col[:, ds(g + COL["conv_b"], 1)], ALU.mult, ALU.add))
                for tap in range(1, 4):
                    step = dve.scalar_tensor_tensor(y, conv_in[:, b, tap:tap + S], cw(g, tap), y, ALU.mult, ALU.add)
                    if tap < 3:
                        own(step)
                step.then_inc(sem("conv_done"), 1)
            for b in range(4):
                g = 4 * i + b
                dve.wait_ge(sem("vg_mm"), 4 + g + 1)
                for half in range(2):
                    src = bank[4 + 2 * (b % 2) + half]
                    part = src[:, 0:272].rearrange("p (t n) -> p t n", n=136)
                    dst = v_m[:, 2 * half:2 * half + 2, ds(g * P, P)]
                    dve.tensor_copy(dst, part[:, :, 0:P])
                    acc = g_tok[:, 2 * half:2 * half + 2, :]
                    step = dve.tensor_tensor(acc, acc, part[:, :, P:136], ALU.add)
                    if half == 0:
                        own(step)
                own(step)
                dve.sem_inc(sem("vg_done"), 1)
        own.n = n0 + 20 * 4

        dve.wait_ge(sem("gates_mm"), 1)
        own(dve.tensor_tensor(gs, bank[6][:, 0:32].rearrange("p (t g) -> p t g", g=8), g_tok, ALU.add))
        for t in range(4):
            last = dve.tensor_tensor(gs[:, t, :], gs[:, t, :], col[:, COL["b_if"]:COL["b_if"] + 8], ALU.add)
        own(last)
        dve.sem_inc(sem("g_ready"), 1)
        dve.wait_ge(sem("ln_ready"), 1)
        own(dve.tensor_scalar(lf, gs[:, :, 4:8], 0.0, None, ALU.min))
        dve.tensor_tensor(lf, lf, ga, ALU.subtract).then_inc(sem("lf_ready"), 1)
        dve.wait_ge(sem("b_mm"), 1)
        own(dve.tensor_copy(b_c, bank[6][:, 64:80].rearrange("p (t g) -> p t g", g=4)))
        dve.tensor_tensor(u_c, gs[:, :, 0:4], b_c, ALU.subtract).then_inc(sem("u_ready"), 1)
        dve.wait_ge(sem("rows_mm"), 1)
        own(dve.tensor_copy(sq[0:4, 0, :], bank[6][0:4, :]))
        own(dve.tensor_tensor_scan(sq[0:4, 1, :], sq[0:4, 0, :], sq[0:4, 0, :], 0.0, ALU.max, ALU.max))
        own(dve.tensor_scalar(rows[0:4, :], sq[0:4, 1, :], -1.0, None, ALU.mult))
        own(dve.tensor_tensor(root[0:4, :], bank[7][0:4, :], sq[0:4, 1, :], ALU.add))
        dve.tensor_copy(root[32:36, :], root[0:4, :]).then_inc(sem("bm_ready"), 1)

        for h in range(4):
            dve.wait_ge(sem("bc_mm"), h + 1)
            if h:
                dve.wait_ge(sem("y_done"), 4 * h)
            dve.tensor_copy(tt[:, 0, :], bank[6][:, :])
            for j in range(4):
                last = dve.tensor_tensor(tt[:, 1, P * j:P * j + P], bank[6][:, P * j:P * j + P], neg, ALU.add)
            own(last)
            own(dve.tensor_copy(var[:, :], bank[7][:, :]))
            dve.sem_inc(sem("nm_ready"), 1)
            for j in range(4):
                dve.wait_ge(sem("s_mm"), 4 * h + j + 1)
                dve.wait_ge(sem("e_done"), 4 * h + j + 1)
                n = S - P * j
                dve.tensor_tensor(p_t[:, j, :n], bank[4 + j % 2][:, :n], p_t[:, j, :n], ALU.mult).then_inc(sem("pt_done"), 1)
            dve.wait_ge(sem("abs_done"), h + 1)
            own(dve.tensor_tensor(var[:, :], var[:, :], root[:, :], ALU.max))
            own(dve.reciprocal(var[:, :], var[:, :]))
            dve.wait_ge(ev_act, LEAD + EV[f"o_m{h}"][1]["act"] + 4)
            for e in range(4):
                own(dve.tensor_tensor(q_t[:, e, :], q_t[:, e, :], var[:, :], ALU.mult))
                dve.wait_ge(sem("h_mm"), 4 * h + e + 1)
                dve.tensor_tensor(q_t[:, e, :], bank[HB[e]][:, :], q_t[:, e, :], ALU.mult).then_inc(sem("h_done"), 1)
            dve.wait_ge(sem("sum_mm"), h + 1)
            own(dve.tensor_scalar(tt[:, 0, :], bank[4][:, :], 1.0 / 512, None, ALU.mult))
            own(dve.tensor_tensor(tt[:, 1, :], tt[:, 0, :], tt[:, 0, :], ALU.mult))
            dve.wait_ge(sem("hs_mm"), 4 * h + 4)
            own(dve.scalar_tensor_tensor(root[:, :], bank[5][:, :], 1.0 / 512, tt[:, 1, :], ALU.mult, ALU.subtract))
            dve.tensor_scalar(root[:, :], root[:, :], EPS, None, ALU.add).then_inc(sem("hvar_ready"), 1)
            dve.wait_ge(sem("hroot_ready"), h + 1)
            own(dve.reciprocal(root[:, :], var[:, :]))
            for e in range(4):
                own(dve.tensor_tensor(q_t[:, e, :], q_t[:, e, :], tt[:, 0, :], ALU.subtract))
                own(dve.scalar_tensor_tensor(q_t[:, e, :], q_t[:, e, :], c1("g_head", 4 * h + e), root[:, :], ALU.mult, ALU.mult))
                own(dve.scalar_tensor_tensor(q_t[:, e, :], x_c[:, 4 * h + e, :], c1("skip", 4 * h + e), q_t[:, e, :], ALU.mult, ALU.add))
            for e in range(4):
                dve.wait_ge(ev_act, LEAD + EV[f"z_m{h}"][1]["act"] + e + 1)
                dve.tensor_tensor(q_t[:, e, :], q_t[:, e, :], sq[:, e % 2, :], ALU.mult).then_inc(sem("prod_done"), 1)
                dve.wait_ge(sem("yh_done"), 4 * h + e + 1)
                dve.tensor_tensor(y_lo[:, e, :], q_t[:, e, :], y_hi[:, e, :].bitcast(F32), ALU.subtract).then_inc(sem("y_done"), 1)

            def pb_free(g, b, i):
                if h == 0:
                    dve.tensor_copy(pb[:, g, :], bank[b][:, :]).then_inc(ev_dve, 1)
                else:
                    dve.tensor_tensor(pb[:, g, :], bank[b][:, :], pb[:, g, :], ALU.add).then_inc(ev_dve, 1)
            stage(f"w_pb{h}", pb_free)

        dve.wait_ge(mm_done, 1 + GROUP0["w_pb3"])
        own(dve.memset(rel_sb[32:33, :], 1.0))
        dve.sem_inc(sem("rel_one"), 1)

        def v_a_free(g, b, i):
            dve.tensor_copy(v_a[:, b, ds((g - b) * 64, 256)], bank[b][:, 0:256]).then_inc(ev_dve, 1)
        stage("v_a", v_a_free)

        def finish(h):
            own(dve.reciprocal(stat(h, 3), stat(h, 2)))
            dve.wait_ge(sem("pv_mm"), h + 1)
            dve.tensor_tensor(y_a[:, :, 64 * h:64 * h + 64], bank[7][:, 0:256].rearrange("p (t n) -> p t n", n=64),
                              stat(h, 3).unsqueeze(2).to_broadcast([P, 4, 64]), ALU.mult).then_inc(sem("ya_done"), 1)

        for h in range(16):
            dve.wait_ge(sem("qk_a_mm"), h + 1)
            dve.wait_ge(sem(f"strip_in{h % 2}"), 16 * (h // 2) + 16)
            if h:
                dve.wait_ge(sem("p_done"), h)
            for i in range(4):
                o, n = TRI_AT[i], P * (i + 1)
                src = bank[SB[i]][:, SO[i]:SO[i] + n]
                last = dve.tensor_tensor_reduce(s_r[:, o:o + n], src, strip[:, h % 2, S - n:S], 1.0, -3e38,
                                                ALU.add, ALU.max, stat(h, 0)[:, i:i + 1])
            own(last)
            dve.tensor_scalar(stat(h, 1), stat(h, 0), -1.0, None, ALU.mult).then_inc(sem("max_ready"), 1)
            if h:
                finish(h - 1)
            dve.wait_ge(sem("t_mm"), 3 * h + 3)
            dve.tensor_copy(p_c[:, S:S + 384], bank[5][:, 0:384])
            dve.tensor_copy(p_c[:, S + 384:TRI], bank[6][:, 0:384]).then_inc(sem("pc_dve"), 1)
        finish(15)
        for c in range(9):
            if c < 8:
                dve.wait_ge(ev_act, LEAD + EV["gate_a"][1]["act"])
                dve.wait_ge(sem("yt_mm"), c + 1)
                if c >= 2:
                    dve.wait_ge(sem("yz_l"), c - 1)
                dve.tensor_tensor(tt[:, c % 2, :].rearrange("p (t n) -> p t n", n=P), backward(4 + c % 4),
                                  z_a[:, c, :].rearrange("p (t n) -> p t n", n=P), ALU.mult).then_inc(sem("yz_f"), 1)
            if c:
                dve.wait_ge(sem("yz_h"), c)
                dve.tensor_tensor(yz_lo[:, c - 1, :], tt[:, (c - 1) % 2, :], yz_hi[:, c - 1, :].bitcast(F32), ALU.subtract)\
                   .then_inc(sem("yz_l"), 1)
        stage("w_pa", lambda g, b, i: dve.tensor_tensor(merged[:, ds(g, 1), :], bank[b][:, :], gate[:, ds(g, 1), :], ALU.mult)
              .then_inc(ev_dve, 1))
        dve.wait_ge(ev_dve, LEAD + EV["gate_m"][1]["dve"])
        n0 = own.n
        with dve.Fori(0, 2) as i:
            own.n = n0 + 4 * i
            for b in range(4):
                g = 4 * i + b
                dve.wait_ge(ev_act, LEAD + EV["gate_m"][1]["act"] + g + 1)
                own(dve.tensor_tensor(tt[:, b % 2, :], gate[:, ds(g, 1), :], pb[:, ds(g, 1), :], ALU.mult))
                dve.tensor_tensor(merged[:, ds(g, 1), :], merged[:, ds(g, 1), :], tt[:, b % 2, :], ALU.add).then_inc(sem("mrg"), 1)
            for b in range(4):
                g = 4 * i + b
                dve.wait_ge(sem("mrg_hi"), g + 1)
                dve.tensor_tensor(yz_lo[:, ds(g, 1), :], merged[:, ds(g, 1), :], yz_hi[:, ds(g, 1), :].bitcast(F32), ALU.subtract)\
                   .then_inc(sem("mrg_lo"), 1)
        own.n = n0 + 8
        dve.wait_ge(sem("res_in"), 16)
        stage("w_out", lambda g, b, i: dve.tensor_tensor(res[:, ds(g, 1), :], bank[b][:, :], res[:, ds(g, 1), :], ALU.add)
              .then_inc(ev_dve, 1))
        dve.wait_ge(ev_dve, LEAD + EV["a_e"][1]["dve"])
        dve.sem_inc(sem("merge_over"), 1)
        norm(lambda k: res[:, k, :], lambda k: c1("g_out", k), into=lambda k: res[:, k, :])
        dve.sem_inc(sem("x1_ready"), 1)
        dve.wait_ge(sem("ada_mm"), 48)
        own(dve.tensor_tensor(mod[:, :, :], bank[7][:, 0:192].rearrange("p (m n) -> p m n", n=2),
                              col[:, COL["ada_b"]:COL["ada_b"] + 96].unsqueeze(2).to_broadcast([P, 96, 2]), ALU.add))
        for j, (m0, w0, who) in enumerate(((8, 0, 0), (32, 8, 0), (56, 16, 0), (80, 24, 0), (8, 0, 1))):
            w0 += COL["norm_w"]
            last = dve.scalar_tensor_tensor(coef[:, j, :], mod[:, m0:m0 + 8, who], 1.0, col[:, w0:w0 + 8], ALU.add, ALU.mult)
        own(last)
        dve.sem_inc(sem("mod_ready"), 1)

        def shift(m0, who=0):
            return lambda k: mod[:, m0 + k, who:who + 1]
        own(dve.memset(conv_u[:, :, 0:15], 0.0))
        own(dve.memset(conv_u[:, :, 15 + S:CW], 0.0))
        dve.sem_inc(sem("pad2_ready"), 1)
        norm(lambda k: c_in[:, k, :], lambda k: coef[:, 4, k:k + 1], n=CTX, shift=shift(0, 1), dst=(c_hi, c_lo))
        norm(lambda k: res[:, k, :], lambda k: coef[:, 0, k:k + 1], shift=shift(0))
        for b in range(4):
            dve.wait_ge(ev_act, LEAD + EV["b_e"][1]["act"] + b + 1)
            last = dve.tensor_tensor(conv_u[:, b, 15:15 + S], conv_u[:, b, 15:15 + S], sq[:, b % 2, :], ALU.mult)
            last.then_inc(sem("u_made"), 1)

        def convolve(c0):
            w = COL["conv2_w"]
            dve.wait_ge(sem("u_made"), c0 + 2)
            for c in (c0, c0 + 1):
                last = dve.tensor_scalar(conv_c[:, c, :], conv_u[:, c, 0:S], col[:, w + 31 * c:w + 31 * c + 1], None, ALU.mult)
                last.then_inc(sem("tap"), 1)
            n = 60 * (c0 // 2) + 2 * (c0 // 2)
            with dve.Fori(0, 10) as i:
                for tap in range(3):
                    for k, c in enumerate((c0, c0 + 1)):
                        dve.wait_ge(sem("tap"), 6 * i + (n + 2 * tap + k + 1))
                        dve.scalar_tensor_tensor(conv_c[:, c, :], conv_u[:, c, ds(3 * i + (tap + 1), S)],
                                                 col[:, ds(3 * i + (w + 31 * c + tap + 1), 1)], conv_c[:, c, :], ALU.mult, ALU.add)\
                           .then_inc(sem("tap"), 1)
            dve.wait_ge(sem("tap"), n + 62)
            dve.sem_inc(sem("conv_made"), 2)

        def rope(x, other, table):
            own(dve.tensor_tensor(x, x, table[:, 0, :], ALU.mult))
            own(dve.tensor_tensor(other, other, table[:, 1, :], ALU.mult))
            dve.tensor_tensor(x, x, other, ALU.add).then_inc(sem("roped"), 1)
        convolve(0)
        dve.wait_ge(sem("rope_in"), 32)
        for h in range(4):
            dve.wait_ge(ev_act, LEAD + EV["q_r"][1]["act"] + h + 1)
            rope(q_r[:, h, :], g_r[:, h, :], rope_t)
        for h in range(4):
            dve.wait_ge(ev_act, LEAD + EV["k_r"][1]["act"] + 2 * h + 2)
            rope(k_r[:, h, :], v_r[:, h, :], rope_t)
            swap = v_x[:, :, :].rearrange("p a (b n) -> p (a b) n", n=CTX)[:, h, :]
            rope(k_x[:, h, :], swap, rope_u)
        convolve(2)
        dve.wait_ge(sem("lg_ln"), 1)
        own(dve.tensor_scalar(lg[:, 0:8], col[:, COL["decay"]:COL["decay"] + 8], 0.0, None, ALU.min))
        own(dve.tensor_tensor(lg[:, 0:8], lg[:, 0:8], lg[:, 8:16], ALU.subtract))
        for j in range(2):
            dve.tensor_scalar(lg[:, 24 + 4 * j:28 + 4 * j], lg[:, 0:4], float(CTX - P * j), None, ALU.mult)
            dve.tensor_scalar(lg[:, 32 + 4 * j:36 + 4 * j], lg[:, 4:8], float(S - 1 + P * j), None, ALU.mult)
        own(dve.tensor_scalar(lg[:, 40:44], lg[:, 4:8], -1.0, None, ALU.mult))
        dve.wait_ge(sem("diff_in"), 16)
        dve.tensor_scalar(ahead[:, :], diff_t[:, :], 0.0, None, ALU.max)
        own(dve.tensor_scalar(behind[:, :], diff_t[:, :], 1.0, 0.0, ALU.add, ALU.min))
        dve.wait_ge(mm_done, 1 + GROUP0["g_r"])
        for h in range(4):
            if h:
                dve.wait_ge(sem("yr_mm"), h)
            own(dve.tensor_scalar(decay[:, :], ahead[:, :], lg[:, h:h + 1], None, ALU.mult))
            own(dve.scalar_tensor_tensor(decay[:, :], behind[:, :], lg[:, 40 + h:41 + h], decay[:, :], ALU.mult, ALU.add))
            dve.sem_inc(sem("decay_arg"), 1)
            for j in range(2):
                dve.wait_ge(sem("dx_ready"), 2 * h + j + 1)
                own(dve.tensor_tensor(decay_x[:, j, :], decay_x[:, j, :], tt[:, 0, :], ALU.add))
                dve.sem_inc(sem("dx_used"), 1)
            for j in range(6):
                dve.wait_ge(sem("sr_mm"), 6 * h + j + 1)
                m = decay[:, S - P - P * j:TOEP - P * j] if j < 4 else decay_x[:, j - 4, :]
                dve.tensor_tensor(w_r[:, j, :], bank[4 + j % 2][:, :], m, ALU.mult).then_inc(sem("wr_done"), 1)
            dve.wait_ge(sem("yr_mm"), h + 1)
            dve.tensor_copy(q_r[:, h, :], bank[6][:, :]).then_inc(sem("y_out"), 1)
        for h in range(4):
            dve.wait_ge(sem("ysq_mm"), h + 1)
            dve.wait_ge(ev_act, LEAD + EV["g_r"][1]["act"] + 4)
            dve.tensor_scalar(var[:, :], bank[7][:, :], 1.0 / P, EPS, ALU.mult, ALU.add).then_inc(sem("yvar"), 1)
            own(dve.tensor_tensor(q_r[:, h, :], q_r[:, h, :], g_r[:, h, :], ALU.mult))
            dve.wait_ge(sem("yroot"), h + 1)
            own(dve.reciprocal(root[:, :], root[:, :]))
            dve.tensor_tensor(tt[:, 0, :], q_r[:, h, :], root[:, :], ALU.mult).then_inc(sem("mix_f"), 1)
            dve.wait_ge(sem("mix_hi"), h + 1)
            dve.tensor_tensor(x_lo[:, h, :], tt[:, 0, :], x_hi[:, h, :].bitcast(F32), ALU.subtract).then_inc(sem("mix_lo"), 1)
        dve.wait_ge(sem("mix_lo"), 4)
        dve.wait_ge(sem("csq_mm"), 4)
        own(dve.tensor_scalar(tt[:, 0, :], bank[4][:, :], 1.0 / 512, None, ALU.mult))
        own(dve.tensor_tensor(tt[:, 1, :], tt[:, 0, :], tt[:, 0, :], ALU.mult))
        own(dve.scalar_tensor_tensor(var[:, :], bank[5][:, :], 1.0 / 512, tt[:, 1, :], ALU.mult, ALU.subtract))
        own(dve.tensor_scalar(var[:, :], var[:, :], EPS, None, ALU.add))
        dve.sem_inc(sem("cvar"), 1)
        dve.wait_ge(sem("croot"), 1)
        own(dve.reciprocal(root[:, :], root[:, :]))
        for c in range(4):
            own(dve.tensor_tensor(conv_c[:, c, :], conv_c[:, c, :], tt[:, 0, :], ALU.subtract))
            dve.scalar_tensor_tensor(conv_c[:, c, :], conv_c[:, c, :], c1("ln_w", c), root[:, :], ALU.mult, ALU.mult)\
               .then_inc(sem("c_norm"), 1)
        for c in range(4):
            dve.wait_ge(sem("mix_hi"), 5 + c)
            dve.tensor_tensor(x_lo[:, 4 + c, :], conv_c[:, c, :], x_hi[:, 4 + c, :].bitcast(F32), ALU.subtract).then_inc(sem("mix_lo"), 1)

        def add_gated(name, m0):
            stage(name, lambda g, b, i: dve.scalar_tensor_tensor(res[:, ds(g, 1), :], bank[b][:, :], mod[:, ds(g + m0, 1), 0:1].rearrange("p a b -> p (a b)"),
                                                                 res[:, ds(g, 1), :], ALU.mult, ALU.add).then_inc(ev_dve, 1))
        add_gated("even_out", 16)

        def ffn(i):
            dve.wait_ge(ev_dve, LEAD + EV[f"up{i}"][1]["dve"])
            norm(lambda k: res[:, k, :], lambda k: coef[:, 2 * i + 1, k:k + 1], shift=shift(48 * i + 24))
            g0, before = GROUP0[f"up{i}"], EV[f"up{i}"][1]
            with dve.Fori(0, FF // 2) as j:
                for s in range(2):
                    n = 2 * j + s
                    dve.wait_ge(mm_done, 3 + g0 + 2 * n)
                    dve.wait_ge(ev_act, LEAD + before["act"] + n + 1)
                    dve.wait_ge(sem("hid_l"), FF * i + n + 1)
                    dve.tensor_tensor(tt[:, s, :], bank[2 * s + 1][:, :], sq[:, s, :], ALU.mult).then_inc(ev_dve, 1)
                    dve.wait_ge(sem("hid_h"), FF * i + n + 1)
                    dve.tensor_tensor(hid_lo[:, ds(n, 1), :], tt[:, s, :], hid_hi[:, ds(n, 1), :].bitcast(F32), ALU.subtract)\
                       .then_inc(sem("hid_l"), 1)
            g0 = GROUP0[f"down{i}"]
            m0 = 48 * i + 40
            with dve.Fori(0, 4) as j:
                for b in range(2):
                    dve.wait_ge(mm_done, 4 * j + (g0 + 2 * b + 3))
                    r = res[:, ds(2 * j + b, 1), :]
                    dve.scalar_tensor_tensor(r, bank[b][:, :], mod[:, ds(2 * j + (b + m0), 1), 0:1].rearrange("p a b -> p (a b)"), r, ALU.mult, ALU.add)\
                       .then_inc(ev_dve, 1)
        dve.sem_inc(sem("hid_l"), 2)
        ffn(0)

        own(dve.memset(pc[:, :, 0:8], 0.0))
        own(dve.memset(pc[:, :, 8 + S:PW], 0.0))
        dve.sem_inc(sem("pad3_ready"), 1)
        dve.wait_ge(ev_dve, LEAD + EV["pool"][1]["dve"])
        norm(lambda k: res[:, k, :], lambda k: coef[:, 2, k:k + 1], shift=shift(48))
        dve.wait_ge(sem("odd_in"), 64)
        for g, w in enumerate((2, 4, 8, 16)):
            dve.wait_ge(ev_act, LEAD + EV["pool"][1]["act"] + g + 1)
            src, n = pc[:, g, :], PW
            for step in range(g + 1):
                dst = (pool_a, pool_b)[step % 2][:, g, :]
                n -= 1 << step
                own(dve.tensor_tensor(dst[:, 0:n], src[:, 0:n], src[:, (1 << step):(1 << step) + n], ALU.add))
                src = dst
            own(dve.tensor_tensor(src[:, 8 - w // 2:8 - w // 2 + S], src[:, 8 - w // 2:8 - w // 2 + S], inv_t[:, g, :], ALU.mult))
            dve.tensor_tensor(pc[:, g, 8:8 + S], src[:, 8 - w // 2:8 - w // 2 + S], pc[:, g, 8:8 + S], ALU.subtract).then_inc(sem("m_ready"), 1)
        for t in range(4):
            dve.wait_ge(ev_act, LEAD + EV["v_s"][1]["act"] + 5 + t)
            own(dve.bn_stats(bn[:, t, 0:6], v_s[:, t, :]))
            own(dve.bn_aggr(bn[:, t, 6:8], bn[:, t, 0:6]))
        own(dve.tensor_scalar(bn[:, :, 7:8], bn[:, :, 7:8], EPS, None, ALU.add))
        dve.sem_inc(sem("sg_var"), 1)
        for g in range(4):
            dve.wait_ge(sem("omix_hi"), g + 1)
            dve.scalar_tensor_tensor(x_lo[:, g, :], bank[4 + g % 2][:, :], c1("pool_scale", g), x_hi[:, g, :].bitcast(F32), ALU.mult, ALU.subtract)\
               .then_inc(sem("omix_lo"), 1)
        dve.wait_ge(sem("sg_root"), 1)
        own(dve.reciprocal(bn[:, :, 9:10], bn[:, :, 8:9]))
        for t in range(4):
            v = v_s[:, t, :]
            own(dve.tensor_scalar(v, v, bn[:, t, 6:7], bn[:, t, 9:10], ALU.subtract, ALU.mult))
            own(dve.tensor_tensor(v, v, sg_r[:, 0, :], ALU.mult))
            dve.tensor_tensor(v, v, sg_r[:, 1, :], ALU.add).then_inc(sem("v_norm"), 1)
        for g in range(4):
            dve.wait_ge(sem("sg_mm"), g + 1)
            if g >= 2:
                dve.wait_ge(sem("omix_lo"), 4 + g - 1)
            t3 = tt[:, g % 2, :].rearrange("p (n q) -> p n q", q=P)
            own(dve.tensor_tensor(t3, bank[6 + g % 2][:, :].rearrange("p (n q) -> p n q", q=P),
                                  sg_r[:, 2, P * g:P * g + P].unsqueeze(1).to_broadcast([P, 4, P]), ALU.add))
            dve.tensor_tensor(tt[:, g % 2, :], tt[:, g % 2, :], u_s[:, g, :], ALU.mult).then_inc(sem("omix_f"), 1)
            dve.wait_ge(sem("omix_hi"), 5 + g)
            dve.tensor_tensor(x_lo[:, 4 + g, :], tt[:, g % 2, :], x_hi[:, 4 + g, :].bitcast(F32), ALU.subtract).then_inc(sem("omix_lo"), 1)
        add_gated("odd_out", 64)
        ffn(1)
        norm(lambda k: res[:, k, :], lambda k: c1("g_final", k), into=lambda k: res[:, k, :])
        dve.sem_inc(sem("out_ready"), 1)

    @block.tensor
    def _(pe):
        norms = [0, 0]
        pe.sem_inc(mm_done, 1)
        pe.sem_inc(sem("vg_mm"), 4)

        def three(dst, wh, wl, xh, xl, first, last):
            pe.matmul(dst, wh, xh, start=first, stop=False)
            pe.matmul(dst, wh, xl, start=False, stop=False)
            return pe.matmul(dst, wl, xh, start=False, stop=last)

        def bank_free(name, i, g):
            by, before = EV[name]
            if by == "act":
                pe.wait_ge(ev_act, LEAD + before["act"] + g - 3)
            else:
                pe.wait_ge(ev_dve, LEAD + before["dve"] + g - 3)

        def begin(name):
            pe.wait_ge(ev_act, LEAD + EV[name][1]["act"])
            pe.wait_ge(ev_dve, LEAD + EV[name][1]["dve"])

        def stage(name, xh=x_hi, xl=x_lo, kts=KT, between=None):
            n0, per = FIRST[name], PER[name]
            blocks_ = COUNT[name]
            begin(name)

            def pair(i):
                for s in range(2):
                    pe.wait_ge(lo_done, n0 + 2 * i + s + 1)
                    wh = w_hi[:, s, :].rearrange("p (k n) -> p k n", k=kts)
                    wl = w_lo[:, s, :].rearrange("p (k n) -> p k n", k=kts)
                    for m in range(per):
                        b = (per * s + m) % 4
                        bank_free(name, i, per * (2 * i + s) + m)
                        for k in range(kts):
                            last = three(bank[b][:, :], wh[:, k, P * m:P * m + P], wl[:, k, P * m:P * m + P],
                                         xh[:, k, :], xl[:, k, :], k == 0, k == kts - 1)
                        last.then_inc(mm_done, 1)
                if between:
                    between(i)
            if blocks_ > 2:
                with pe.Fori(0, blocks_ // 2) as i:
                    pair(i)
            else:
                pair(0)

        def norm(n=S):
            v = norms[0]
            if v:
                pe.wait_ge(sem("var_ready"), v)
            for k in range(KT):
                pe.wait_ge(sem("sq_ready"), 8 * v + k + 1)
                pe.matmul(bank[4][:, :n], ones[:, :], sq[:, k % 2, :n], start=(k == 0), stop=(k == KT - 1))\
                  .then_inc(sem("sq_used"), 1)
            norms[0] += 1

        pe.wait_ge(sem("ones_ready"), 1)
        pe.wait_ge(sem("bd_in"), 48)
        for g in range(16):
            pe.matmul(bank[5][:, 8 * g:8 * g + 8], bd_b[:, g, 0, :], wif[:, g, :], start=True, stop=False)
            pe.matmul(bank[5][:, 8 * g:8 * g + 8], bd_b[:, g, 1, :], wif[:, 16 + g, :], start=False, stop=True)
            last = pe.matmul(bank[5][:, 128 + 8 * g:136 + 8 * g], bd_b[:, g, 2, :], wif[:, 32 + g, :], start=True, stop=True)
        last.then_inc(sem("fold_mm"), 1)
        norm()
        pe.wait_ge(sem("fold_ready"), 1)
        pe.wait_ge(sem("xl_ready"), 8)

        def x_m_values(i):
            for b in range(4):
                g = 4 * i + b
                pe.wait_ge(ev_act, LEAD + g + 1)
                pe.wait_ge(sem("vg_done"), g - 1 + 2)
                for t in range(4):
                    last = pe.matmul(bank[4 + 2 * (b % 2) + t // 2][:, 136 * (t % 2):136 * (t % 2) + 136],
                                     conv_in[:, b, 3 + P * t:3 + P * t + P], v_w[:, ds(g, 1), :], start=True, stop=True)
                last.then_inc(sem("vg_mm"), 1)
        pe.sem_inc(sem("vg_done"), 2)
        stage("x_m", between=x_m_values)

        pe.wait_ge(sem("xc_ready"), 4 + 16)
        pe.wait_ge(sem("vg_done"), 2 + 16)
        for t in range(4):
            for g in range(16):
                last = pe.matmul(bank[6][:, 8 * t:8 * t + 8], x_c[:, g, P * t:P * t + P], w_g[:, g, :], start=(g == 0), stop=(g == 15))
        last.then_inc(sem("gates_mm"), 1)
        pe.wait_ge(sem("lf_ready"), 1)
        for t in range(4):
            for s in range(t + 1):
                last = pe.matmul(bank[6][:, 64 + 4 * t:68 + 4 * t], (tri if s == t else ones[:, :]), lf[:, s, :],
                                 start=(s == 0), stop=(s == t))
        last.then_inc(sem("b_mm"), 1)
        pe.wait_ge(sem("u_ready"), 1)
        for t in range(4):
            pe.transpose(bank[6][0:4, P * t:P * t + P], u_c[:, t, :], ident)
            last = pe.transpose(bank[7][0:4, P * t:P * t + P], b_c[:, t, :], ident)
        last.then_inc(sem("rows_mm"), 1)

        for h in range(4):
            pe.wait_ge(sem("bd_ready"), 16 * h + 16)
            if h:
                pe.wait_ge(sem("hvar_ready"), h)
            for j in range(8):
                if j >= 2:
                    pe.wait_ge(sem("qk_ev"), 8 * h + j - 1)
                last = pe.matmul(bank[4 + j % 2][:, :], bd[:, j % 4, j // 4, :], x_c[:, 4 * h + j % 4, :], start=True, stop=True)
                last.then_inc(sem("qk_mm"), 1)
            if h == 0:
                pe.wait_ge(sem("rows_ready"), 1)
            pe.matmul(bank[6][:, :], ident[0:4, h:h + 1].to_broadcast([4, P]), rows[0:4, :], start=True, stop=True)
            pe.matmul(bank[7][:, :], ident[32:36, 32 + h:33 + h].to_broadcast([4, P]), rows[32:36, :], start=True, stop=True)\
              .then_inc(sem("bc_mm"), 1)
            pe.wait_ge(sem("qk_ev"), 8 * h + 8)
            pe.sem_inc(sem("qk_used"), 1)
            for j in range(4):
                if j >= 2:
                    pe.wait_ge(sem("pt_done"), 4 * h + j - 1)
                for c in range(4):
                    last = pe.matmul(bank[4 + j % 2][:, :S - P * j], k_t[:, c, P * j:P * j + P], q_t[:, c, P * j:S],
                                     start=(c == 0), stop=(c == 3))
                last.then_inc(sem("s_mm"), 1)
            stage(f"o_m{h}")
            pe.wait_ge(sem("nm_ready"), h + 1)
            pe.wait_ge(sem("pt_done"), 4 * h + 4)
            for j in range(4):
                last = pe.matmul(bank[6][:, P * j:S], ones[:, :], p_t[:, j, :S - P * j], start=(j == 0), stop=(j == 3))
            last.then_inc(sem("den_mm"), 1)
            for e in range(4):
                if e == 3:
                    pe.wait_ge(sem("abs_done"), h + 1)
                for j in range(4):
                    last = pe.matmul(bank[HB[e]][:, P * j:S], v_m[:, j, P * (4 * h + e):P * (4 * h + e) + P],
                                     p_t[:, j, :S - P * j], start=(j == 0), stop=(j == 3))
                last.then_inc(sem("h_mm"), 1)
            pe.wait_ge(sem("h_done"), 4 * h + 4)
            for e in range(4):
                last = pe.matmul(bank[4][:, :], ones[:, :], q_t[:, e, :], start=(e == 0), stop=(e == 3))
            last.then_inc(sem("sum_mm"), 1)
            for e in range(4):
                pe.wait_ge(sem("hsq_ready"), 4 * h + e + 1)
                pe.matmul(bank[5][:, :], ones[:, :], sq[:, e % 2, :], start=(e == 0), stop=(e == 3)).then_inc(sem("hs_mm"), 1)
            stage(f"z_m{h}")
            pe.wait_ge(sem("y_done"), 4 * h + 4)
            stage(f"w_pb{h}", y_hi, y_lo, kts=4)

        pe.wait_ge(sem("rel_in"), 32)
        pe.wait_ge(sem("rel_one"), 1)
        pe.matmul(bank[4][0:16, :], rel_sb[:, :], hot_sb[:, 0:S], start=True, stop=True)
        pe.matmul(bank[5][0:16, 0:P], rel_sb[:, :], hot_sb[:, S:], start=True, stop=True).then_inc(sem("bias_mm"), 1)
        stage("q_a")
        stage("k_a")

        def stage_tokens(name):
            n0 = FIRST[name]
            begin(name)

            def pair(i):
                for s in range(2):
                    pe.wait_ge(lo_done, n0 + 2 * i + s + 1)
                    wh = w_hi[:, s, :].rearrange("p (k n) -> p k n", k=KT)
                    wl = w_lo[:, s, :].rearrange("p (k n) -> p k n", k=KT)
                    for t in range(4):
                        bank_free(name, i, 4 * (2 * i + s) + t)
                        for k in range(KT):
                            c = slice(P * t, P * t + P)
                            d = bank[t][:, 0:256]
                            pe.matmul(d, x_hi[:, k, c], wh[:, k, :], start=(k == 0), stop=False)
                            pe.matmul(d, x_hi[:, k, c], wl[:, k, :], start=False, stop=False)
                            last = pe.matmul(d, x_lo[:, k, c], wh[:, k, :], start=False, stop=(k == KT - 1))
                        last.then_inc(mm_done, 1)
            if COUNT[name] > 2:
                with pe.Fori(0, COUNT[name] // 2) as i:
                    pair(i)
            else:
                pair(0)
        stage_tokens("v_a")
        begin("z_a")

        def head(h):
            return slice(64 * (h % 2), 64 * (h % 2) + 64), h // 2
        for h in range(-1, 16):
            if h + 1 < 16:
                r, c = head(h + 1)
                if h >= 0:
                    pe.wait_ge(sem("max_ready"), h + 1)
                for i in range(4):
                    n = P * (i + 1)
                    last = pe.matmul(bank[SB[i]][:, SO[i]:SO[i] + n], q_a[r, c, P * i:P * i + P], k_a[r, c, 0:n], start=True, stop=True)
                last.then_inc(sem("qk_a_mm"), 1)
            if h >= 0:
                pe.wait_ge(sem("p_done"), h + 1)
                if h:
                    pe.wait_ge(sem("pc_act"), h)
                    pe.wait_ge(sem("pc_dve"), h)
                else:
                    pe.wait_ge(sem("bias_ready"), 1)
                for j, (b, o) in enumerate(((4, 0), (5, 0), (6, 0), (6, 256))):
                    for i in range(j, 4):
                        last = pe.transpose(bank[b][:, o + P * (i - j):o + P * (i - j) + P],
                                            p_r[:, TRI_AT[i] + P * j:TRI_AT[i] + P * j + P], ident)
                    if j != 2:
                        last.then_inc(sem("t_mm"), 1)
            if h >= 0:
                pe.wait_ge(sem("pc_act"), h + 1)
                pe.wait_ge(sem("pc_dve"), h + 1)
                if h:
                    pe.wait_ge(sem("ya_done"), h)
                for i in range(4):
                    for j in range(i + 1):
                        o = PC_AT[j] + P * (i - j)
                        last = pe.matmul(bank[7][:, 64 * i:64 * i + 64], p_c[:, o:o + P], v_a[:, j, 64 * h:64 * h + 64],
                                         start=(j == 0), stop=(j == i))
                last.then_inc(sem("pv_mm"), 1)
        stage("z_a")
        pe.wait_ge(sem("ya_done"), 16)
        for c in range(8):
            if c >= 4:
                pe.wait_ge(sem("yz_f"), c - 3)
            for t in range(4):
                last = pe.transpose(bank[4 + c % 4][:, P * t:P * t + P], y_a[:, t, P * c:P * c + P], ident)
            last.then_inc(sem("yt_mm"), 1)
        stage("gate_a")
        pe.wait_ge(sem("yz_l"), 8)
        stage("w_pa", yz_hi, yz_lo)
        stage("gate_m")
        pe.wait_ge(sem("mrg_lo"), 8)
        stage("w_out", yz_hi, yz_lo)
        begin("a_e")
        norm()
        pe.wait_ge(sem("silu_c"), 1)
        with pe.Fori(0, 12) as i:
            for n in range(4):
                pe.wait_ge(sem(f"ada_in{n}"), 16 * i + 16)
                w = ada_w[:, n, :].rearrange("p (k m) -> p k m", k=KT)
                for m in range(2):
                    for k in range(KT):
                        last = pe.matmul(bank[7][:, ds(16 * i + 4 * n + 2 * m, 2)], w[:, k, P * m:P * m + P], silu_c[:, k, :],
                                         start=(k == 0), stop=(k == KT - 1))
                last.then_inc(sem("ada_mm"), 1)

        norm(CTX)
        norm()
        pe.wait_ge(sem("xl_ready"), 24)
        stage("a_e")
        stage("b_e")
        stage("q_r")

        begin("k_r")
        for s in range(2):
            pe.wait_ge(lo_done, FIRST["k_r"] + s + 1)
            wh = w_hi[:, s, :].rearrange("p (k n) -> p k n", k=KT)
            wl = w_lo[:, s, :].rearrange("p (k n) -> p k n", k=KT)
            for m in range(2):
                for j, (xh, xl, n) in enumerate(((x_hi, x_lo, S), (c_hi, c_lo, CTX))):
                    bank_free("k_r", 0, 4 * s + 2 * m + j)
                    for k in range(KT):
                        last = three(bank[2 * m + j][:, :n], wh[:, k, P * m:P * m + P], wl[:, k, P * m:P * m + P],
                                     xh[:, k, :], xl[:, k, :], k == 0, k == KT - 1)
                    last.then_inc(mm_done, 1)
        begin("v_r")
        for s in range(2):
            pe.wait_ge(lo_done, FIRST["v_r"] + s + 1)
            wh = w_hi[:, s, :].rearrange("p (k n) -> p k n", k=KT)
            wl = w_lo[:, s, :].rearrange("p (k n) -> p k n", k=KT)
            for t in range(6):
                bank_free("v_r", 0, 6 * s + t)
                d = bank[(6 * s + t) % 4][:, 0:256]
                ah, al = (x_hi, x_lo) if t < 4 else (c_hi, c_lo)
                c = slice(P * (t % 4), P * (t % 4) + P)
                for k in range(KT):
                    last = three(d, ah[:, k, c], al[:, k, c], wh[:, k, :], wl[:, k, :], k == 0, k == KT - 1)
                last.then_inc(mm_done, 1)
        stage("g_r")
        pe.wait_ge(sem("roped"), 12)
        begin("even_out")
        for h in range(4):
            for j in range(6):
                if j >= 2:
                    pe.wait_ge(sem("wr_done"), 6 * h + j - 1)
                key = k_r[:, h, P * j:P * j + P] if j < 4 else k_x[:, h, P * (j - 4):P * (j - 4) + P]
                pe.matmul(bank[4 + j % 2][:, :], key, q_r[:, h, :], start=True, stop=True).then_inc(sem("sr_mm"), 1)
            pe.wait_ge(sem("wr_done"), 6 * h + 6)
            if h:
                pe.wait_ge(sem("y_out"), h)
            for j in range(6):
                v = v_r[:, j, P * h:P * h + P] if j < 4 else v_x[:, j - 4, P * h:P * h + P]
                last = pe.matmul(bank[6][:, :], v, w_r[:, j, :], start=(j == 0), stop=(j == 5))
            last.then_inc(sem("yr_mm"), 1)
        for h in range(4):
            pe.wait_ge(sem("ysq"), h + 1)
            if h:
                pe.wait_ge(sem("yvar"), h)
            pe.matmul(bank[7][:, :], ones[:, :], sq[:, h % 2, :], start=True, stop=True).then_inc(sem("ysq_mm"), 1)
        pe.wait_ge(sem("conv_made"), 4)
        for c in range(4):
            pe.matmul(bank[4][:, :], ones[:, :], conv_c[:, c, :], start=(c == 0), stop=(c == 3))
        for c in range(4):
            pe.wait_ge(sem("csq"), c + 1)
            pe.matmul(bank[5][:, :], ones[:, :], sq[:, c % 2, :], start=(c == 0), stop=(c == 3)).then_inc(sem("csq_mm"), 1)
        pe.wait_ge(sem("mix_lo"), 8)
        stage("even_out")

        def ffn(i):
            norm()
            pe.wait_ge(sem("xl_ready"), 8 * (4, 6)[i])
            name = f"up{i}"
            begin(name)
            n0, before = FIRST[name], EV[name][1]
            with pe.Fori(0, FF // 2) as j:
                for s in range(2):
                    n = 2 * j + s
                    pe.wait_ge(lo_done, n + (n0 + 1))
                    for m in range(2):
                        pe.wait_ge((ev_act, ev_dve)[m], n + (LEAD + before[("act", "dve")[m]] - 1))
                        for k in range(KT):
                            o = 256 * k + P * m
                            last = three(bank[2 * s + m][:, :], w_hi[:, s, o:o + P], w_lo[:, s, o:o + P],
                                         x_hi[:, k, :], x_lo[:, k, :], k == 0, k == KT - 1)
                        last.then_inc(mm_done, 1)
            name = f"down{i}"
            begin(name)
            pe.wait_ge(sem("hid_l"), 2 + FF * (i + 1))
            n0, before = FIRST[name], EV[name][1]["dve"]
            with pe.Fori(0, 4) as j:
                for b in range(2):
                    pe.wait_ge(ev_dve, 2 * j + (LEAD + before + b - 1))
                    for s in range(2):
                        pe.wait_ge(lo_done, 4 * j + (n0 + 2 * b + s + 1))
                        for k in range(FF // 2):
                            last = three(bank[b][:, :], w_hi[:, s, P * k:P * k + P], w_lo[:, s, P * k:P * k + P],
                                         hid_hi[:, FF // 2 * s + k, :], hid_lo[:, FF // 2 * s + k, :],
                                         s == 0 and k == 0, s == 1 and k == FF // 2 - 1)
                        last.then_inc(mm_done, 1)
        ffn(0)

        norm()
        pe.wait_ge(sem("xl_ready"), 40)
        stage("pool")
        stage("u_s")
        stage_tokens("v_s")
        pe.wait_ge(sem("odd_in"), 64)
        for g in range(4):
            pe.wait_ge(sem("m_ready"), g + 1)
            if g >= 2:
                pe.wait_ge(sem("omix_lo"), g - 1)
            pe.matmul(bank[4 + g % 2][:, :], pool_ws[:, g, :], pc[:, g, 8:8 + S], start=True, stop=True).then_inc(sem("pool_mm"), 1)
        pe.wait_ge(sem("v_norm"), 4)
        for g in range(4):
            if g >= 2:
                pe.wait_ge(sem("omix_f"), g - 1)
            for n in range(4):
                last = pe.matmul(bank[6 + g % 2][:, P * n:P * n + P], v_s[:, n, P * g:P * g + P], sg_ws[:, g, :], start=True, stop=True)
            last.then_inc(sem("sg_mm"), 1)
        pe.wait_ge(sem("omix_lo"), 8)
        stage("odd_out")
        ffn(1)
        norm()
def rope_table(seq, row, col):
    parts = []
    for p, n in zip((seq, row, col), ROPE_PAIRS):
        freq = np.float32(10000.0) ** (-np.arange(n, dtype=np.float32) / np.float32(n))
        parts.append(freq[:, None] * p[None, :].astype(np.float32))
    ang = np.concatenate(parts, 0)
    return np.concatenate([np.cos(ang), np.cos(ang)], 0), np.concatenate([-np.sin(ang), np.sin(ang)], 0)


def shape_tables():
    f = np.float32
    p = np.arange(P)
    dist = S - 1 - np.arange(S + P)
    d0 = np.maximum(dist, 0)
    large = 16 + (np.log(np.maximum(d0, 16).astype(f) / f(16)) / f(math.log(128.0)) * f(16)).astype(np.int32)
    bucket = np.where(d0 < 16, d0, np.minimum(large, 31))
    times = 1 * (d0 <= 128) + 1 * (d0 % 4 == 0) + 1 * (d0 % 16 == 0)
    hot = np.zeros((33, S + P), f)
    hot[bucket, np.arange(S + P)] = 1.0
    hot[32] = np.where((dist >= 0) & (times > 0), np.log(np.maximum(times, 1)), -1e30)
    t = np.arange(S)
    x_cos, x_sin = rope_table(np.full(S, float(CTX), f), t // 64, t % 64)
    c_cos, c_sin = rope_table(np.arange(CTX), np.zeros(CTX), np.zeros(CTX))
    inv = np.zeros((4, S), f)
    for g, w in enumerate((2, 4, 8, 16)):
        lo, hi = np.clip(t - w // 2, 0, S - 1), np.clip(t + w - 1 - w // 2, 0, S - 1)
        inv[g] = 1.0 / (hi - lo + 1)
    square = np.stack([np.eye(P, dtype=f), (p[:, None] <= p[None, :]).astype(f),
                       np.where(p[None, :] >= p[:, None], 0.0, -1e30).astype(f)], 1)
    diff = (np.arange(TOEP)[None, :] - (S - P) - p[:, None]).astype(f)
    return dict(square=square, hot=hot, diff=diff,
                rope_x=np.stack([x_cos, x_sin], 1).astype(f), rope_c=np.stack([c_cos, c_sin], 1).astype(f),
                inv=np.ascontiguousarray(np.broadcast_to(inv[None], (P, 4, S))))


def column_pack(v):
    col = lambda a: np.asarray(a).reshape(-1, P).T
    row = lambda a: np.broadcast_to(np.asarray(a).reshape(1, -1), (P, np.asarray(a).size))
    parts = {
        "g_in": col(v["norm_in_g"]), "g_out": col(v["norm_out_g"]), "gate_b": col(v["gate_b"]),
        "conv_w": v["conv_w"][0].reshape(4, 16, P).transpose(2, 1, 0).reshape(P, 64),
        "conv_b": col(v["conv_b"]), "g_head": col(v["head_norm_g"]), "skip": col(v["skip_m"]),
        "b_if": row(v["b_if"]),
        "c": np.stack([v["c_2"].reshape(8, P).T, v["c_ctx_2"].reshape(8, P).T], 2).reshape(P, 16),
        "ada_b": col(v["ada_b_2"]), "norm_w": col(v["norm_w_2"]), "decay": row(v["ret_decay_logit_2"]),
        "conv2_w": v["conv_dw_w_2"][0].reshape(31, 4, P).transpose(2, 1, 0).reshape(P, 124),
        "ln_w": col(v["conv_ln_w_2"]), "ln_b": col(v["conv_ln_b_2"]),
        "pool_scale": col(v["pool_scale_2"]), "g_final": col(v["final_norm_w_2"]),
    }
    assert {k: a.shape[1] for k, a in parts.items()} == WIDTHS
    return np.ascontiguousarray(np.concatenate(list(parts.values()), 1))


def weight_blocks(v):
    def cols(w, lo, hi, k=8):
        n = 2048 // k
        w = w[:, lo:hi].reshape(k, P, (hi - lo) // n, n)
        return w.transpose(2, 1, 0, 3).reshape(-1, P, 2048)
    w_in, even, odd = v["w_in"][0], v["even_w_in_2"][0], v["odd_w_in_2"][0]
    out = [cols(w_in, 4096, 6144)]
    for h in range(4):
        o = 512 * h
        out += [cols(w_in, 8192 + o, 8704 + o), cols(w_in, 6144 + o, 6656 + o), cols(v["w_pb"][0][o:o + 512], 0, 1024, 4)]
    out += [cols(w_in, 0, 3072), cols(w_in, 3072, 4096), cols(w_in, 10240, 11264), cols(v["w_pa"][0], 0, 1024),
            cols(w_in, 11264, 12288), cols(v["w_out"][0], 0, 1024)]
    out += [cols(even, 2048, 3072), cols(even, 0, 2048), cols(v["even_w_out_2"][0], 0, 1024)]

    def ffn(i):
        gate, up, down = v["ffn_w_gate_2"][i], v["ffn_w_up_2"][i], v["ffn_w_down_2"][i]
        both = np.stack([gate.reshape(8, P, 22, P), up.reshape(8, P, 22, P)], 3)
        d = down.reshape(2, 11, P, 8, P).transpose(3, 0, 2, 1, 4).reshape(16, P, 1408)
        full = np.zeros((16, P, 2048), d.dtype)
        full[:, :, :1408] = d
        return [both.transpose(2, 1, 0, 3, 4).reshape(22, P, 2048), full]
    out += ffn(0)
    out += [cols(odd, 0, 1536), cols(v["odd_w_out_2"][0], 0, 1024)]
    out += ffn(1)
    return np.concatenate(out, 0)


def block_diagonal(w):
    out = np.zeros((16, 32, 4, 32, 4), w.dtype)
    b = np.arange(32)
    out[:, b, :, b, :] = w.reshape(16, 32, 4, 4).transpose(1, 0, 2, 3)
    return out.reshape(16, P, P)


def lay_out(v):
    tiles = lambda a, n: np.ascontiguousarray(a.T.reshape(8, P, n).transpose(1, 0, 2))
    q, k, w = (block_diagonal(v[n][0]) for n in ("wq_m", "wk_m", "wv_m"))
    qk = np.stack([q, k], 1).reshape(4, 4, 2, P, P).transpose(3, 0, 1, 2, 4).reshape(P, 4, 1024)
    back = np.stack([q, k, w], 1).transpose(3, 0, 1, 2).reshape(P, 16 * 3 * P)
    ada = v["ada_w_2"].reshape(2, 8, P, 24, 256).transpose(0, 3, 2, 1, 4).reshape(48, P, 2048)
    return dict(
        xt=tiles(v["x"][0], S), ctxt=tiles(v["ctx_2"][0], CTX), cols=column_pack(v), blocks=weight_blocks(v),
        bd_qk=np.ascontiguousarray(qk), bd_v=np.ascontiguousarray(w.transpose(1, 0, 2)),
        bd_back=np.ascontiguousarray(back), w_if=np.ascontiguousarray(v["w_if"][0].reshape(48, P, 8).transpose(1, 0, 2)),
        sg_rows=np.ascontiguousarray(np.broadcast_to(np.stack([v["sg_ln_w_2"].reshape(-1), v["sg_ln_b_2"].reshape(-1),
                                                               v["sg_b_2"].reshape(-1)])[None], (P, 3, 512))),
        rel=np.ascontiguousarray(v["rel_bias"]), ada=np.ascontiguousarray(ada),
        pool_w=np.ascontiguousarray(v["pool_w_2"][0].transpose(1, 0, 2)),
        sg_w=np.ascontiguousarray(v["sg_w_2"][0].transpose(2, 0, 1)), **shape_tables())


def kernel(**inputs):
    import concourse.bacc as bacc
    from concourse.bass_utils import run_bass_kernel_spmd

    nc = bacc.Bacc("TRN2", target_bir_lowering=False, num_devices=1)
    arrays = lay_out({k: np.asarray(v) for k, v in inputs.items()})
    aps = {k: nc.dram_tensor(k, a.shape, F32, kind="ExternalInput").ap() for k, a in arrays.items()}
    aps["out"] = nc.dram_tensor("out", (D, S), F32, kind="ExternalOutput").ap()
    program(nc, **aps)
    r = run_bass_kernel_spmd(nc, [arrays], core_ids=[0])
    return np.ascontiguousarray(r.results[0]["out"].T)[None]
```

```python
import math
from contextlib import ExitStack

import concourse.bass as bass
import numpy as np
from concourse import mybir

P = 128
S = 512
CTX = 256
D = 1024
KT = D // P
EPS = 1e-6
HB = (4, 5, 7, 6)
ROPE_PAIRS = (16, 24, 24)
TOEP = 2 * S - P
TRI = 10 * P
TRI_AT = (0, P, 3 * P, 6 * P)
PC_AT = (0, 4 * P, 7 * P, 9 * P)
SB, SO = (2, 2, 1, 0), (256, 0, 0, 0)
FF = 22
CW = S + 30
PW = S + 16
F32 = mybir.dt.float32
F32R = mybir.dt.float32r
ALU = mybir.AluOpType
ACT = mybir.ActivationFunctionType
AX = mybir.AxisListType
ds = bass.ds

WIDTHS = dict(g_in=8, g_out=8, gate_b=16, conv_w=64, conv_b=16, g_head=16, skip=16, b_if=8, ada_b=96,
              norm_w=32, decay=8, conv2_w=124, ln_w=4, ln_b=4, pool_scale=4, g_final=8)
COL, at = {}, 0
for name, width in WIDTHS.items():
    COL[name] = at
    at += width
NCOL = at

STAGES = [("x_m", 8, 2)]
for h in range(4):
    STAGES += [(f"o_m{h}", 2, 2), (f"z_m{h}", 2, 2), (f"w_pb{h}", 2, 4)]
STAGES += [("q_a", 4, 2), ("k_a", 4, 2), ("v_a", 4, 4), ("z_a", 4, 2), ("gate_a", 4, 2), ("w_pa", 4, 2), ("gate_m", 4, 2),
           ("w_out", 4, 2), ("a_e", 2, 2), ("b_e", 2, 2), ("q_r", 2, 2), ("k_r", 2, 4), ("v_r", 2, 6), ("g_r", 2, 2), ("even_out", 4, 2),
           ("up0", 22, 2), ("down0", 16, 1), ("pool", 2, 2), ("u_s", 2, 2), ("v_s", 2, 4), ("odd_out", 4, 2),
           ("up1", 22, 2), ("down1", 16, 1)]
FIRST, GROUP0, PER = {}, {}, {}
nb = ng = 0
for name, blocks, groups in STAGES:
    FIRST[name], GROUP0[name], PER[name] = nb, ng, groups
    nb += blocks
    ng += blocks * groups
ADA_AT = {name: 4 * j for j, name in enumerate(("q_a", "k_a", "v_a", "z_a", "gate_a", "w_pa", "gate_m", "w_out"))}
ADA = 32
COUNT = {name: blocks for name, blocks, _ in STAGES}


class Tally:

    def __init__(self, engine, sem):
        self.engine, self.sem, self.n = engine, sem, 0

    def __call__(self, instruction):
        instruction.then_inc(self.sem, 1)
        self.n = self.n + 1
        self.engine.wait_ge(self.sem, self.n)


def program(nc, xt, ctxt, cols, blocks, bd_qk, bd_v, fold_w, fold_c, c_rows, rel, ada, pool_w, sg_w, sg_rows, square, hot,
            diff, rope_x, rope_c, inv, out):
    ctx = ExitStack()
    with ctx:
        body(nc, ctx, xt, ctxt, cols, blocks, bd_qk, bd_v, fold_w, fold_c, c_rows, rel, ada, pool_w, sg_w, sg_rows, square, hot,
             diff, rope_x, rope_c, inv, out)


def body(nc, ctx, xt, ctxt, cols, blocks, bd_qk, bd_v, fold_w, fold_c, c_rows, rel, ada, pool_w, sg_w, sg_rows, square, hot,
         diff, rope_x, rope_c, inv, out):
    def sb(name, shape, dt=F32, stack=ctx):
        return stack.enter_context(nc.sbuf_tensor(name, shape, dt))

    sems = {}

    def sem(name):
        if name not in sems:
            sems[name] = ctx.enter_context(nc.semaphore(name))
        return sems[name]

    raw = sb("raw", [P, 2, 2048])
    w_hi = sb("w_hi", [P, 2, 2048], F32R)
    w_lo = sb("w_lo", [P, 2, 2048], F32R)
    x_hi = sb("x_hi", [P, KT, S], F32R)
    x_lo = sb("x_lo", [P, KT, S], F32R)
    col = sb("col", [P, NCOL])
    sq_c = sb("sq_c", [P, 2, P])
    mod = sb("mod", [P, 96])
    ada_col = sb("ada_col", [P, 8])
    mod_c = sb("mod_c", [P, 16])
    coef = sb("coef", [P, 5, 8])
    ones = sb("ones", [P, P])
    sq = sb("sq", [P, 2, S])
    tt = sb("tt", [P, 2, S])
    vr = sb("vr", [P, 2, S])
    var, root = vr[:, 0, :], vr[:, 1, :]
    low = sb("low", [P, KT * S])
    def c1(name, j):
        return col[:, COL[name] + j:COL[name] + j + 1]

    def stat(h, what):
        o = 16 * (h % 4) + 4 * what
        return sq[:, 0, o:o + 4]

    def backward(b):
        a = bank[b][:, :]
        return bass.AP(a.tensor, a.offset + P - 1, [list(a.ap[0]), [P, 4], [-1, P]])

    ident, tri = sq_c[:, 0, :], sq_c[:, 1, :]

    m1, m2, m3 = ExitStack(), ExitStack(), ExitStack()
    pb = sb("pb", [P, KT, S], stack=m1)
    fold = sb("fold", [P, 3, P, 4], stack=m2)
    fold_b = sb("fold_b", [P, 3, 16, 4], stack=m2)
    fold_s = sb("fold_s", [P, 3, P], stack=m2)
    m2.close()
    m2 = ExitStack()
    v_m = sb("v_m", [P, 4, 2048], stack=m2)
    x_c = sb("x_c", [P, 16, S], stack=m2)
    k_t = sb("k_t", [P, 4, S], stack=m3)
    p_t = sb("p_t", [P, 4, S], stack=m3)
    m3.close()
    m3 = ExitStack()
    y_hi = sb("y_hi", [P, 4, S], F32R, stack=m3)
    y_lo = sb("y_lo", [P, 4, S], F32R, stack=m3)
    m3.close()
    m2.close()

    a1, a2 = ExitStack(), ExitStack()
    k_a = sb("k_a", [P, KT, S], stack=a1)
    v_a = sb("v_a", [P, 4, D], stack=a1)
    y_a = sb("y_a", [P, 4, D], stack=a1)
    s_r = sb("s_r", [P, TRI], stack=a2)
    p_r = sb("p_r", [P, TRI], stack=a2)
    p_c = sb("p_c", [P, TRI], stack=a2)
    strip = sb("strip", [P, 2, S], stack=a2)
    ada_w = sb("ada_w", [P, 3, D], stack=a2)
    a2.close()
    hot_sb = sb("hot_sb", [33, S + P], stack=a2)
    rel_sb = sb("rel_sb", [33, 16], stack=a2)
    bias_v = sb("bias_v", [16, S + P], stack=a2)
    a2.close()
    a1.close()
    a1 = ExitStack()
    yz_lo = sb("yz_lo", [P, KT, S], F32R, stack=a1)
    sb("gap", [P, 2 * KT * S], stack=a1)
    yz_hi = sb("yz_hi", [P, KT, S], F32R, stack=a1)
    a1.close()
    m1.close()
    q_a = low[:, :].rearrange("p (k n) -> p k n", n=S)
    z_a = res = q_a
    gate = v_a[:, :, :].rearrange("p t (a n) -> p (t a) n", n=S)
    merged = y_a[:, :, :].rearrange("p t (a n) -> p (t a) n", n=S)
    c_x = vr[:, :, :].rearrange("p a n -> p (a n)")
    spare = p_r[:, P:P + D]
    c_ctx = p_c[:, 0:D]
    skew = nc.dram_tensor("skew", (16, S + P), F32, kind="Internal").ap()

    e1 = ExitStack()
    conv_c = sb("conv_c", [P, 4, S], stack=e1)
    conv_u = sb("conv_u", [P, 4, CW], stack=e1)
    q_r = sb("q_r", [P, 4, S], stack=e1)
    k_r = sb("k_r", [P, 4, S], stack=e1)
    v_r = sb("v_r", [P, 4, S], stack=e1)
    g_r = sb("g_r", [P, 4, S], stack=e1)
    k_x = sb("k_x", [P, 4, CTX], stack=e1)
    v_x = sb("v_x", [P, 2, S], stack=e1)
    rope_t = sb("rope_t", [P, 2, S], stack=e1)
    rope_u = sb("rope_u", [P, 2, CTX], stack=e1)
    diff_t = sb("diff_t", [P, TOEP], stack=e1)
    ahead = sb("ahead", [P, TOEP], stack=e1)
    behind = sb("behind", [P, TOEP], stack=e1)
    lg = sb("lg", [P, 48], stack=e1)
    e2 = ExitStack()
    c_hi = sb("c_hi", [P, KT, CTX], F32R, stack=e2)
    c_lo = sb("c_lo", [P, KT, CTX], F32R, stack=e2)
    e2.close()
    e2 = ExitStack()
    w_r = sb("w_r", [P, 6, S], stack=e2)
    decay = sb("decay", [P, TOEP], stack=e2)
    decay_x = sb("decay_x", [P, 2, S], stack=e2)
    e2.close()
    e1.close()
    c_in = g_r[:, :, :].rearrange("p a (b n) -> p (a b) n", n=CTX)
    f1 = ExitStack()
    hid_hi = sb("hid_hi", [P, FF, S], F32R, stack=f1)
    hid_lo = sb("hid_lo", [P, FF, S], F32R, stack=f1)
    f1.close()
    o1 = ExitStack()
    pc = sb("pc", [P, 4, PW], stack=o1)
    pool_a = sb("pool_a", [P, 4, PW], stack=o1)
    pool_b = sb("pool_b", [P, 4, PW], stack=o1)
    u_s = sb("u_s", [P, 4, S], stack=o1)
    v_s = sb("v_s", [P, 4, S], stack=o1)
    inv_t = sb("inv_t", [P, 4, S], stack=o1)
    sg_r = sb("sg_r", [P, 3, S], stack=o1)
    pool_ws = sb("pool_ws", [P, 4, P], stack=o1)
    sg_ws = sb("sg_ws", [P, 4, P], stack=o1)
    bn = sb("bn", [P, 4, 16], stack=o1)
    o1.close()
    conv_out = k_t
    conv_in = pb[:, 0:5, :].rearrange("p a b -> p (a b)")[:, 0:4 * 516].rearrange("p (b n) -> p b n", n=516)
    q_t = low[:, 0:2048].rearrange("p (c n) -> p c n", n=S)
    bd = low[:, 2048:3072].rearrange("p (c w n) -> p c w n", w=2, n=P)
    v_w = low[:, 0:2176].rearrange("p (k n) -> p k n", n=136)
    small = low[:, 3072:4096]
    g_tok = small[:, 0:32].rearrange("p (t g) -> p t g", g=8)
    w_g = small[:, 32:160].rearrange("p (k g) -> p k g", g=8)
    lf = small[:, 160:176].rearrange("p (t g) -> p t g", g=4)
    u_c = small[:, 176:192].rearrange("p (t g) -> p t g", g=4)
    b_c = small[:, 192:208].rearrange("p (t g) -> p t g", g=4)
    gs = small[:, 208:240].rearrange("p (t g) -> p t g", g=8)
    ga = small[:, 240:256].rearrange("p (t g) -> p t g", g=4)
    gb = small[:, 256:272].rearrange("p (t g) -> p t g", g=4)
    neg = small[:, 784:912]
    rows = small[0:64, 272:784]

    bank = [ctx.enter_context(nc.psum_tensor(f"bank{i}", [P, S], F32)) for i in range(8)]

    raw_in = [sem("raw_in0"), sem("raw_in1")]
    hi_done, lo_done, mm_done = sem("hi_done"), sem("lo_done"), sem("mm_done")
    ev_act, ev_dve = sem("ev_act"), sem("ev_dve")
    LEAD = 4
    evs = {"act": 0, "dve": 0}
    EV = {}
    for name, blocks_, groups in STAGES:
        base = name.rstrip("0123")
        if base == "up":
            EV[name] = ("both", dict(evs))
            evs["act"] += blocks_
            evs["dve"] += blocks_
            continue
        by = "act" if base in ("x_m", "o_m", "z_m", "z_a", "gate_a", "q_a", "k_a", "gate_m", "a_e", "b_e", "q_r", "k_r", "v_r", "g_r", "pool", "u_s", "v_s") else "dve"
        EV[name] = (by, dict(evs))
        n = blocks_ * groups // (2 if base == "down" else 1)
        evs[by] += n
    block = ctx.enter_context(nc.Block())
    LAST = STAGES[-1][0]
    BLOCKS = FIRST[LAST] + COUNT[LAST]

    @block.sync
    def _(sp):
        def stream(lo, hi):
            with sp.Fori((lo - 2) // 2, (hi - 2) // 2) as i:
                for s in range(2):
                    sp.wait_ge(lo_done, 2 * i + s + 1)
                    sp.dma_start(raw[:, s, :], blocks[ds(2 * i + s + 2, 1)].rearrange("a p n -> p (a n)"))\
                      .then_inc(raw_in[s], 16)

        for s in range(2):
            sp.dma_start(raw[:, s, :], blocks[s]).then_inc(raw_in[s], 16)
        a0 = FIRST["q_a"]
        stream(2, a0)
        with sp.Fori(0, ADA // 2) as i:
            for s in range(2):
                n = 2 * i + s
                sp.wait_ge(lo_done, n + (a0 - 1))
                sp.dma_start(raw[:, s, :], blocks[ds(n + a0, 1)].rearrange("a p n -> p (a n)")).then_inc(raw_in[s], 16)
                for r in range(3):
                    sp.wait_ge(sem(f"ada_sum{r}"), n + 1)
                    sp.dma_start(ada_w[:, r, :], ada[ds(3 * n + r, 1)].rearrange("a p d -> p (a d)"))\
                      .then_inc(sem(f"ada_in{r}"), 16)
        stream(a0 + ADA, BLOCKS)
        sp.wait_ge(sem("out_ready"), 1)
        sp.dma_start(out.rearrange("(k p) n -> p k n", p=P), low[:, :].rearrange("p (k n) -> p k n", n=S))\
          .then_inc(sem("out_sent"), 16)
        sp.wait_ge(sem("out_sent"), 16)

    @block.gpsimd
    def _(pool):
        with pool.Fori(0, BLOCKS // 2) as i:
            for s in range(2):
                pool.wait_ge(hi_done, 2 * i + s + 1)
                pool.tensor_tensor(w_lo[:, s, :], raw[:, s, :], w_hi[:, s, :].bitcast(F32), ALU.subtract)\
                    .then_inc(lo_done, 1)

    @block.scalar
    def _(act):
        own = Tally(act, sem("act_own"))

        def split(n, s, after):
            act.wait_ge(raw_in[s], 16 * n + 16)
            act.wait_ge(mm_done, after)
            act.activation(w_hi[:, s, :], raw[:, s, :], ACT.Copy).then_inc(hi_done, 1)

        def stage(name, free, between=None):
            n0, g0, per = FIRST[name], GROUP0[name], PER[name]
            blocks_ = COUNT[name]

            def pair(i, last=False):
                for s in range(2):
                    if not (last and s == 1):
                        split(n0 // 2 + i + (s + 1) // 2, 1 - s, 1 + g0 + per * (2 * i + s))
                    if free:
                        for m in range(per):
                            act.wait_ge(mm_done, 2 + g0 + per * (2 * i + s) + m)
                            free(per * (2 * i + s) + m, (per * s + m) % 4, i)
                if between:
                    between(i)

            pairs = blocks_ // 2
            whole = pairs - 1 if name == LAST else pairs
            if whole > 1:
                with act.Fori(0, whole) as i:
                    pair(i)
            elif whole == 1:
                pair(0)
            if name == LAST:
                pair(whole, last=True)

        act.sem_inc(ev_act, LEAD)
        act.sem_inc(sem("xc_ready"), 4)
        for k in range(0, KT, 4):
            act.dma_start(pb[:, k:k + 4, :], xt[:, k:k + 4, :]).then_inc(sem(f"x_in{k}"), 16)
        act.dma_start(col[:, :], cols).then_inc(sem("consts"), 16)
        act.dma_start(sq_c[:, :, :], square[:, 0:2, :]).then_inc(sem("consts"), 16)
        act.dma_start(neg, square[:, 2, :]).then_inc(sem("consts"), 16)
        act.dma_start(fold[:, :, :, :], fold_w).then_inc(sem("fold_in"), 16)
        act.dma_start(fold_b[:, :, :, :], fold_c).then_inc(sem("fold_in"), 16)
        act.dma_start(v_w[:, :, 0:P], bd_v).then_inc(sem("bd_in"), 16)
        norms = [0, 0]

        def norm(src, n=S, shift=None, dst=x_hi, after=None, first_split=False):
            v, w = norms
            for k in range(KT):
                if v or k >= 2:
                    act.wait_ge(sem("sq_used"), 8 * v + k - 1)
                if after:
                    act.wait_ge(ev_dve, LEAD + EV[after][1]["dve"] + k + 1)
                act.activation(sq[:, k % 2, :n], src(k), ACT.Square).then_inc(sem("sq_ready"), 1)
            act.wait_ge(sem("sq_used"), 8 * v + 8)
            act.activation(var[:, :n], bank[4][:, :n], ACT.Ln, scale=1.0 / D, bias=EPS).then_inc(sem("var_ready"), 1)
            act.wait_ge(sem("var_ready"), v + 1)
            act.activation(root[:, :n], var[:, :n], ACT.Exp, scale=-0.5).then_inc(sem("root_ready"), 1)
            norms[0] += 1
            if first_split:
                act.wait_ge(raw_in[0], 16)
                act.activation(w_hi[:, 0, :], raw[:, 0, :], ACT.Copy).then_inc(hi_done, 1)
            if dst is None:
                return
            for k in range(KT):
                act.wait_ge(sem("t_ready"), 8 * w + k + 1)
                if shift is None:
                    act.activation(dst[:, k, :n], tt[:, k % 2, :n], ACT.Copy).then_inc(sem("xh_ready"), 1)
                else:
                    act.activation(dst[:, k, :n], tt[:, k % 2, :n], ACT.Identity, bias=shift(k)).then_inc(sem("xh_ready"), 1)
            norms[1] += 1

        def x_tile(k):
            if k % 4 == 0:
                act.wait_ge(sem(f"x_in{k}"), 16)
            return pb[:, k, :]
        norm(x_tile, first_split=True)

        def x_m_free(g, b, i):
            act.wait_ge(sem("conv_done"), 4 * i + b + 1)
            act.wait_ge(sem("vg_mm"), 4 * i + b + 1)
            act.activation(conv_in[:, b, 3:3 + S], bank[b][:, :], ACT.Copy).then_inc(ev_act, 1)

        def x_m_silu(i):
            for b in range(4):
                act.wait_ge(sem("conv_done"), 4 + 4 * i + b + 1)
                act.activation(x_c[:, ds(4 * i + b, 1), :], conv_out[:, b, :], ACT.Silu).then_inc(sem("xc_ready"), 1)

        act.wait_ge(sem("pad_ready"), 1)
        stage("x_m", x_m_free, x_m_silu)

        def load_bd(h):
            act.dma_start(bd, bd_qk[:, h, :].rearrange("p (c w n) -> p c w n", w=2, n=P)).then_inc(sem("bd_ready"), 16)

        def query_key(h):
            for j in range(8):
                act.wait_ge(sem("qk_mm"), 8 * h + j + 1)
                dst = (q_t, k_t)[j // 4][:, j % 4, :]
                act.activation(dst, bank[4 + j % 2][:, :], ACT.Copy, scale=1.0 if j < 4 else 512 ** -0.5)\
                   .then_inc(sem("qk_ev"), 1)

        act.wait_ge(mm_done, 1 + GROUP0["o_m0"])
        act.wait_ge(sem("vg_done"), 2 + 16)
        load_bd(0)
        query_key(0)
        act.wait_ge(sem("g_ready"), 1)
        own(act.activation(ga, gs[:, :, 4:8], ACT.Abs))
        own(act.activation(gb, ga, ACT.Exp, scale=-1.0))
        act.activation(ga, gb, ACT.Ln, bias=1.0).then_inc(sem("ln_ready"), 1)
        act.wait_ge(sem("bm_ready"), 1)
        act.activation(rows[32:36, :], root[32:36, :], ACT.Exp, scale=-1.0).then_inc(sem("rows_ready"), 1)

        for h in range(4):
            if h:
                act.wait_ge(mm_done, 1 + GROUP0[f"o_m{h}"])
                act.wait_ge(sem("y_done"), 4 * h)
                query_key(h)
            act.wait_ge(sem("nm_ready"), h + 1)
            for j in range(4):
                last = act.activation(p_t[:, j, 0:P], tt[:, 1, P * j:P * j + P], ACT.Exp, bias=u_c[:, j, h:h + 1])
                if j < 3:
                    last = act.activation(p_t[:, j, P:S - P * j], tt[:, 0, P * j + P:S], ACT.Exp, bias=u_c[:, j, h:h + 1])
                last.then_inc(sem("e_done"), 1)
            act.wait_ge(sem("s_mm"), 4 * h + 4)
            if h < 3:
                load_bd(h + 1)
            stage(f"o_m{h}", lambda g, b, i: act.activation(q_t[:, b, :], bank[b][:, :], ACT.Sigmoid).then_inc(ev_act, 1))
            act.wait_ge(sem("den_mm"), h + 1)
            act.activation(root[:, :], bank[6][:, :], ACT.Abs).then_inc(sem("abs_done"), 1)
            for e in range(4):
                act.wait_ge(sem("h_done"), 4 * h + e + 1)
                if e >= 2:
                    act.wait_ge(sem("hs_mm"), 4 * h + e - 1)
                act.activation(sq[:, e % 2, :], q_t[:, e, :], ACT.Square).then_inc(sem("hsq_ready"), 1)
            act.wait_ge(sem("hvar_ready"), h + 1)
            own(act.activation(var[:, :], root[:, :], ACT.Ln, bias=EPS))
            act.activation(root[:, :], var[:, :], ACT.Exp, scale=-0.5).then_inc(sem("hroot_ready"), 1)
            act.wait_ge(sem("hs_mm"), 4 * h + 4)

            def z_free(g, b, i):
                if b >= 2:
                    act.wait_ge(sem("prod_done"), 4 * h + b - 1)
                act.activation(sq[:, b % 2, :], bank[b][:, :], ACT.Silu).then_inc(ev_act, 1)
                act.wait_ge(sem("prod_done"), 4 * h + b + 1)
                act.activation(y_hi[:, b, :], q_t[:, b, :], ACT.Copy).then_inc(sem("yh_done"), 1)
            stage(f"z_m{h}", z_free)
            if h == 3:
                act.wait_ge(sem("y_done"), 16)
                act.dma_start(rel_sb[0:32, :], rel).then_inc(sem("rel_in"), 16)
                act.dma_start(hot_sb[:, :], hot).then_inc(sem("rel_in"), 16)
                act.dma_start(c_x, c_rows[:, 0, :]).then_inc(sem("c_in"), 16)
                act.dma_start(c_ctx, c_rows[:, 1, :]).then_inc(sem("c_in"), 16)
            stage(f"w_pb{h}", None)

        act.wait_ge(sem("c_in"), 32)
        act.activation(c_ctx, c_ctx, ACT.Silu)
        act.activation(c_x, c_x, ACT.Silu).then_inc(sem("silu_c"), 1)
        act.wait_ge(sem("bias_mm"), 1)
        act.activation(bias_v[:, 0:S], bank[4][0:16, :], ACT.Copy)
        act.activation(bias_v[:, S:], bank[5][0:16, 0:P], ACT.Copy).then_inc(sem("bias_ready"), 1)
        act.wait_ge(sem("bias_ready"), 1)
        act.dma_start(skew, bias_v[:, :]).then_inc(sem("skew_out"), 16)

        def load_strip(h):
            src = bass.AP(skew.tensor, h * (S + P), [[1, P], [1, S]])
            act.dma_start(strip[:, h % 2, :], src).then_inc(sem(f"strip_in{h % 2}"), 16)
        stage("q_a", lambda g, b, i: act.activation(q_a[:, ds(g, 1), :].rearrange("p a (t n) -> p (a t) n", n=P), backward(b), ACT.Copy, scale=0.125)
              .then_inc(ev_act, 1))
        act.wait_ge(sem("skew_out"), 16)
        load_strip(0)
        load_strip(1)
        stage("k_a", lambda g, b, i: act.activation(k_a[:, ds(g, 1), :], bank[b][:, :], ACT.Copy).then_inc(ev_act, 1))
        stage("v_a", None)
        def pc_half(h):
            act.wait_ge(sem("t_mm"), 3 * h + 1)
            if h:
                act.wait_ge(sem("pv_mm"), h)
            act.activation(p_c[:, 0:S], bank[4][:, :], ACT.Copy).then_inc(sem("pc_act"), 1)

        for h in range(16):
            if h:
                pc_half(h - 1)
                act.wait_ge(sem("t_mm"), 3 * h)
            act.wait_ge(sem("max_ready"), h + 1)
            for i in range(4):
                o = TRI_AT[i]
                last = act.activation(p_r[:, o:o + P * (i + 1)], s_r[:, o:o + P * (i + 1)], ACT.Exp,
                                      bias=stat(h, 1)[:, i:i + 1], accum_out=stat(h, 2)[:, i:i + 1])
            last.then_inc(sem("p_done"), 1)
            if h < 14:
                load_strip(h + 2)
        pc_half(15)
        act.wait_ge(sem("qk_a_mm"), 16)
        stage("z_a", lambda g, b, i: act.activation(z_a[:, ds(g, 1), :], bank[b][:, :], ACT.Silu).then_inc(ev_act, 1))
        for c in range(8):
            act.wait_ge(sem("yz_f"), c + 1)
            act.activation(yz_hi[:, c, :], tt[:, c % 2, :], ACT.Copy).then_inc(sem("yz_h"), 1)
        act.wait_ge(sem("yz_l"), 8)
        act.dma_start(res, xt).then_inc(sem("res_in"), 16)

        def gate_b(g, more=0):
            return col[:, ds(g + (COL["gate_b"] + more), 1)]
        stage("gate_a", lambda g, b, i: act.activation(gate[:, ds(g, 1), :], bank[b][:, :], ACT.Sigmoid, bias=gate_b(g)).then_inc(ev_act, 1))
        stage("w_pa", None)
        act.wait_ge(ev_dve, LEAD + EV["gate_m"][1]["dve"])

        def merged_hi(i):
            for b in range(4):
                act.wait_ge(sem("mrg"), 4 * i + b + 1)
                act.activation(yz_hi[:, ds(4 * i + b, 1), :], merged[:, ds(4 * i + b, 1), :], ACT.Copy).then_inc(sem("mrg_hi"), 1)
        stage("gate_m", lambda g, b, i: act.activation(gate[:, ds(g, 1), :], bank[b][:, :], ACT.Sigmoid, bias=gate_b(g, 8)).then_inc(ev_act, 1),
              merged_hi)
        stage("w_out", None)
        act.wait_ge(sem("ada_sum2"), 1 + ADA)
        norm(lambda k: res[:, k, :], dst=None, after="w_out")
        act.wait_ge(sem("mod_ready"), 1)
        act.dma_start(c_in, ctxt).then_inc(sem("ctx_in"), 16)
        act.dma_start(rope_t[:, :, :], rope_x).then_inc(sem("rope_in"), 16)
        act.dma_start(rope_u[:, :, :], rope_c).then_inc(sem("rope_in"), 16)
        act.dma_start(diff_t[:, :], diff).then_inc(sem("diff_in"), 16)

        def shift(m0, who=0):
            return lambda k: (mod_c if who else mod)[:, m0 + k:m0 + k + 1]
        act.wait_ge(sem("ctx_in"), 16)
        norm(lambda k: c_in[:, k, :], n=CTX, shift=shift(0, 1), dst=c_hi)
        act.wait_ge(sem("x1_ready"), 1)
        norm(lambda k: res[:, k, :], shift=shift(0))
        act.wait_ge(sem("pad2_ready"), 1)
        stage("a_e", lambda g, b, i: act.activation(conv_u[:, b, 15:15 + S], bank[b][:, :], ACT.Copy).then_inc(ev_act, 1))

        def b_free(g, b, i):
            if b >= 2:
                act.wait_ge(sem("u_made"), b - 1)
            act.activation(sq[:, b % 2, :], bank[b][:, :], ACT.Sigmoid).then_inc(ev_act, 1)
        stage("b_e", b_free)

        def swapped(scale):
            def free(src, to, other):
                act.activation(to, src, ACT.Copy, scale=scale)
                act.activation(other[0:64], src[64:P], ACT.Copy, scale=scale)
                return act.activation(other[64:P], src[0:64], ACT.Copy, scale=scale)
            return free
        q_swap = swapped(P ** -0.5)
        stage("q_r", lambda g, b, i: q_swap(bank[b][:, :], q_r[:, g, :], g_r[:, g, :]).then_inc(ev_act, 1))
        k_swap = swapped(1.0)

        def k_free(g, b, i):
            h = g // 2
            if g % 2 == 0:
                k_swap(bank[b][:, :], k_r[:, h, :], v_r[:, h, :]).then_inc(ev_act, 1)
            else:
                swap = v_x[:, :, :].rearrange("p a (b n) -> p (a b) n", n=CTX)[:, h, :]
                k_swap(bank[b][:, :CTX], k_x[:, h, :], swap).then_inc(ev_act, 1)
        stage("k_r", k_free)

        def v_free(g, b, i):
            if g == 0:
                act.wait_ge(sem("roped"), 12)
            s, t = g // 6, g % 6
            dst = v_r[:, t, 256 * s:256 * s + 256] if t < 4 else v_x[:, t - 4, 256 * s:256 * s + 256]
            act.activation(dst, bank[b][:, 0:256], ACT.Copy).then_inc(ev_act, 1)
        stage("v_r", v_free)
        own(act.activation(lg[:, 8:16], col[:, COL["decay"]:COL["decay"] + 8], ACT.Abs))
        own(act.activation(lg[:, 16:24], lg[:, 8:16], ACT.Exp, scale=-1.0))
        act.activation(lg[:, 8:16], lg[:, 16:24], ACT.Ln, bias=1.0).then_inc(sem("lg_ln"), 1)
        stage("g_r", lambda g, b, i: act.activation(g_r[:, g, :], bank[b][:, :], ACT.Silu).then_inc(ev_act, 1))
        for h in range(4):
            act.wait_ge(sem("decay_arg"), h + 1)
            own(act.activation(decay[:, :], decay[:, :], ACT.Exp))
            for j in range(2):
                own(act.activation(decay_x[:, j, :], diff_t[:, S - P:], ACT.Exp, scale=lg[:, h:h + 1], bias=lg[:, 24 + 4 * j + h:25 + 4 * j + h]))
                if h or j:
                    act.wait_ge(sem("dx_used"), 2 * h + j)
                act.activation(tt[:, 0, :], diff_t[:, S - P:], ACT.Exp, scale=lg[:, 40 + h:41 + h], bias=lg[:, 32 + 4 * j + h:33 + 4 * j + h])\
                   .then_inc(sem("dx_ready"), 1)
        for h in range(4):
            act.wait_ge(sem("y_out"), h + 1)
            if h:
                act.wait_ge(sem("mix_lo"), h)
            act.activation(sq[:, h % 2, :], q_r[:, h, :], ACT.Square).then_inc(sem("ysq"), 1)
            act.wait_ge(sem("ysq_mm"), h + 1)
            act.activation(var[:, :], bank[7][:, :], ACT.Ln, scale=1.0 / P, bias=EPS).then_inc(sem("yvar"), 1)
            act.wait_ge(sem("yvar"), h + 1)
            act.activation(root[:, :], var[:, :], ACT.Exp, scale=-0.5).then_inc(sem("yroot"), 1)
            act.wait_ge(sem("mix_f"), h + 1)
            act.activation(x_hi[:, h, :], tt[:, 0, :], ACT.Copy).then_inc(sem("mix_hi"), 1)
        for c in range(4):
            act.wait_ge(sem("conv_made"), 2 * (c // 2) + 2)
            if c >= 2:
                act.wait_ge(sem("csq_mm"), c - 1)
            act.activation(sq[:, c % 2, :], conv_c[:, c, :], ACT.Square).then_inc(sem("csq"), 1)
        act.wait_ge(sem("cvar"), 1)
        own(act.activation(root[:, :], var[:, :], ACT.Ln, bias=EPS))
        act.activation(root[:, :], root[:, :], ACT.Exp, scale=-0.5).then_inc(sem("croot"), 1)
        for c in range(4):
            act.wait_ge(sem("c_norm"), c + 1)
            own(act.activation(conv_c[:, c, :], conv_c[:, c, :], ACT.Silu, bias=c1("ln_b", c)))
            act.activation(x_hi[:, 4 + c, :], conv_c[:, c, :], ACT.Copy).then_inc(sem("mix_hi"), 1)
        stage("even_out", None)

        def ffn(i):
            norm(lambda k: res[:, k, :], shift=shift(48 * i + 24), after=("even_out", "odd_out")[i])
            before = EV[f"up{i}"][1]["dve"]

            n0, g0 = FIRST[f"up{i}"], GROUP0[f"up{i}"]
            with act.Fori(0, FF // 2) as j:
                for s in range(2):
                    n = 2 * j + s
                    split(n0 // 2 + j + (s + 1) // 2, 1 - s, 1 + g0 + 2 * n)
                    act.wait_ge(mm_done, 2 + g0 + 2 * n)
                    act.wait_ge(ev_dve, LEAD + before + n - 1)
                    act.activation(sq[:, s, :], bank[2 * s][:, :], ACT.Silu).then_inc(ev_act, 1)
                    act.wait_ge(ev_dve, LEAD + before + n + 1)
                    act.activation(hid_hi[:, ds(n, 1), :], tt[:, s, :], ACT.Copy).then_inc(sem("hid_h"), 1)
            stage(f"down{i}", None)
        ffn(0)

        act.wait_ge(mm_done, 1 + GROUP0["pool"])
        act.dma_start(inv_t[:, :, :], inv).then_inc(sem("odd_in"), 16)
        act.dma_start(sg_r[:, :, :], sg_rows).then_inc(sem("odd_in"), 16)
        act.dma_start(pool_ws[:, :, :], pool_w).then_inc(sem("odd_in"), 16)
        act.dma_start(sg_ws[:, :, :], sg_w).then_inc(sem("odd_in"), 16)
        norm(lambda k: res[:, k, :], shift=shift(48), after="down0")
        act.wait_ge(sem("pad3_ready"), 1)
        stage("pool", lambda g, b, i: act.activation(pc[:, g, 8:8 + S], bank[b][:, :], ACT.Copy).then_inc(ev_act, 1))
        stage("u_s", lambda g, b, i: act.activation(u_s[:, g, :], bank[b][:, :], ACT.Gelu).then_inc(ev_act, 1))
        stage("v_s", lambda g, b, i: act.activation(v_s[:, b, 256 * (g // 4):256 * (g // 4) + 256], bank[b][:, 0:256], ACT.Gelu)
              .then_inc(ev_act, 1))
        for g in range(4):
            act.wait_ge(sem("pool_mm"), g + 1)
            act.activation(x_hi[:, g, :], bank[4 + g % 2][:, :], ACT.Copy, scale=c1("pool_scale", g)).then_inc(sem("omix_hi"), 1)
        act.wait_ge(sem("sg_var"), 1)
        act.activation(bn[:, :, 8:9], bn[:, :, 7:8], ACT.Sqrt).then_inc(sem("sg_root"), 1)
        for g in range(4):
            act.wait_ge(sem("omix_f"), g + 1)
            act.activation(x_hi[:, 4 + g, :], tt[:, g % 2, :], ACT.Copy).then_inc(sem("omix_hi"), 1)
        stage("odd_out", None)
        ffn(1)
        norm(lambda k: res[:, k, :], dst=None, after="down1")

    @block.vector
    def _(dve):
        own = Tally(dve, sem("dve_own"))
        norms = [0, 0]

        def ada_sums(name, i, s):
            n, early = 2 * i + (ADA_AT[name] + s), ADA_AT[name] < 8
            dve.wait_ge(sem("ada_kept"), n + 1)
            for r in range(2 if early else 0):
                dve.wait_ge(sem(f"ada_in{r}"), 16 * n + 16)
                dve.wait_ge(sem("ada_ctx"), 2 * n + r + 1)
                dve.tensor_tensor_reduce(spare, ada_w[:, r, :], c_ctx, 1.0, 0.0, ALU.mult, ALU.add,
                                         ada_col[:, 3 + r:4 + r]).then_inc(sem("ada_ctx"), 1)
            for r in range(3):
                if early:
                    dve.wait_ge(sem("ada_ctx"), 2 * n + 3)
                dve.wait_ge(sem(f"ada_in{r}"), 16 * n + 16)
                dve.tensor_tensor_reduce(ada_w[:, r, :], ada_w[:, r, :], c_x, 1.0, 0.0, ALU.mult, ALU.add,
                                         ada_col[:, r:r + 1]).then_inc(sem(f"ada_sum{r}"), 1)
            for r in range(3):
                dve.wait_ge(sem(f"ada_sum{r}"), n + 2)
            if early:
                dve.tensor_copy(mod[:, ds(2 * n, 2)], ada_col[:, 0:2])
                dve.tensor_copy(mod_c[:, ds(2 * n, 2)], ada_col[:, 3:5])
                last = dve.tensor_copy(mod[:, ds(n + 16, 1)], ada_col[:, 2:3])
            else:
                last = dve.tensor_copy(mod[:, ds(3 * n, 3)], ada_col[:, 0:3])
            last.then_inc(sem("ada_kept"), 1)

        def stage(name, free):
            g0, per = GROUP0[name], PER[name]
            blocks_ = COUNT[name]

            def pair(i):
                for s in range(2):
                    if name in ADA_AT:
                        ada_sums(name, i, s)
                    if free:
                        for m in range(per):
                            dve.wait_ge(mm_done, 2 + g0 + per * (2 * i + s) + m)
                            free(per * (2 * i + s) + m, (per * s + m) % 4, i)

            if blocks_ > 2:
                n0 = own.n
                with dve.Fori(0, blocks_ // 2) as i:
                    pair(i)
                assert own.n == n0, "no own waits in this loop"
            else:
                pair(0)

        def norm(src, scale, n=S, shift=None, dst=(x_hi, x_lo), into=None):
            v, w = norms
            dve.wait_ge(sem("root_ready"), v + 1)
            norms[0] += 1
            for k in range(KT + 1):
                if k < KT:
                    if into is not None:
                        last = dve.scalar_tensor_tensor(into(k), src(k), scale(k), root[:, :n], ALU.mult, ALU.mult)
                        continue
                    if w or k >= 2:
                        dve.wait_ge(sem("xl_ready"), 8 * w + k - 1)
                    dve.scalar_tensor_tensor(tt[:, k % 2, :n], src(k), scale(k), root[:, :n], ALU.mult, ALU.mult)\
                       .then_inc(sem("t_ready"), 1)
                if k and into is None:
                    dve.wait_ge(sem("xh_ready"), 8 * w + k)
                    if shift is None:
                        dve.tensor_tensor(dst[1][:, k - 1, :n], tt[:, (k - 1) % 2, :n], dst[0][:, k - 1, :n].bitcast(F32), ALU.subtract)\
                           .then_inc(sem("xl_ready"), 1)
                    else:
                        dve.scalar_tensor_tensor(dst[1][:, k - 1, :n], tt[:, (k - 1) % 2, :n], shift(k - 1),
                                                 dst[0][:, k - 1, :n].bitcast(F32), ALU.add, ALU.subtract)\
                           .then_inc(sem("xl_ready"), 1)
            if into is not None:
                own(last)
            else:
                norms[1] += 1

        dve.sem_inc(ev_dve, LEAD)
        dve.sem_inc(sem("conv_done"), 4)
        dve.memset(ones[:, :], 1.0).then_inc(sem("ones_ready"), 1)
        dve.wait_ge(sem("consts"), 48)
        norm(lambda k: pb[:, k, :], lambda k: c1("g_in", k))
        dve.wait_ge(sem("fold_in"), 32)
        for j in range(3):
            part = fold[:, j, :, :].rearrange("p (k g) c -> p k g c", g=8)
            last = dve.tensor_tensor(part, part, fold_b[:, j, :, :].unsqueeze(2).to_broadcast([P, 16, 8, 4]), ALU.mult)
        own(last)
        own(dve.tensor_reduce(fold_s[:, :, :], fold[:, :, :, :], AX.X, ALU.add))
        k_g = lambda j: fold_s[:, j, :].rearrange("p (k g) -> p k g", g=8)
        own(dve.tensor_tensor(w_g, k_g(0), k_g(1), ALU.add))
        dve.tensor_copy(v_w[:, :, P:136], k_g(2)).then_inc(sem("fold_ready"), 1)
        own(dve.memset(g_tok, 0.0))
        dve.memset(conv_in[:, :, 0:3], 0.0).then_inc(sem("pad_ready"), 1)

        def cw(g, tap):
            return col[:, ds(g * 4 + (COL["conv_w"] + tap), 1)]

        def values_out(i, b):
            g = 4 * i + b
            dve.wait_ge(sem("vg_mm"), 4 + g + 1)
            for half in range(2):
                src = bank[4 + 2 * (b % 2) + half]
                part = src[:, 0:272].rearrange("p (t n) -> p t n", n=136)
                dst = v_m[:, 2 * half:2 * half + 2, ds(g * P, P)]
                dve.tensor_copy(dst, part[:, :, 0:P])
                acc = g_tok[:, 2 * half:2 * half + 2, :]
                step = dve.tensor_tensor(acc, acc, part[:, :, P:136], ALU.add)
                if half == 0:
                    own(step)
            own(step)
            dve.sem_inc(sem("vg_done"), 1)

        n0 = own.n
        with dve.Fori(0, 4) as i:
            own.n = n0 + 20 * i
            for b in range(5):
                if b:
                    values_out(i, b - 1)
                if b == 4:
                    break
                g = 4 * i + b
                dve.wait_ge(ev_act, LEAD + g + 1)
                dve.wait_ge(sem("xc_ready"), g + 1)
                y = conv_out[:, b, :]
                own(dve.tensor_scalar(y, conv_in[:, b, 0:S], cw(g, 0), col[:, ds(g + COL["conv_b"], 1)], ALU.mult, ALU.add))
                for tap in range(1, 4):
                    step = dve.scalar_tensor_tensor(y, conv_in[:, b, tap:tap + S], cw(g, tap), y, ALU.mult, ALU.add)
                    if tap < 3:
                        own(step)
                step.then_inc(sem("conv_done"), 1)
        own.n = n0 + 20 * 4

        dve.wait_ge(sem("grow_mm"), 1)
        dve.tensor_copy(sq[0:8, 0, :], bank[6][0:8, :]).then_inc(sem("grow_out"), 1)
        dve.wait_ge(sem("gates_mm"), 1)
        own(dve.tensor_tensor(gs, bank[7][:, 0:32].rearrange("p (t g) -> p t g", g=8), g_tok, ALU.add))
        for t in range(4):
            last = dve.tensor_tensor(gs[:, t, :], gs[:, t, :], col[:, COL["b_if"]:COL["b_if"] + 8], ALU.add)
        own(last)
        dve.sem_inc(sem("g_ready"), 1)
        dve.wait_ge(sem("ln_ready"), 1)
        own(dve.tensor_scalar(lf, gs[:, :, 4:8], 0.0, None, ALU.min))
        dve.tensor_tensor(lf, lf, ga, ALU.subtract).then_inc(sem("lf_ready"), 1)
        dve.wait_ge(sem("b_mm"), 1)
        own(dve.tensor_copy(b_c, bank[6][:, 64:80].rearrange("p (t g) -> p t g", g=4)))
        dve.tensor_tensor(u_c, gs[:, :, 0:4], b_c, ALU.subtract).then_inc(sem("u_ready"), 1)
        dve.wait_ge(sem("rows_mm"), 1)
        own(dve.tensor_copy(sq[0:4, 0, :], bank[6][0:4, :]))
        own(dve.tensor_tensor_scan(sq[0:4, 1, :], sq[0:4, 0, :], sq[0:4, 0, :], 0.0, ALU.max, ALU.max))
        own(dve.tensor_scalar(rows[0:4, :], sq[0:4, 1, :], -1.0, None, ALU.mult))
        own(dve.tensor_tensor(root[0:4, :], bank[7][0:4, :], sq[0:4, 1, :], ALU.add))
        dve.tensor_copy(root[32:36, :], root[0:4, :]).then_inc(sem("bm_ready"), 1)

        for h in range(4):
            dve.wait_ge(sem("bc_mm"), h + 1)
            if h:
                dve.wait_ge(sem("y_done"), 4 * h)
            dve.tensor_copy(tt[:, 0, :], bank[6][:, :])
            for j in range(4):
                last = dve.tensor_tensor(tt[:, 1, P * j:P * j + P], bank[6][:, P * j:P * j + P], neg, ALU.add)
            own(last)
            own(dve.tensor_copy(var[:, :], bank[7][:, :]))
            dve.sem_inc(sem("nm_ready"), 1)
            for j in range(4):
                dve.wait_ge(sem("s_mm"), 4 * h + j + 1)
                dve.wait_ge(sem("e_done"), 4 * h + j + 1)
                n = S - P * j
                dve.tensor_tensor(p_t[:, j, :n], bank[4 + j % 2][:, :n], p_t[:, j, :n], ALU.mult).then_inc(sem("pt_done"), 1)
            dve.wait_ge(sem("abs_done"), h + 1)
            own(dve.tensor_tensor(var[:, :], var[:, :], root[:, :], ALU.max))
            own(dve.reciprocal(var[:, :], var[:, :]))
            dve.wait_ge(ev_act, LEAD + EV[f"o_m{h}"][1]["act"] + 4)
            for e in range(4):
                own(dve.tensor_tensor(q_t[:, e, :], q_t[:, e, :], var[:, :], ALU.mult))
                dve.wait_ge(sem("h_mm"), 4 * h + e + 1)
                dve.tensor_tensor(q_t[:, e, :], bank[HB[e]][:, :], q_t[:, e, :], ALU.mult).then_inc(sem("h_done"), 1)
            dve.wait_ge(sem("sum_mm"), h + 1)
            own(dve.tensor_scalar(tt[:, 0, :], bank[4][:, :], 1.0 / 512, None, ALU.mult))
            own(dve.tensor_tensor(tt[:, 1, :], tt[:, 0, :], tt[:, 0, :], ALU.mult))
            dve.wait_ge(sem("hs_mm"), 4 * h + 4)
            dve.scalar_tensor_tensor(root[:, :], bank[5][:, :], 1.0 / 512, tt[:, 1, :], ALU.mult, ALU.subtract)\
               .then_inc(sem("hvar_ready"), 1)
            dve.wait_ge(sem("hroot_ready"), h + 1)
            for e in range(4):
                own(dve.tensor_tensor(q_t[:, e, :], q_t[:, e, :], tt[:, 0, :], ALU.subtract))
                own(dve.scalar_tensor_tensor(q_t[:, e, :], q_t[:, e, :], c1("g_head", 4 * h + e), root[:, :], ALU.mult, ALU.mult))
                own(dve.scalar_tensor_tensor(q_t[:, e, :], x_c[:, 4 * h + e, :], c1("skip", 4 * h + e), q_t[:, e, :], ALU.mult, ALU.add))
            for e in range(4):
                dve.wait_ge(ev_act, LEAD + EV[f"z_m{h}"][1]["act"] + e + 1)
                dve.tensor_tensor(q_t[:, e, :], q_t[:, e, :], sq[:, e % 2, :], ALU.mult).then_inc(sem("prod_done"), 1)
                dve.wait_ge(sem("yh_done"), 4 * h + e + 1)
                dve.tensor_tensor(y_lo[:, e, :], q_t[:, e, :], y_hi[:, e, :].bitcast(F32), ALU.subtract).then_inc(sem("y_done"), 1)

            def pb_free(g, b, i):
                if h == 0:
                    dve.tensor_copy(pb[:, g, :], bank[b][:, :]).then_inc(ev_dve, 1)
                else:
                    dve.tensor_tensor(pb[:, g, :], bank[b][:, :], pb[:, g, :], ALU.add).then_inc(ev_dve, 1)
            stage(f"w_pb{h}", pb_free)

        own(dve.memset(rel_sb[32:33, :], 1.0))
        dve.sem_inc(sem("rel_one"), 1)
        dve.wait_ge(mm_done, 1 + GROUP0["w_pb3"] + 8)
        for r in range(3):
            dve.sem_inc(sem(f"ada_sum{r}"), 1)
        dve.sem_inc(sem("ada_ctx"), 1)
        dve.sem_inc(sem("ada_kept"), 1)
        dve.wait_ge(sem("silu_c"), 1)
        stage("q_a", None)
        stage("k_a", None)

        def v_a_free(g, b, i):
            dve.tensor_copy(v_a[:, b, ds((g - b) * 64, 256)], bank[b][:, 0:256]).then_inc(ev_dve, 1)
        stage("v_a", v_a_free)

        def finish(h):
            own(dve.reciprocal(stat(h, 3), stat(h, 2)))
            dve.wait_ge(sem("pv_mm"), h + 1)
            dve.tensor_tensor(y_a[:, :, 64 * h:64 * h + 64], bank[7][:, 0:256].rearrange("p (t n) -> p t n", n=64),
                              stat(h, 3).unsqueeze(2).to_broadcast([P, 4, 64]), ALU.mult).then_inc(sem("ya_done"), 1)

        def weights(h):
            dve.wait_ge(sem("t_mm"), 3 * h + 3)
            if h:
                dve.wait_ge(sem("pv_mm"), h)
            dve.tensor_copy(p_c[:, S:S + 384], bank[5][:, 0:384])
            dve.tensor_copy(p_c[:, S + 384:TRI], bank[6][:, 0:384]).then_inc(sem("pc_dve"), 1)

        for h in range(16):
            dve.wait_ge(sem("qk_a_mm"), h + 1)
            dve.wait_ge(sem(f"strip_in{h % 2}"), 16 * (h // 2) + 16)
            if h:
                dve.wait_ge(sem("p_done"), h)
            for i in range(4):
                o, n = TRI_AT[i], P * (i + 1)
                src = bank[SB[i]][:, SO[i]:SO[i] + n]
                last = dve.tensor_tensor_reduce(s_r[:, o:o + n], src, strip[:, h % 2, S - n:S], 1.0, -3e38,
                                                ALU.add, ALU.max, stat(h, 0)[:, i:i + 1])
            own(last)
            dve.tensor_scalar(stat(h, 1), stat(h, 0), -1.0, None, ALU.mult).then_inc(sem("max_ready"), 1)
            if h > 1:
                finish(h - 2)
            if h:
                weights(h - 1)
        finish(14)
        weights(15)
        finish(15)
        stage("z_a", None)
        for c in range(9):
            if c < 8:
                dve.wait_ge(ev_act, LEAD + EV["gate_a"][1]["act"])
                dve.wait_ge(sem("yt_mm"), c + 1)
                if c >= 2:
                    dve.wait_ge(sem("yz_l"), c - 1)
                dve.tensor_tensor(tt[:, c % 2, :].rearrange("p (t n) -> p t n", n=P), backward(4 + c % 3),
                                  z_a[:, c, :].rearrange("p (t n) -> p t n", n=P), ALU.mult).then_inc(sem("yz_f"), 1)
            if c:
                dve.wait_ge(sem("yz_h"), c)
                dve.tensor_tensor(yz_lo[:, c - 1, :], tt[:, (c - 1) % 2, :], yz_hi[:, c - 1, :].bitcast(F32), ALU.subtract)\
                   .then_inc(sem("yz_l"), 1)
        stage("gate_a", None)
        stage("w_pa", lambda g, b, i: dve.tensor_tensor(merged[:, ds(g, 1), :], bank[b][:, :], gate[:, ds(g, 1), :], ALU.mult)
              .then_inc(ev_dve, 1))
        dve.wait_ge(ev_dve, LEAD + EV["gate_m"][1]["dve"])
        n0 = own.n
        with dve.Fori(0, 2) as i:
            own.n = n0 + 4 * i
            for b in range(4):
                if b % 2 == 0:
                    ada_sums("gate_m", i, b // 2)
                g = 4 * i + b
                dve.wait_ge(ev_act, LEAD + EV["gate_m"][1]["act"] + g + 1)
                own(dve.tensor_tensor(tt[:, b % 2, :], gate[:, ds(g, 1), :], pb[:, ds(g, 1), :], ALU.mult))
                dve.tensor_tensor(merged[:, ds(g, 1), :], merged[:, ds(g, 1), :], tt[:, b % 2, :], ALU.add).then_inc(sem("mrg"), 1)
            for b in range(4):
                g = 4 * i + b
                dve.wait_ge(sem("mrg_hi"), g + 1)
                dve.tensor_tensor(yz_lo[:, ds(g, 1), :], merged[:, ds(g, 1), :], yz_hi[:, ds(g, 1), :].bitcast(F32), ALU.subtract)\
                   .then_inc(sem("mrg_lo"), 1)
        own.n = n0 + 8
        dve.wait_ge(sem("res_in"), 16)
        stage("w_out", lambda g, b, i: dve.tensor_tensor(res[:, ds(g, 1), :], bank[b][:, :], res[:, ds(g, 1), :], ALU.add)
              .then_inc(ev_dve, 1))
        dve.wait_ge(ev_dve, LEAD + EV["a_e"][1]["dve"])
        norm(lambda k: res[:, k, :], lambda k: c1("g_out", k), into=lambda k: res[:, k, :])
        dve.sem_inc(sem("x1_ready"), 1)
        dve.wait_ge(sem("ada_kept"), 1 + ADA)
        b0 = COL["ada_b"]
        own(dve.tensor_tensor(mod[:, :], mod[:, :], col[:, b0:b0 + 96], ALU.add))
        own(dve.tensor_tensor(mod_c[:, :], mod_c[:, :], col[:, b0:b0 + 16], ALU.add))
        for j, (m0, w0, who) in enumerate(((8, 0, 0), (32, 8, 0), (56, 16, 0), (80, 24, 0), (8, 0, 1))):
            w0 += COL["norm_w"]
            last = dve.scalar_tensor_tensor(coef[:, j, :], (mod_c if who else mod)[:, m0:m0 + 8], 1.0, col[:, w0:w0 + 8], ALU.add, ALU.mult)
        own(last)
        dve.sem_inc(sem("mod_ready"), 1)

        def shift(m0, who=0):
            return lambda k: (mod_c if who else mod)[:, m0 + k:m0 + k + 1]
        own(dve.memset(conv_u[:, :, 0:15], 0.0))
        own(dve.memset(conv_u[:, :, 15 + S:CW], 0.0))
        dve.sem_inc(sem("pad2_ready"), 1)
        norm(lambda k: c_in[:, k, :], lambda k: coef[:, 4, k:k + 1], n=CTX, shift=shift(0, 1), dst=(c_hi, c_lo))
        norm(lambda k: res[:, k, :], lambda k: coef[:, 0, k:k + 1], shift=shift(0))
        for b in range(4):
            dve.wait_ge(ev_act, LEAD + EV["b_e"][1]["act"] + b + 1)
            last = dve.tensor_tensor(conv_u[:, b, 15:15 + S], conv_u[:, b, 15:15 + S], sq[:, b % 2, :], ALU.mult)
            last.then_inc(sem("u_made"), 1)

        def convolve(c0):
            w = COL["conv2_w"]
            dve.wait_ge(sem("u_made"), c0 + 2)
            for c in (c0, c0 + 1):
                last = dve.tensor_scalar(conv_c[:, c, :], conv_u[:, c, 0:S], col[:, w + 31 * c:w + 31 * c + 1], None, ALU.mult)
                last.then_inc(sem("tap"), 1)
            n = 60 * (c0 // 2) + 2 * (c0 // 2)
            with dve.Fori(0, 10) as i:
                for tap in range(3):
                    for k, c in enumerate((c0, c0 + 1)):
                        dve.wait_ge(sem("tap"), 6 * i + (n + 2 * tap + k + 1))
                        dve.scalar_tensor_tensor(conv_c[:, c, :], conv_u[:, c, ds(3 * i + (tap + 1), S)],
                                                 col[:, ds(3 * i + (w + 31 * c + tap + 1), 1)], conv_c[:, c, :], ALU.mult, ALU.add)\
                           .then_inc(sem("tap"), 1)
            dve.wait_ge(sem("tap"), n + 62)
            dve.sem_inc(sem("conv_made"), 2)

        def rope(x, other, table):
            own(dve.tensor_tensor(x, x, table[:, 0, :], ALU.mult))
            own(dve.tensor_tensor(other, other, table[:, 1, :], ALU.mult))
            dve.tensor_tensor(x, x, other, ALU.add).then_inc(sem("roped"), 1)
        convolve(0)
        dve.wait_ge(sem("rope_in"), 32)
        for h in range(4):
            dve.wait_ge(ev_act, LEAD + EV["q_r"][1]["act"] + h + 1)
            rope(q_r[:, h, :], g_r[:, h, :], rope_t)
        for h in range(4):
            dve.wait_ge(ev_act, LEAD + EV["k_r"][1]["act"] + 2 * h + 2)
            rope(k_r[:, h, :], v_r[:, h, :], rope_t)
            swap = v_x[:, :, :].rearrange("p a (b n) -> p (a b) n", n=CTX)[:, h, :]
            rope(k_x[:, h, :], swap, rope_u)
        convolve(2)
        dve.wait_ge(sem("lg_ln"), 1)
        own(dve.tensor_scalar(lg[:, 0:8], col[:, COL["decay"]:COL["decay"] + 8], 0.0, None, ALU.min))
        own(dve.tensor_tensor(lg[:, 0:8], lg[:, 0:8], lg[:, 8:16], ALU.subtract))
        for j in range(2):
            dve.tensor_scalar(lg[:, 24 + 4 * j:28 + 4 * j], lg[:, 0:4], float(CTX - P * j), None, ALU.mult)
            dve.tensor_scalar(lg[:, 32 + 4 * j:36 + 4 * j], lg[:, 4:8], float(S - 1 + P * j), None, ALU.mult)
        own(dve.tensor_scalar(lg[:, 40:44], lg[:, 4:8], -1.0, None, ALU.mult))
        dve.wait_ge(sem("diff_in"), 16)
        dve.tensor_scalar(ahead[:, :], diff_t[:, :], 0.0, None, ALU.max)
        own(dve.tensor_scalar(behind[:, :], diff_t[:, :], 1.0, 0.0, ALU.add, ALU.min))
        dve.wait_ge(mm_done, 1 + GROUP0["g_r"])
        for h in range(4):
            if h:
                dve.wait_ge(sem("yr_mm"), h)
            own(dve.tensor_scalar(decay[:, :], ahead[:, :], lg[:, h:h + 1], None, ALU.mult))
            own(dve.scalar_tensor_tensor(decay[:, :], behind[:, :], lg[:, 40 + h:41 + h], decay[:, :], ALU.mult, ALU.add))
            dve.sem_inc(sem("decay_arg"), 1)
            for j in range(2):
                dve.wait_ge(sem("dx_ready"), 2 * h + j + 1)
                own(dve.tensor_tensor(decay_x[:, j, :], decay_x[:, j, :], tt[:, 0, :], ALU.add))
                dve.sem_inc(sem("dx_used"), 1)
            for j in range(6):
                dve.wait_ge(sem("sr_mm"), 6 * h + j + 1)
                m = decay[:, S - P - P * j:TOEP - P * j] if j < 4 else decay_x[:, j - 4, :]
                dve.tensor_tensor(w_r[:, j, :], bank[4 + j % 2][:, :], m, ALU.mult).then_inc(sem("wr_done"), 1)
            dve.wait_ge(sem("yr_mm"), h + 1)
            dve.tensor_copy(q_r[:, h, :], bank[6][:, :]).then_inc(sem("y_out"), 1)
        for h in range(4):
            dve.wait_ge(ev_act, LEAD + EV["g_r"][1]["act"] + 4)
            dve.wait_ge(sem("ysq"), h + 1)
            own(dve.tensor_tensor(q_r[:, h, :], q_r[:, h, :], g_r[:, h, :], ALU.mult))
            dve.wait_ge(sem("yroot"), h + 1)
            dve.tensor_tensor(tt[:, 0, :], q_r[:, h, :], root[:, :], ALU.mult).then_inc(sem("mix_f"), 1)
            dve.wait_ge(sem("mix_hi"), h + 1)
            dve.tensor_tensor(x_lo[:, h, :], tt[:, 0, :], x_hi[:, h, :].bitcast(F32), ALU.subtract).then_inc(sem("mix_lo"), 1)
        dve.wait_ge(sem("mix_lo"), 4)
        dve.wait_ge(sem("csq_mm"), 4)
        own(dve.tensor_scalar(tt[:, 0, :], bank[4][:, :], 1.0 / 512, None, ALU.mult))
        own(dve.tensor_tensor(tt[:, 1, :], tt[:, 0, :], tt[:, 0, :], ALU.mult))
        own(dve.scalar_tensor_tensor(var[:, :], bank[5][:, :], 1.0 / 512, tt[:, 1, :], ALU.mult, ALU.subtract))
        dve.sem_inc(sem("cvar"), 1)
        dve.wait_ge(sem("croot"), 1)
        for c in range(4):
            own(dve.tensor_tensor(conv_c[:, c, :], conv_c[:, c, :], tt[:, 0, :], ALU.subtract))
            dve.scalar_tensor_tensor(conv_c[:, c, :], conv_c[:, c, :], c1("ln_w", c), root[:, :], ALU.mult, ALU.mult)\
               .then_inc(sem("c_norm"), 1)
        for c in range(4):
            dve.wait_ge(sem("mix_hi"), 5 + c)
            dve.tensor_tensor(x_lo[:, 4 + c, :], conv_c[:, c, :], x_hi[:, 4 + c, :].bitcast(F32), ALU.subtract).then_inc(sem("mix_lo"), 1)

        def add_gated(name, m0):
            stage(name, lambda g, b, i: dve.scalar_tensor_tensor(res[:, ds(g, 1), :], bank[b][:, :], mod[:, ds(g + m0, 1)],
                                                                 res[:, ds(g, 1), :], ALU.mult, ALU.add).then_inc(ev_dve, 1))
        add_gated("even_out", 16)

        def ffn(i):
            dve.wait_ge(ev_dve, LEAD + EV[f"up{i}"][1]["dve"])
            norm(lambda k: res[:, k, :], lambda k: coef[:, 2 * i + 1, k:k + 1], shift=shift(48 * i + 24))
            g0, before = GROUP0[f"up{i}"], EV[f"up{i}"][1]
            with dve.Fori(0, FF // 2) as j:
                for s in range(2):
                    n = 2 * j + s
                    dve.wait_ge(mm_done, 3 + g0 + 2 * n)
                    dve.wait_ge(ev_act, LEAD + before["act"] + n + 1)
                    dve.wait_ge(sem("hid_l"), FF * i + n + 1)
                    dve.tensor_tensor(tt[:, s, :], bank[2 * s + 1][:, :], sq[:, s, :], ALU.mult).then_inc(ev_dve, 1)
                    dve.wait_ge(sem("hid_h"), FF * i + n + 1)
                    dve.tensor_tensor(hid_lo[:, ds(n, 1), :], tt[:, s, :], hid_hi[:, ds(n, 1), :].bitcast(F32), ALU.subtract)\
                       .then_inc(sem("hid_l"), 1)
            g0 = GROUP0[f"down{i}"]
            m0 = 48 * i + 40
            with dve.Fori(0, 4) as j:
                for b in range(2):
                    dve.wait_ge(mm_done, 4 * j + (g0 + 2 * b + 3))
                    r = res[:, ds(2 * j + b, 1), :]
                    dve.scalar_tensor_tensor(r, bank[b][:, :], mod[:, ds(2 * j + (b + m0), 1)], r, ALU.mult, ALU.add)\
                       .then_inc(ev_dve, 1)
        dve.sem_inc(sem("hid_l"), 2)
        ffn(0)

        own(dve.memset(pc[:, :, 0:8], 0.0))
        own(dve.memset(pc[:, :, 8 + S:PW], 0.0))
        dve.sem_inc(sem("pad3_ready"), 1)
        dve.wait_ge(ev_dve, LEAD + EV["pool"][1]["dve"])
        norm(lambda k: res[:, k, :], lambda k: coef[:, 2, k:k + 1], shift=shift(48))
        dve.wait_ge(sem("odd_in"), 64)
        for g, w in enumerate((2, 4, 8, 16)):
            dve.wait_ge(ev_act, LEAD + EV["pool"][1]["act"] + g + 1)
            src, n = pc[:, g, :], PW
            for step in range(g + 1):
                dst = (pool_a, pool_b)[step % 2][:, g, :]
                n -= 1 << step
                own(dve.tensor_tensor(dst[:, 0:n], src[:, 0:n], src[:, (1 << step):(1 << step) + n], ALU.add))
                src = dst
            own(dve.tensor_tensor(src[:, 8 - w // 2:8 - w // 2 + S], src[:, 8 - w // 2:8 - w // 2 + S], inv_t[:, g, :], ALU.mult))
            dve.tensor_tensor(pc[:, g, 8:8 + S], src[:, 8 - w // 2:8 - w // 2 + S], pc[:, g, 8:8 + S], ALU.subtract).then_inc(sem("m_ready"), 1)
        for t in range(4):
            dve.wait_ge(ev_act, LEAD + EV["v_s"][1]["act"] + 5 + t)
            own(dve.bn_stats(bn[:, t, 0:6], v_s[:, t, :]))
            own(dve.bn_aggr(bn[:, t, 6:8], bn[:, t, 0:6]))
        own(dve.tensor_scalar(bn[:, :, 7:8], bn[:, :, 7:8], EPS, None, ALU.add))
        dve.sem_inc(sem("sg_var"), 1)
        for g in range(4):
            dve.wait_ge(sem("omix_hi"), g + 1)
            dve.scalar_tensor_tensor(x_lo[:, g, :], bank[4 + g % 2][:, :], c1("pool_scale", g), x_hi[:, g, :].bitcast(F32), ALU.mult, ALU.subtract)\
               .then_inc(sem("omix_lo"), 1)
        dve.wait_ge(sem("sg_root"), 1)
        own(dve.reciprocal(bn[:, :, 9:10], bn[:, :, 8:9]))
        for t in range(4):
            v = v_s[:, t, :]
            own(dve.tensor_scalar(v, v, bn[:, t, 6:7], bn[:, t, 9:10], ALU.subtract, ALU.mult))
            own(dve.tensor_tensor(v, v, sg_r[:, 0, :], ALU.mult))
            dve.tensor_tensor(v, v, sg_r[:, 1, :], ALU.add).then_inc(sem("v_norm"), 1)
        for g in range(4):
            dve.wait_ge(sem("sg_mm"), g + 1)
            if g >= 2:
                dve.wait_ge(sem("omix_lo"), 4 + g - 1)
            t3 = tt[:, g % 2, :].rearrange("p (n q) -> p n q", q=P)
            own(dve.tensor_tensor(t3, bank[6 + g % 2][:, :].rearrange("p (n q) -> p n q", q=P),
                                  sg_r[:, 2, P * g:P * g + P].unsqueeze(1).to_broadcast([P, 4, P]), ALU.add))
            dve.tensor_tensor(tt[:, g % 2, :], tt[:, g % 2, :], u_s[:, g, :], ALU.mult).then_inc(sem("omix_f"), 1)
            dve.wait_ge(sem("omix_hi"), 5 + g)
            dve.tensor_tensor(x_lo[:, 4 + g, :], tt[:, g % 2, :], x_hi[:, 4 + g, :].bitcast(F32), ALU.subtract).then_inc(sem("omix_lo"), 1)
        add_gated("odd_out", 64)
        ffn(1)
        norm(lambda k: res[:, k, :], lambda k: c1("g_final", k), into=lambda k: res[:, k, :])
        dve.sem_inc(sem("out_ready"), 1)

    @block.tensor
    def _(pe):
        norms = [0, 0]
        pe.sem_inc(mm_done, 1)
        pe.sem_inc(sem("vg_mm"), 4)

        def three(dst, wh, wl, xh, xl, first, last):
            pe.matmul(dst, wh, xh, start=first, stop=False)
            pe.matmul(dst, wh, xl, start=False, stop=False)
            return pe.matmul(dst, wl, xh, start=False, stop=last)

        def bank_free(name, i, g):
            by, before = EV[name]
            if by == "act":
                pe.wait_ge(ev_act, LEAD + before["act"] + g - 3)
            else:
                pe.wait_ge(ev_dve, LEAD + before["dve"] + g - 3)

        def begin(name):
            pe.wait_ge(ev_act, LEAD + EV[name][1]["act"])
            pe.wait_ge(ev_dve, LEAD + EV[name][1]["dve"])

        def stage(name, xh=x_hi, xl=x_lo, kts=KT, behind_by_one=None, ready=None):
            n0, per = FIRST[name], PER[name]
            blocks_ = COUNT[name]
            begin(name)

            def pair(i):
                for s in range(2):
                    pe.wait_ge(lo_done, n0 + 2 * i + s + 1)
                    wh = w_hi[:, s, :].rearrange("p (k n) -> p k n", k=kts)
                    wl = w_lo[:, s, :].rearrange("p (k n) -> p k n", k=kts)
                    for m in range(per):
                        b = (per * s + m) % 4
                        bank_free(name, i, per * (2 * i + s) + m)
                        for k in range(kts):
                            if ready and s == m == 0:
                                pe.wait_ge(ready[0], ready[1] + k + 1)
                            last = three(bank[b][:, :], wh[:, k, P * m:P * m + P], wl[:, k, P * m:P * m + P],
                                         xh[:, k, :], xl[:, k, :], k == 0, k == kts - 1)
                        last.then_inc(mm_done, 1)
                        if behind_by_one and b:
                            behind_by_one(i, b - 1)
                if behind_by_one:
                    behind_by_one(i, 3)
            if blocks_ > 2:
                with pe.Fori(0, blocks_ // 2) as i:
                    pair(i)
            else:
                pair(0)

        def norm(n=S):
            v = norms[0]
            if v:
                pe.wait_ge(sem("var_ready"), v)
            for k in range(KT):
                pe.wait_ge(sem("sq_ready"), 8 * v + k + 1)
                pe.matmul(bank[4][:, :n], ones[:, :], sq[:, k % 2, :n], start=(k == 0), stop=(k == KT - 1))\
                  .then_inc(sem("sq_used"), 1)
            norms[0] += 1

        pe.wait_ge(sem("ones_ready"), 1)
        norm()

        def x_m_values(i, b):
            g = 4 * i + b
            pe.wait_ge(sem("fold_ready"), 1)
            pe.wait_ge(sem("bd_in"), 16)
            pe.wait_ge(ev_act, LEAD + g + 1)
            pe.wait_ge(sem("vg_done"), g - 1 + 2)
            for t in range(4):
                last = pe.matmul(bank[4 + 2 * (b % 2) + t // 2][:, 136 * (t % 2):136 * (t % 2) + 136],
                                 conv_in[:, b, 3 + P * t:3 + P * t + P], v_w[:, ds(g, 1), :], start=True, stop=True)
            last.then_inc(sem("vg_mm"), 1)
        pe.sem_inc(sem("vg_done"), 2)
        stage("x_m", behind_by_one=x_m_values, ready=(sem("xl_ready"), 0))

        def query_key(h, parts):
            for j in parts:
                if j == 0:
                    pe.wait_ge(sem("bd_ready"), 16 * h + 16)
                    if h:
                        pe.wait_ge(sem("hvar_ready"), h)
                if j >= 2:
                    pe.wait_ge(sem("qk_ev"), 8 * h + j - 1)
                last = pe.matmul(bank[4 + j % 2][:, :], bd[:, j % 4, j // 4, :], x_c[:, 4 * h + j % 4, :], start=True, stop=True)
                last.then_inc(sem("qk_mm"), 1)

        pe.wait_ge(sem("xc_ready"), 4 + 16)
        pe.wait_ge(sem("vg_done"), 2 + 16)
        for g in range(16):
            last = pe.matmul(bank[6][0:8, :], w_g[:, g, :], x_c[:, g, :], start=(g == 0), stop=(g == 15))
        last.then_inc(sem("grow_mm"), 1)
        query_key(0, range(4))
        pe.wait_ge(sem("grow_out"), 1)
        for t in range(4):
            last = pe.transpose(bank[7][:, 8 * t:8 * t + 8], sq[0:8, 0, P * t:P * t + P], ident[0:8, 0:8])
        last.then_inc(sem("gates_mm"), 1)
        query_key(0, range(4, 8))
        pe.wait_ge(sem("lf_ready"), 1)
        for t in range(4):
            for s in range(t + 1):
                last = pe.matmul(bank[6][:, 64 + 4 * t:68 + 4 * t], (tri if s == t else ones[:, :]), lf[:, s, :],
                                 start=(s == 0), stop=(s == t))
        last.then_inc(sem("b_mm"), 1)
        pe.wait_ge(sem("u_ready"), 1)
        for t in range(4):
            pe.transpose(bank[6][0:4, P * t:P * t + P], u_c[:, t, :], ident)
            last = pe.transpose(bank[7][0:4, P * t:P * t + P], b_c[:, t, :], ident)
        last.then_inc(sem("rows_mm"), 1)

        for h in range(4):
            if h:
                query_key(h, range(8))
            if h == 0:
                pe.wait_ge(sem("rows_ready"), 1)
            pe.matmul(bank[6][:, :], ident[0:4, h:h + 1].to_broadcast([4, P]), rows[0:4, :], start=True, stop=True)
            pe.matmul(bank[7][:, :], ident[32:36, 32 + h:33 + h].to_broadcast([4, P]), rows[32:36, :], start=True, stop=True)\
              .then_inc(sem("bc_mm"), 1)
            pe.wait_ge(sem("qk_ev"), 8 * h + 8)
            for j in range(4):
                if j >= 2:
                    pe.wait_ge(sem("pt_done"), 4 * h + j - 1)
                for c in range(4):
                    last = pe.matmul(bank[4 + j % 2][:, :S - P * j], k_t[:, c, P * j:P * j + P], q_t[:, c, P * j:S],
                                     start=(c == 0), stop=(c == 3))
                last.then_inc(sem("s_mm"), 1)
            stage(f"o_m{h}")
            pe.wait_ge(sem("nm_ready"), h + 1)
            pe.wait_ge(sem("pt_done"), 4 * h + 4)
            for j in range(4):
                last = pe.matmul(bank[6][:, P * j:S], ones[:, :], p_t[:, j, :S - P * j], start=(j == 0), stop=(j == 3))
            last.then_inc(sem("den_mm"), 1)
            for e in range(4):
                if e == 3:
                    pe.wait_ge(sem("abs_done"), h + 1)
                for j in range(4):
                    last = pe.matmul(bank[HB[e]][:, P * j:S], v_m[:, j, P * (4 * h + e):P * (4 * h + e) + P],
                                     p_t[:, j, :S - P * j], start=(j == 0), stop=(j == 3))
                last.then_inc(sem("h_mm"), 1)
            pe.wait_ge(sem("h_done"), 4 * h + 4)
            for e in range(4):
                last = pe.matmul(bank[4][:, :], ones[:, :], q_t[:, e, :], start=(e == 0), stop=(e == 3))
            last.then_inc(sem("sum_mm"), 1)
            for e in range(4):
                pe.wait_ge(sem("hsq_ready"), 4 * h + e + 1)
                pe.matmul(bank[5][:, :], ones[:, :], sq[:, e % 2, :], start=(e == 0), stop=(e == 3)).then_inc(sem("hs_mm"), 1)
            stage(f"z_m{h}")
            stage(f"w_pb{h}", y_hi, y_lo, kts=4, ready=(sem("y_done"), 4 * h))

        pe.wait_ge(sem("rel_in"), 32)
        pe.wait_ge(sem("rel_one"), 1)
        pe.matmul(bank[4][0:16, :], rel_sb[:, :], hot_sb[:, 0:S], start=True, stop=True)
        pe.matmul(bank[5][0:16, 0:P], rel_sb[:, :], hot_sb[:, S:], start=True, stop=True).then_inc(sem("bias_mm"), 1)
        stage("q_a")
        stage("k_a")

        def stage_tokens(name):
            n0 = FIRST[name]
            begin(name)

            def pair(i):
                for s in range(2):
                    pe.wait_ge(lo_done, n0 + 2 * i + s + 1)
                    wh = w_hi[:, s, :].rearrange("p (k n) -> p k n", k=KT)
                    wl = w_lo[:, s, :].rearrange("p (k n) -> p k n", k=KT)
                    for t in range(4):
                        bank_free(name, i, 4 * (2 * i + s) + t)
                        for k in range(KT):
                            c = slice(P * t, P * t + P)
                            d = bank[t][:, 0:256]
                            pe.matmul(d, x_hi[:, k, c], wh[:, k, :], start=(k == 0), stop=False)
                            pe.matmul(d, x_hi[:, k, c], wl[:, k, :], start=False, stop=False)
                            last = pe.matmul(d, x_lo[:, k, c], wh[:, k, :], start=False, stop=(k == KT - 1))
                        last.then_inc(mm_done, 1)
            if COUNT[name] > 2:
                with pe.Fori(0, COUNT[name] // 2) as i:
                    pair(i)
            else:
                pair(0)
        stage_tokens("v_a")
        begin("z_a")

        def head(h):
            return slice(64 * (h % 2), 64 * (h % 2) + 64), h // 2
        def values(h):
            pe.wait_ge(sem("pc_act"), h + 1)
            pe.wait_ge(sem("pc_dve"), h + 1)
            if h:
                pe.wait_ge(sem("ya_done"), h)
            for i in range(4):
                for j in range(i + 1):
                    o = PC_AT[j] + P * (i - j)
                    last = pe.matmul(bank[7][:, 64 * i:64 * i + 64], p_c[:, o:o + P], v_a[:, j, 64 * h:64 * h + 64],
                                     start=(j == 0), stop=(j == i))
            last.then_inc(sem("pv_mm"), 1)

        pe.wait_ge(sem("bias_ready"), 1)
        for h in range(-1, 16):
            if h + 1 < 16:
                r, c = head(h + 1)
                if h >= 0:
                    pe.wait_ge(sem("max_ready"), h + 1)
                for i in range(4):
                    n = P * (i + 1)
                    last = pe.matmul(bank[SB[i]][:, SO[i]:SO[i] + n], q_a[r, c, P * i:P * i + P], k_a[r, c, 0:n], start=True, stop=True)
                last.then_inc(sem("qk_a_mm"), 1)
            if h >= 1:
                values(h - 1)
            if h >= 0:
                pe.wait_ge(sem("p_done"), h + 1)
                for j, (b, o) in enumerate(((4, 0), (5, 0), (6, 0), (6, 256))):
                    for i in range(j, 4):
                        last = pe.transpose(bank[b][:, o + P * (i - j):o + P * (i - j) + P],
                                            p_r[:, TRI_AT[i] + P * j:TRI_AT[i] + P * j + P], ident)
                    if j != 2:
                        last.then_inc(sem("t_mm"), 1)
        values(15)
        pe.wait_ge(sem("ya_done"), 16)
        stage("z_a")
        for c in range(8):
            if c >= 3:
                pe.wait_ge(sem("yz_f"), c - 2)
            for t in range(4):
                last = pe.transpose(bank[4 + c % 3][:, P * t:P * t + P], y_a[:, t, P * c:P * c + P], ident)
            last.then_inc(sem("yt_mm"), 1)
        stage("gate_a")
        pe.wait_ge(sem("yz_l"), 8)
        stage("w_pa", yz_hi, yz_lo)
        stage("gate_m")
        stage("w_out", yz_hi, yz_lo, ready=(sem("mrg_lo"), 0))
        begin("a_e")
        norm()

        norm(CTX)
        norm()
        stage("a_e", ready=(sem("xl_ready"), 16))
        stage("b_e")
        stage("q_r")

        begin("k_r")
        for s in range(2):
            pe.wait_ge(lo_done, FIRST["k_r"] + s + 1)
            wh = w_hi[:, s, :].rearrange("p (k n) -> p k n", k=KT)
            wl = w_lo[:, s, :].rearrange("p (k n) -> p k n", k=KT)
            for m in range(2):
                for j, (xh, xl, n) in enumerate(((x_hi, x_lo, S), (c_hi, c_lo, CTX))):
                    bank_free("k_r", 0, 4 * s + 2 * m + j)
                    for k in range(KT):
                        last = three(bank[2 * m + j][:, :n], wh[:, k, P * m:P * m + P], wl[:, k, P * m:P * m + P],
                                     xh[:, k, :], xl[:, k, :], k == 0, k == KT - 1)
                    last.then_inc(mm_done, 1)
        begin("v_r")
        for s in range(2):
            pe.wait_ge(lo_done, FIRST["v_r"] + s + 1)
            wh = w_hi[:, s, :].rearrange("p (k n) -> p k n", k=KT)
            wl = w_lo[:, s, :].rearrange("p (k n) -> p k n", k=KT)
            for t in range(6):
                bank_free("v_r", 0, 6 * s + t)
                d = bank[(6 * s + t) % 4][:, 0:256]
                ah, al = (x_hi, x_lo) if t < 4 else (c_hi, c_lo)
                c = slice(P * (t % 4), P * (t % 4) + P)
                for k in range(KT):
                    last = three(d, ah[:, k, c], al[:, k, c], wh[:, k, :], wl[:, k, :], k == 0, k == KT - 1)
                last.then_inc(mm_done, 1)
        stage("g_r")
        pe.wait_ge(sem("roped"), 12)
        begin("even_out")
        for h in range(4):
            for j in range(6):
                if j >= 2:
                    pe.wait_ge(sem("wr_done"), 6 * h + j - 1)
                key = k_r[:, h, P * j:P * j + P] if j < 4 else k_x[:, h, P * (j - 4):P * (j - 4) + P]
                pe.matmul(bank[4 + j % 2][:, :], key, q_r[:, h, :], start=True, stop=True).then_inc(sem("sr_mm"), 1)
            pe.wait_ge(sem("wr_done"), 6 * h + 6)
            if h:
                pe.wait_ge(sem("y_out"), h)
            for j in range(6):
                v = v_r[:, j, P * h:P * h + P] if j < 4 else v_x[:, j - 4, P * h:P * h + P]
                last = pe.matmul(bank[6][:, :], v, w_r[:, j, :], start=(j == 0), stop=(j == 5))
            last.then_inc(sem("yr_mm"), 1)
        for h in range(4):
            pe.wait_ge(sem("ysq"), h + 1)
            if h:
                pe.wait_ge(sem("yvar"), h)
            pe.matmul(bank[7][:, :], ones[:, :], sq[:, h % 2, :], start=True, stop=True).then_inc(sem("ysq_mm"), 1)
        pe.wait_ge(sem("conv_made"), 4)
        for c in range(4):
            pe.matmul(bank[4][:, :], ones[:, :], conv_c[:, c, :], start=(c == 0), stop=(c == 3))
        for c in range(4):
            pe.wait_ge(sem("csq"), c + 1)
            pe.matmul(bank[5][:, :], ones[:, :], sq[:, c % 2, :], start=(c == 0), stop=(c == 3)).then_inc(sem("csq_mm"), 1)
        stage("even_out", ready=(sem("mix_lo"), 0))

        def ffn(i):
            norm()
            name = f"up{i}"
            begin(name)
            n0, before = FIRST[name], EV[name][1]
            with pe.Fori(0, FF // 2) as j:
                for s in range(2):
                    n = 2 * j + s
                    pe.wait_ge(lo_done, n + (n0 + 1))
                    for m in range(2):
                        pe.wait_ge((ev_act, ev_dve)[m], n + (LEAD + before[("act", "dve")[m]] - 1))
                        for k in range(KT):
                            if s == m == 0:
                                pe.wait_ge(sem("xl_ready"), 8 * (3, 5)[i] + k + 1)
                            o = 256 * k + P * m
                            last = three(bank[2 * s + m][:, :], w_hi[:, s, o:o + P], w_lo[:, s, o:o + P],
                                         x_hi[:, k, :], x_lo[:, k, :], k == 0, k == KT - 1)
                        last.then_inc(mm_done, 1)
            name = f"down{i}"
            begin(name)
            pe.wait_ge(sem("hid_l"), 2 + FF * (i + 1))
            n0, before = FIRST[name], EV[name][1]["dve"]
            with pe.Fori(0, 4) as j:
                for b in range(2):
                    pe.wait_ge(ev_dve, 2 * j + (LEAD + before + b - 1))
                    for s in range(2):
                        pe.wait_ge(lo_done, 4 * j + (n0 + 2 * b + s + 1))
                        for k in range(FF // 2):
                            last = three(bank[b][:, :], w_hi[:, s, P * k:P * k + P], w_lo[:, s, P * k:P * k + P],
                                         hid_hi[:, FF // 2 * s + k, :], hid_lo[:, FF // 2 * s + k, :],
                                         s == 0 and k == 0, s == 1 and k == FF // 2 - 1)
                        last.then_inc(mm_done, 1)
        ffn(0)

        norm()
        stage("pool", ready=(sem("xl_ready"), 32))
        stage("u_s")
        stage_tokens("v_s")
        pe.wait_ge(sem("odd_in"), 64)
        for g in range(4):
            pe.wait_ge(sem("m_ready"), g + 1)
            if g >= 2:
                pe.wait_ge(sem("omix_lo"), g - 1)
            pe.matmul(bank[4 + g % 2][:, :], pool_ws[:, g, :], pc[:, g, 8:8 + S], start=True, stop=True).then_inc(sem("pool_mm"), 1)
        pe.wait_ge(sem("v_norm"), 4)
        for g in range(4):
            if g >= 2:
                pe.wait_ge(sem("omix_f"), g - 1)
            for n in range(4):
                last = pe.matmul(bank[6 + g % 2][:, P * n:P * n + P], v_s[:, n, P * g:P * g + P], sg_ws[:, g, :], start=True, stop=True)
            last.then_inc(sem("sg_mm"), 1)
        stage("odd_out", ready=(sem("omix_lo"), 0))
        ffn(1)
        norm()
def rope_table(seq, row, col):
    parts = []
    for p, n in zip((seq, row, col), ROPE_PAIRS):
        freq = np.float32(10000.0) ** (-np.arange(n, dtype=np.float32) / np.float32(n))
        parts.append(freq[:, None] * p[None, :].astype(np.float32))
    ang = np.concatenate(parts, 0)
    return np.concatenate([np.cos(ang), np.cos(ang)], 0), np.concatenate([-np.sin(ang), np.sin(ang)], 0)


def shape_tables():
    f = np.float32
    p = np.arange(P)
    dist = S - 1 - np.arange(S + P)
    d0 = np.maximum(dist, 0)
    large = 16 + (np.log(np.maximum(d0, 16).astype(f) / f(16)) / f(math.log(128.0)) * f(16)).astype(np.int32)
    bucket = np.where(d0 < 16, d0, np.minimum(large, 31))
    times = 1 * (d0 <= 128) + 1 * (d0 % 4 == 0) + 1 * (d0 % 16 == 0)
    hot = np.zeros((33, S + P), f)
    hot[bucket, np.arange(S + P)] = 1.0
    hot[32] = np.where((dist >= 0) & (times > 0), np.log(np.maximum(times, 1)), -1e30)
    t = np.arange(S)
    x_cos, x_sin = rope_table(np.full(S, float(CTX), f), t // 64, t % 64)
    c_cos, c_sin = rope_table(np.arange(CTX), np.zeros(CTX), np.zeros(CTX))
    inv = np.zeros((4, S), f)
    for g, w in enumerate((2, 4, 8, 16)):
        lo, hi = np.clip(t - w // 2, 0, S - 1), np.clip(t + w - 1 - w // 2, 0, S - 1)
        inv[g] = 1.0 / (hi - lo + 1)
    square = np.stack([np.eye(P, dtype=f), (p[:, None] <= p[None, :]).astype(f),
                       np.where(p[None, :] >= p[:, None], 0.0, -1e30).astype(f)], 1)
    diff = (np.arange(TOEP)[None, :] - (S - P) - p[:, None]).astype(f)
    return dict(square=square, hot=hot, diff=diff,
                rope_x=np.stack([x_cos, x_sin], 1).astype(f), rope_c=np.stack([c_cos, c_sin], 1).astype(f),
                inv=np.ascontiguousarray(np.broadcast_to(inv[None], (P, 4, S))))


def column_pack(v):
    col = lambda a: np.asarray(a).reshape(-1, P).T
    row = lambda a: np.broadcast_to(np.asarray(a).reshape(1, -1), (P, np.asarray(a).size))
    parts = {
        "g_in": col(v["norm_in_g"]), "g_out": col(v["norm_out_g"]), "gate_b": col(v["gate_b"]),
        "conv_w": v["conv_w"][0].reshape(4, 16, P).transpose(2, 1, 0).reshape(P, 64),
        "conv_b": col(v["conv_b"]), "g_head": col(v["head_norm_g"]), "skip": col(v["skip_m"]),
        "b_if": row(v["b_if"]),
        "ada_b": col(v["ada_b_2"]), "norm_w": col(v["norm_w_2"]), "decay": row(v["ret_decay_logit_2"]),
        "conv2_w": v["conv_dw_w_2"][0].reshape(31, 4, P).transpose(2, 1, 0).reshape(P, 124),
        "ln_w": col(v["conv_ln_w_2"]), "ln_b": col(v["conv_ln_b_2"]),
        "pool_scale": col(v["pool_scale_2"]), "g_final": col(v["final_norm_w_2"]),
    }
    assert {k: a.shape[1] for k, a in parts.items()} == WIDTHS
    return np.ascontiguousarray(np.concatenate(list(parts.values()), 1))


def weight_blocks(v):
    def cols(w, lo, hi, k=8):
        n = 2048 // k
        w = w[:, lo:hi].reshape(k, P, (hi - lo) // n, n)
        return w.transpose(2, 1, 0, 3).reshape(-1, P, 2048)
    w_in, even, odd = v["w_in"][0], v["even_w_in_2"][0], v["odd_w_in_2"][0]
    out = [cols(w_in, 4096, 6144)]
    for h in range(4):
        o = 512 * h
        out += [cols(w_in, 8192 + o, 8704 + o), cols(w_in, 6144 + o, 6656 + o), cols(v["w_pb"][0][o:o + 512], 0, 1024, 4)]
    out += [cols(w_in, 0, 3072), cols(w_in, 3072, 4096), cols(w_in, 10240, 11264), cols(v["w_pa"][0], 0, 1024),
            cols(w_in, 11264, 12288), cols(v["w_out"][0], 0, 1024)]
    out += [cols(even, 2048, 3072), cols(even, 0, 2048), cols(v["even_w_out_2"][0], 0, 1024)]

    def ffn(i):
        gate, up, down = v["ffn_w_gate_2"][i], v["ffn_w_up_2"][i], v["ffn_w_down_2"][i]
        both = np.stack([gate.reshape(8, P, 22, P), up.reshape(8, P, 22, P)], 3)
        d = down.reshape(2, 11, P, 8, P).transpose(3, 0, 2, 1, 4).reshape(16, P, 1408)
        full = np.zeros((16, P, 2048), d.dtype)
        full[:, :, :1408] = d
        return [both.transpose(2, 1, 0, 3, 4).reshape(22, P, 2048), full]
    out += ffn(0)
    out += [cols(odd, 0, 1536), cols(v["odd_w_out_2"][0], 0, 1024)]
    out += ffn(1)
    return np.concatenate(out, 0)


def block_diagonal(w):
    out = np.zeros((16, 32, 4, 32, 4), w.dtype)
    b = np.arange(32)
    out[:, b, :, b, :] = w.reshape(16, 32, 4, 4).transpose(1, 0, 2, 3)
    return out.reshape(16, P, P)


def lay_out(v):
    tiles = lambda a, n: np.ascontiguousarray(a.T.reshape(8, P, n).transpose(1, 0, 2))
    q, k, w = (block_diagonal(v[n][0]) for n in ("wq_m", "wk_m", "wv_m"))
    qk = np.stack([q, k], 1).reshape(4, 4, 2, P, P).transpose(3, 0, 1, 2, 4).reshape(P, 4, 1024)
    four = np.stack([v[n][0].reshape(16, P, 4) for n in ("wq_m", "wk_m", "wv_m")])
    fold = np.repeat(v["w_if"][0].reshape(3, 16, 32, 1, 4, 8), 4, 3).reshape(3, 16, P, 4, 8)
    ada = v["ada_w_2"].transpose(0, 2, 1).reshape(96, P, D)
    order = [m for n in range(8) for m in (2 * n, 2 * n + 1, 16 + n)] + list(range(24, 96))
    ada = ada[order]
    return dict(
        xt=tiles(v["x"][0], S), ctxt=tiles(v["ctx_2"][0], CTX), cols=column_pack(v), blocks=weight_blocks(v),
        bd_qk=np.ascontiguousarray(qk), bd_v=np.ascontiguousarray(w.transpose(1, 0, 2)),
        fold_w=np.ascontiguousarray(fold.transpose(2, 0, 1, 4, 3)).reshape(P, 3, P, 4),
        fold_c=np.ascontiguousarray(four.transpose(2, 0, 1, 3)),
        c_rows=np.ascontiguousarray(np.broadcast_to(np.stack([v["c_2"].reshape(-1), v["c_ctx_2"].reshape(-1)])[None], (P, 2, D))),
        sg_rows=np.ascontiguousarray(np.broadcast_to(np.stack([v["sg_ln_w_2"].reshape(-1), v["sg_ln_b_2"].reshape(-1),
                                                               v["sg_b_2"].reshape(-1)])[None], (P, 3, 512))),
        rel=np.ascontiguousarray(v["rel_bias"]), ada=np.ascontiguousarray(ada),
        pool_w=np.ascontiguousarray(v["pool_w_2"][0].transpose(1, 0, 2)),
        sg_w=np.ascontiguousarray(v["sg_w_2"][0].transpose(2, 0, 1)), **shape_tables())


def kernel(**inputs):
    import concourse.bacc as bacc
    from concourse.bass_utils import run_bass_kernel_spmd

    nc = bacc.Bacc("TRN2", target_bir_lowering=False, num_devices=1)
    arrays = lay_out({k: np.asarray(v) for k, v in inputs.items()})
    aps = {k: nc.dram_tensor(k, a.shape, F32, kind="ExternalInput").ap() for k, a in arrays.items()}
    aps["out"] = nc.dram_tensor("out", (D, S), F32, kind="ExternalOutput").ap()
    program(nc, **aps)
    r = run_bass_kernel_spmd(nc, [arrays], core_ids=[0])
    return np.ascontiguousarray(r.results[0]["out"].T)[None]
```

```python
import math
from contextlib import ExitStack

import concourse.bass as bass
import numpy as np
from concourse import mybir

P = 128
S = 512
CTX = 256
D = 1024
KT = D // P
EPS = 1e-6
HB = (4, 5, 7, 6)
ROPE_PAIRS = (16, 24, 24)
TOEP = 2 * S - P
TRI = 10 * P
TRI_AT = (0, P, 3 * P, 6 * P)
PC_AT = (0, 4 * P, 7 * P, 9 * P)
SB, SO = (2, 2, 1, 0), (256, 0, 0, 0)
FF = 22
CW = S + 30
PW = S + 16
F32 = mybir.dt.float32
F32R = mybir.dt.float32r
ALU = mybir.AluOpType
ACT = mybir.ActivationFunctionType
AX = mybir.AxisListType
ds = bass.ds

WIDTHS = dict(g_in=8, g_out=8, gate_b=16, conv_w=64, conv_b=16, g_head=16, skip=16, b_if=8, ada_b=96,
              norm_w=32, decay=8, conv2_w=124, ln_w=4, ln_b=4, pool_scale=4, g_final=8)
COL, at = {}, 0
for name, width in WIDTHS.items():
    COL[name] = at
    at += width
NCOL = at

STAGES = [("x_m", 8, 2)]
for h in range(4):
    STAGES += [(f"o_m{h}", 2, 2), (f"z_m{h}", 2, 2), (f"w_pb{h}", 2, 4)]
STAGES += [("q_a", 4, 2), ("k_a", 4, 2), ("v_a", 4, 4), ("z_a", 4, 2), ("gate_a", 4, 2), ("w_pa", 4, 2), ("gate_m", 4, 2),
           ("w_out", 4, 2), ("a_e", 2, 2), ("b_e", 2, 2), ("q_r", 2, 2), ("k_r", 2, 4), ("v_r", 2, 6), ("g_r", 2, 2), ("even_out", 4, 2),
           ("up0", 22, 2), ("down0", 16, 1), ("pool", 2, 2), ("u_s", 2, 2), ("v_s", 2, 4), ("odd_out", 4, 2),
           ("up1", 22, 2), ("down1", 16, 1)]
FIRST, GROUP0, PER = {}, {}, {}
nb = ng = 0
for name, blocks, groups in STAGES:
    FIRST[name], GROUP0[name], PER[name] = nb, ng, groups
    nb += blocks
    ng += blocks * groups
ADA_AT = {name: 4 * j for j, name in enumerate(("q_a", "k_a", "v_a", "z_a", "gate_a", "w_pa", "gate_m", "w_out"))}
ADA = 32
COUNT = {name: blocks for name, blocks, _ in STAGES}

SUMMED = dict(first=0, out=1, even=0, ctx=0, ffn0=1, pool=1, ffn1=1, final=1)
SQ_AT, NORM = {}, {}
for v, name in enumerate(SUMMED):
    NORM[name] = v
    SQ_AT[name] = 8 * v + sum(list(SUMMED.values())[:v])


class Tally:

    def __init__(self, engine, sem):
        self.engine, self.sem, self.n = engine, sem, 0

    def __call__(self, instruction):
        instruction.then_inc(self.sem, 1)
        self.n = self.n + 1
        self.engine.wait_ge(self.sem, self.n)


def program(nc, xt, ctxt, cols, blocks, bd_qk, bd_v, fold_w, fold_c, c_rows, rel, ada, pool_w, sg_w, sg_rows, square, hot,
            diff, rope_x, rope_c, inv, out):
    ctx = ExitStack()
    with ctx:
        body(nc, ctx, xt, ctxt, cols, blocks, bd_qk, bd_v, fold_w, fold_c, c_rows, rel, ada, pool_w, sg_w, sg_rows, square, hot,
             diff, rope_x, rope_c, inv, out)


def body(nc, ctx, xt, ctxt, cols, blocks, bd_qk, bd_v, fold_w, fold_c, c_rows, rel, ada, pool_w, sg_w, sg_rows, square, hot,
         diff, rope_x, rope_c, inv, out):
    def sb(name, shape, dt=F32, stack=ctx):
        return stack.enter_context(nc.sbuf_tensor(name, shape, dt))

    sems = {}

    def sem(name):
        if name not in sems:
            sems[name] = ctx.enter_context(nc.semaphore(name))
        return sems[name]

    raw = sb("raw", [P, 2, 2048])
    w_hi = sb("w_hi", [P, 2, 2048], F32R)
    w_lo = sb("w_lo", [P, 2, 2048], F32R)
    x_hi = sb("x_hi", [P, KT, S], F32R)
    x_lo = sb("x_lo", [P, KT, S], F32R)
    col = sb("col", [P, NCOL])
    sq_c = sb("sq_c", [P, 2, P])
    mod = sb("mod", [P, 96])
    ada_col = sb("ada_col", [P, 8])
    mod_c = sb("mod_c", [P, 16])
    coef = sb("coef", [P, 5, 8])
    ones = sb("ones", [P, P])
    sq = sb("sq", [P, 2, S])
    tt = sb("tt", [P, 2, S])
    vr = sb("vr", [P, 2, S])
    var, root = vr[:, 0, :], vr[:, 1, :]
    low = sb("low", [P, KT * S])
    def c1(name, j):
        return col[:, COL[name] + j:COL[name] + j + 1]

    def stat(h, what):
        o = 16 * (h % 4) + 4 * what
        return sq[:, 0, o:o + 4]

    def backward(b):
        a = bank[b][:, :]
        return bass.AP(a.tensor, a.offset + P - 1, [list(a.ap[0]), [P, 4], [-1, P]])

    ident, tri = sq_c[:, 0, :], sq_c[:, 1, :]

    m1, m2, m3 = ExitStack(), ExitStack(), ExitStack()
    pb = sb("pb", [P, KT, S], stack=m1)
    fold = sb("fold", [P, 3, P, 4], stack=m2)
    fold_b = sb("fold_b", [P, 3, 16, 4], stack=m2)
    fold_s = sb("fold_s", [P, 3, P], stack=m2)
    m2.close()
    m2 = ExitStack()
    v_m = sb("v_m", [P, 4, 2048], stack=m2)
    x_c = sb("x_c", [P, 16, S], stack=m2)
    k_t = sb("k_t", [P, 4, S], stack=m3)
    p_t = sb("p_t", [P, 4, S], stack=m3)
    m3.close()
    m3 = ExitStack()
    y_hi = sb("y_hi", [P, 4, S], F32R, stack=m3)
    y_lo = sb("y_lo", [P, 4, S], F32R, stack=m3)
    m3.close()
    m2.close()

    a1, a2 = ExitStack(), ExitStack()
    k_a = sb("k_a", [P, KT, S], stack=a1)
    v_a = sb("v_a", [P, 4, D], stack=a1)
    y_a = sb("y_a", [P, 4, D], stack=a1)
    s_r = sb("s_r", [P, TRI], stack=a2)
    p_r = sb("p_r", [P, TRI], stack=a2)
    p_c = sb("p_c", [P, TRI], stack=a2)
    strip = sb("strip", [P, 2, S], stack=a2)
    ada_w = sb("ada_w", [P, 3, D], stack=a2)
    a2.close()
    hot_sb = sb("hot_sb", [33, S + P], stack=a2)
    rel_sb = sb("rel_sb", [33, 16], stack=a2)
    bias_v = sb("bias_v", [16, S + P], stack=a2)
    a2.close()
    a1.close()
    a1 = ExitStack()
    yz_lo = sb("yz_lo", [P, KT, S], F32R, stack=a1)
    sb("gap", [P, 2 * KT * S], stack=a1)
    yz_hi = sb("yz_hi", [P, KT, S], F32R, stack=a1)
    a1.close()
    m1.close()
    q_a = low[:, :].rearrange("p (k n) -> p k n", n=S)
    z_a = res = q_a
    gate = v_a[:, :, :].rearrange("p t (a n) -> p (t a) n", n=S)
    merged = y_a[:, :, :].rearrange("p t (a n) -> p (t a) n", n=S)
    c_x = vr[:, :, :].rearrange("p a n -> p (a n)")
    spare = p_r[:, P:P + D]
    c_ctx = p_c[:, 0:D]
    skew = nc.dram_tensor("skew", (16, S + P), F32, kind="Internal").ap()

    e1 = ExitStack()
    conv_c = sb("conv_c", [P, 4, S], stack=e1)
    conv_u = sb("conv_u", [P, 4, CW], stack=e1)
    q_r = sb("q_r", [P, 4, S], stack=e1)
    k_r = sb("k_r", [P, 4, S], stack=e1)
    v_r = sb("v_r", [P, 4, S], stack=e1)
    g_r = sb("g_r", [P, 4, S], stack=e1)
    k_x = sb("k_x", [P, 4, CTX], stack=e1)
    v_x = sb("v_x", [P, 2, S], stack=e1)
    rope_t = sb("rope_t", [P, 2, S], stack=e1)
    rope_u = sb("rope_u", [P, 2, CTX], stack=e1)
    diff_t = sb("diff_t", [P, TOEP], stack=e1)
    ahead = sb("ahead", [P, TOEP], stack=e1)
    behind = sb("behind", [P, TOEP], stack=e1)
    lg = sb("lg", [P, 48], stack=e1)
    e2 = ExitStack()
    c_hi = sb("c_hi", [P, KT, CTX], F32R, stack=e2)
    c_lo = sb("c_lo", [P, KT, CTX], F32R, stack=e2)
    e2.close()
    e2 = ExitStack()
    w_r = sb("w_r", [P, 6, S], stack=e2)
    decay = sb("decay", [P, TOEP], stack=e2)
    decay_x = sb("decay_x", [P, 2, S], stack=e2)
    e2.close()
    e1.close()
    root_c = k_x[:, 0, :]
    conv_f = conv_u[:, :, :].rearrange("p a b -> p (a b)")
    DECAY = (decay[:, :], conv_f[:, 0:TOEP])
    DECAY_X = (decay_x[:, :, :], conv_f[:, TOEP:TOEP + 2 * S].rearrange("p (a n) -> p a n", n=S))
    BACK = (tt[:, 0, :], rope_u[:, :, :].rearrange("p a n -> p (a n)"))
    c_mean, c_root = rope_t[:, 0, :], rope_t[:, 1, :]
    c_in = g_r[:, :, :].rearrange("p a (b n) -> p (a b) n", n=CTX)
    f1 = ExitStack()
    hid_hi = sb("hid_hi", [P, FF, S], F32R, stack=f1)
    hid_lo = sb("hid_lo", [P, FF, S], F32R, stack=f1)
    f1.close()
    o1 = ExitStack()
    pc = sb("pc", [P, 4, PW], stack=o1)
    pool_a = sb("pool_a", [P, 4, PW], stack=o1)
    pool_b = sb("pool_b", [P, 4, PW], stack=o1)
    u_s = sb("u_s", [P, 4, S], stack=o1)
    v_s = sb("v_s", [P, 4, S], stack=o1)
    inv_t = sb("inv_t", [P, 4, S], stack=o1)
    sg_r = sb("sg_r", [P, 3, S], stack=o1)
    pool_ws = sb("pool_ws", [P, 4, P], stack=o1)
    sg_ws = sb("sg_ws", [P, 4, P], stack=o1)
    bn = sb("bn", [P, 4, 16], stack=o1)
    o1.close()
    conv_out = k_t
    conv_in = pb[:, 0:5, :].rearrange("p a b -> p (a b)")[:, 0:4 * 516].rearrange("p (b n) -> p b n", n=516)
    q_t = low[:, 0:2048].rearrange("p (c n) -> p c n", n=S)
    bd = low[:, 2048:3072].rearrange("p (c w n) -> p c w n", w=2, n=P)
    v_w = low[:, 0:2176].rearrange("p (k n) -> p k n", n=136)
    small = low[:, 3072:4096]
    g_tok = small[:, 0:32].rearrange("p (t g) -> p t g", g=8)
    w_g = small[:, 32:160].rearrange("p (k g) -> p k g", g=8)
    lf = small[:, 160:176].rearrange("p (t g) -> p t g", g=4)
    u_c = small[:, 176:192].rearrange("p (t g) -> p t g", g=4)
    b_c = small[:, 192:208].rearrange("p (t g) -> p t g", g=4)
    gs = small[:, 208:240].rearrange("p (t g) -> p t g", g=8)
    ga = small[:, 240:256].rearrange("p (t g) -> p t g", g=4)
    gb = small[:, 256:272].rearrange("p (t g) -> p t g", g=4)
    neg = small[:, 784:912]
    rows = small[0:64, 272:784]

    bank = [ctx.enter_context(nc.psum_tensor(f"bank{i}", [P, S], F32)) for i in range(8)]

    raw_in = [sem("raw_in0"), sem("raw_in1")]
    hi_done, lo_done, mm_done = sem("hi_done"), sem("lo_done"), sem("mm_done")
    ev_act, ev_dve = sem("ev_act"), sem("ev_dve")
    LEAD = 4
    evs = {"act": 0, "dve": 0}
    EV = {}
    for name, blocks_, groups in STAGES:
        base = name.rstrip("0123")
        if base == "up":
            EV[name] = ("both", dict(evs))
            evs["act"] += blocks_
            evs["dve"] += blocks_
            continue
        by = "act" if base in ("x_m", "o_m", "z_m", "z_a", "gate_a", "q_a", "k_a", "gate_m", "a_e", "b_e", "q_r", "k_r", "v_r", "g_r", "pool", "u_s", "v_s") else "dve"
        EV[name] = (by, dict(evs))
        n = blocks_ * groups // (2 if base == "down" else 1)
        evs[by] += n
    block = ctx.enter_context(nc.Block())
    LAST = STAGES[-1][0]
    BLOCKS = FIRST[LAST] + COUNT[LAST]

    @block.sync
    def _(sp):
        def stream(lo, hi):
            with sp.Fori((lo - 2) // 2, (hi - 2) // 2) as i:
                for s in range(2):
                    sp.wait_ge(lo_done, 2 * i + s + 1)
                    sp.dma_start(raw[:, s, :], blocks[ds(2 * i + s + 2, 1)].rearrange("a p n -> p (a n)"))\
                      .then_inc(raw_in[s], 16)

        for s in range(2):
            sp.dma_start(raw[:, s, :], blocks[s]).then_inc(raw_in[s], 16)
        a0 = FIRST["q_a"]
        stream(2, a0 + 2)
        with sp.Fori(0, ADA // 2) as i:
            for s in range(2):
                n = 2 * i + s
                for r in range(3):
                    sp.wait_ge(sem(f"ada_sum{r}"), n + 1)
                    sp.dma_start(ada_w[:, r, :], ada[ds(3 * n + r, 1)].rearrange("a p d -> p (a d)"))\
                      .then_inc(sem(f"ada_in{r}"), 16)
                sp.wait_ge(lo_done, n + (a0 + 1))
                sp.dma_start(raw[:, s, :], blocks[ds(n + (a0 + 2), 1)].rearrange("a p n -> p (a n)"))\
                  .then_inc(raw_in[s], 16)
        stream(a0 + ADA + 2, BLOCKS)
        sp.wait_ge(sem("out_ready"), 8)
        sp.dma_start(out.rearrange("(k p) n -> p k n", p=P), low[:, :].rearrange("p (k n) -> p k n", n=S))\
          .then_inc(sem("out_sent"), 16)
        sp.wait_ge(sem("out_sent"), 16)

    @block.gpsimd
    def _(pool):
        with pool.Fori(0, BLOCKS // 2) as i:
            for s in range(2):
                pool.wait_ge(hi_done, 2 * i + s + 1)
                pool.tensor_tensor(w_lo[:, s, :], raw[:, s, :], w_hi[:, s, :].bitcast(F32), ALU.subtract)\
                    .then_inc(lo_done, 1)

    @block.scalar
    def _(act):
        own = Tally(act, sem("act_own"))

        def split(n, s, after):
            act.wait_ge(raw_in[s], 16 * n + 16)
            act.wait_ge(mm_done, after)
            act.activation(w_hi[:, s, :], raw[:, s, :], ACT.Copy).then_inc(hi_done, 1)

        def stage(name, free, between=None, has_two=False, late=None):
            n0, g0, per = FIRST[name], GROUP0[name], PER[name]
            blocks_ = COUNT[name]

            def pair(i, last=False, first=False):
                for s in range(2):
                    if not (last and s == 1) and not (first and has_two and s == 0):
                        split(n0 // 2 + i + (s + 1) // 2, 1 - s, 1 + g0 + per * (2 * i + s))
                    if late and s == 0 and not first:
                        late(i - 1)
                    if free:
                        for m in range(per):
                            act.wait_ge(mm_done, 2 + g0 + per * (2 * i + s) + m)
                            free(per * (2 * i + s) + m, (per * s + m) % 4, i)
                if between:
                    between(i)

            pairs = blocks_ // 2
            whole = pairs - 1 if name == LAST else pairs
            if has_two or late:
                pair(0, first=True)
                if whole > 1:
                    with act.Fori(1, whole) as i:
                        pair(i)
            elif whole > 1:
                with act.Fori(0, whole) as i:
                    pair(i)
            elif whole == 1:
                pair(0)
            if name == LAST:
                pair(whole, last=True)
            if late:
                late(pairs - 1)

        act.sem_inc(ev_act, LEAD)
        act.sem_inc(sem("xc_ready"), 4)
        for k in range(0, KT, 2):
            act.dma_start(pb[:, k:k + 2, :], xt[:, k:k + 2, :]).then_inc(sem(f"x_in{k}"), 16)
        act.dma_start(col[:, :], cols).then_inc(sem("consts"), 16)
        act.dma_start(sq_c[:, :, :], square[:, 0:2, :]).then_inc(sem("consts"), 16)
        act.dma_start(neg, square[:, 2, :]).then_inc(sem("consts"), 16)
        act.dma_start(fold[:, :, :, :], fold_w).then_inc(sem("fold_in"), 16)
        act.dma_start(fold_b[:, :, :, :], fold_c).then_inc(sem("fold_in"), 16)
        act.dma_start(v_w[:, :, 0:P], bd_v).then_inc(sem("bd_in"), 16)
        halved = [0]

        def split_part(stage_, k, parts, second=1):
            if k == 0:
                act.wait_ge(raw_in[second], 8 * FIRST[stage_] + 16)
                if second:
                    act.wait_ge(mm_done, 1 + GROUP0[stage_])
            e = slice(2048 // parts * k, 2048 // parts * (k + 1))
            part = act.activation(w_hi[:, second, e], raw[:, second, e], ACT.Copy)
            if k == parts - 1:
                part.then_inc(hi_done, 1)

        def root_of(what, src=None, n=S, ready=None, var=var, root=root, before=None, second=1):
            for k in range(KT if src else 0):
                if what != "first" or k >= 2:
                    act.wait_ge(sem("sq_used"), SQ_AT[what] + k - 1)
                if ready:
                    act.wait_ge(ready, k + 1)
                act.activation(sq[:, k % 2, :n], src(k), ACT.Square).then_inc(sem("sq_ready"), 1)
                if before:
                    split_part(before, k, KT, second)
            v = NORM[what]
            act.wait_ge(sem("sq_used"), SQ_AT[what] + 8 + SUMMED[what])
            act.activation(var[:, :n], bank[4][:, :n], ACT.Ln, scale=1.0 / D, bias=EPS).then_inc(sem("var_ready"), 1)
            act.wait_ge(sem("var_ready"), v + 1)
            act.activation(root[:, :n], var[:, :n], ACT.Exp, scale=-0.5).then_inc(sem("root_ready"), 1)

        def squares_with(name, what):
            def free(g, b, i):
                act.wait_ge(ev_dve, g + (LEAD + EV[name][1]["dve"] + 1))
                act.wait_ge(sem("sq_used"), g + (SQ_AT[what] - 1))
                act.activation(sq[:, b % 2, :], res[:, ds(g, 1), :], ACT.Square).then_inc(sem("sq_ready"), 1)
            return free

        def squares_down(i_, what):
            def late(i):
                act.wait_ge(ev_dve, i + (LEAD + EV[f"down{i_}"][1]["dve"] + 1))
                act.wait_ge(sem("sq_used"), i + SQ_AT[what])
                act.activation(sq[:, 0, :], res[:, ds(i, 1), :], ACT.Square).then_inc(sem("sq_ready"), 1)
            return late

        def upper(n=S, shift=None, dst=x_hi, before=None):
            w = halved[0]
            for k in range(KT):
                act.wait_ge(sem("t_ready"), 8 * w + k + 1)
                if shift is None:
                    act.activation(dst[:, k, :n], tt[:, k % 2, :n], ACT.Copy).then_inc(sem("xh_ready"), 1)
                else:
                    act.activation(dst[:, k, :n], tt[:, k % 2, :n], ACT.Identity, bias=shift(k)).then_inc(sem("xh_ready"), 1)
                if before and k < 4:
                    split_part(before, k, 4)
            halved[0] += 1

        def x_tile(k):
            if k % 2 == 0:
                act.wait_ge(sem(f"x_in{k}"), 16)
            return pb[:, k, :]
        root_of("first", x_tile, before="x_m", second=0)
        split(0, 1, 1)
        upper()

        def x_m_free(g, b, i):
            act.wait_ge(sem("conv_done"), 4 * i + b + 1)
            act.wait_ge(sem("vg_mm"), 4 * i + b + 1)
            act.activation(conv_in[:, b, 3:3 + S], bank[b][:, :], ACT.Copy).then_inc(ev_act, 1)

        def x_m_silu(i):
            for b in range(4):
                act.wait_ge(sem("conv_done"), 4 + 4 * i + b + 1)
                act.activation(x_c[:, ds(4 * i + b, 1), :], conv_out[:, b, :], ACT.Silu).then_inc(sem("xc_ready"), 1)

        act.wait_ge(sem("pad_ready"), 1)
        stage("x_m", x_m_free, x_m_silu, has_two=True)

        def load_bd(h):
            act.dma_start(bd, bd_qk[:, h, :].rearrange("p (c w n) -> p c w n", w=2, n=P)).then_inc(sem("bd_ready"), 16)

        def query_key(h, parts=range(8)):
            for j in parts:
                act.wait_ge(sem("qk_mm"), 8 * h + j + 1)
                dst = (q_t, k_t)[j // 4][:, j % 4, :]
                act.activation(dst, bank[4 + j % 2][:, :], ACT.Copy, scale=1.0 if j < 4 else 512 ** -0.5)\
                   .then_inc(sem("qk_ev"), 1)

        act.wait_ge(mm_done, 1 + GROUP0["o_m0"])
        act.wait_ge(sem("vg_done"), 2 + 16)
        load_bd(0)
        query_key(0, range(6))
        act.wait_ge(sem("g_ready"), 1)
        own(act.activation(ga, gs[:, :, 4:8], ACT.Abs))
        own(act.activation(gb, ga, ACT.Exp, scale=-1.0))
        act.activation(ga, gb, ACT.Ln, bias=1.0).then_inc(sem("ln_ready"), 1)
        query_key(0, range(6, 8))
        act.wait_ge(sem("bm_ready"), 1)
        act.activation(rows[32:36, :], root[32:36, :], ACT.Exp, scale=-1.0).then_inc(sem("rows_ready"), 1)

        for h in range(4):
            if h:
                act.wait_ge(mm_done, 1 + GROUP0[f"o_m{h}"])
                act.wait_ge(sem("y_done"), 4 * h)
                query_key(h)
            act.wait_ge(sem("nm_ready"), h + 1)
            for j in range(4):
                last = act.activation(p_t[:, j, 0:P], tt[:, 1, P * j:P * j + P], ACT.Exp, bias=u_c[:, j, h:h + 1])
                if j < 3:
                    last = act.activation(p_t[:, j, P:S - P * j], tt[:, 0, P * j + P:S], ACT.Exp, bias=u_c[:, j, h:h + 1])
                last.then_inc(sem("e_done"), 1)
            act.wait_ge(sem("s_mm"), 4 * h + 4)
            if h < 3:
                load_bd(h + 1)
            stage(f"o_m{h}", lambda g, b, i: act.activation(q_t[:, b, :], bank[b][:, :], ACT.Sigmoid).then_inc(ev_act, 1))
            act.wait_ge(sem("den_mm"), h + 1)
            act.activation(root[:, :], bank[6][:, :], ACT.Abs).then_inc(sem("abs_done"), 1)
            for k in range(4):
                split_part(f"z_m{h}", k, 4)
            for e in range(4):
                act.wait_ge(sem("h_done"), 4 * h + e + 1)
                if e >= 2:
                    act.wait_ge(sem("pair_added"), h + 1)
                act.activation(sq[:, e % 2, :], q_t[:, e, :], ACT.Square).then_inc(sem("hsq_ready"), 1)
            act.wait_ge(sem("hvar_ready"), h + 1)
            own(act.activation(root[:, :], root[:, :], ACT.Ln, bias=EPS))
            act.activation(root[:, :], root[:, :], ACT.Exp, scale=-0.5).then_inc(sem("hroot_ready"), 1)
            def z_free(g, b, i):
                if b >= 2:
                    act.wait_ge(sem("prod_done"), 4 * h + b - 1)
                act.activation(sq[:, b % 2, :], bank[b][:, :], ACT.Silu).then_inc(ev_act, 1)
                act.wait_ge(sem("prod_done"), 4 * h + b + 1)
                act.activation(y_hi[:, b, :], q_t[:, b, :], ACT.Copy).then_inc(sem("yh_done"), 1)
            stage(f"z_m{h}", z_free, has_two=True)
            if h == 3:
                act.wait_ge(sem("y_done"), 16)
                act.dma_start(rel_sb[0:32, :], rel).then_inc(sem("rel_in"), 16)
                act.dma_start(hot_sb[:, :], hot).then_inc(sem("rel_in"), 16)
                act.dma_start(c_x, c_rows[:, 0, :]).then_inc(sem("c_in"), 16)
                act.dma_start(c_ctx, c_rows[:, 1, :]).then_inc(sem("c_in"), 16)
            stage(f"w_pb{h}", None)

        act.wait_ge(sem("c_in"), 32)
        act.activation(c_ctx, c_ctx, ACT.Silu)
        act.activation(c_x, c_x, ACT.Silu).then_inc(sem("silu_c"), 1)
        act.wait_ge(sem("bias_mm"), 1)
        act.activation(bias_v[:, 0:S], bank[4][0:16, :], ACT.Copy)
        act.activation(bias_v[:, S:], bank[5][0:16, 0:P], ACT.Copy).then_inc(sem("bias_ready"), 1)
        act.wait_ge(sem("bias_ready"), 1)
        act.dma_start(skew, bias_v[:, :]).then_inc(sem("skew_out"), 16)

        def load_strip(h):
            src = bass.AP(skew.tensor, h * (S + P), [[1, P], [1, S]])
            act.dma_start(strip[:, h % 2, :], src).then_inc(sem(f"strip_in{h % 2}"), 16)
        stage("q_a", lambda g, b, i: act.activation(q_a[:, ds(g, 1), :].rearrange("p a (t n) -> p (a t) n", n=P), backward(b), ACT.Copy, scale=0.125)
              .then_inc(ev_act, 1))
        act.wait_ge(sem("skew_out"), 16)
        load_strip(0)
        load_strip(1)
        stage("k_a", lambda g, b, i: act.activation(k_a[:, ds(g, 1), :], bank[b][:, :], ACT.Copy).then_inc(ev_act, 1))
        stage("v_a", None)
        def pc_half(h):
            act.wait_ge(sem("t_mm"), 3 * h + 1)
            if h:
                act.wait_ge(sem("pv_mm"), h)
            act.activation(p_c[:, 0:S], bank[4][:, :], ACT.Copy).then_inc(sem("pc_act"), 1)

        for h in range(16):
            if h:
                pc_half(h - 1)
                act.wait_ge(sem("t_mm"), 3 * h)
            act.wait_ge(sem("max_ready"), h + 1)
            for i in range(4):
                o = TRI_AT[i]
                last = act.activation(p_r[:, o:o + P * (i + 1)], s_r[:, o:o + P * (i + 1)], ACT.Exp,
                                      bias=stat(h, 1)[:, i:i + 1], accum_out=stat(h, 2)[:, i:i + 1])
            last.then_inc(sem("p_done"), 1)
            if h < 14:
                load_strip(h + 2)
        pc_half(15)
        act.wait_ge(sem("qk_a_mm"), 16)
        stage("z_a", lambda g, b, i: act.activation(z_a[:, ds(g, 1), :], bank[b][:, :], ACT.Silu).then_inc(ev_act, 1))
        for c in range(8):
            act.wait_ge(sem("yz_f"), c + 1)
            act.activation(yz_hi[:, c, :], tt[:, c % 2, :], ACT.Copy).then_inc(sem("yz_h"), 1)
        act.wait_ge(sem("yz_l"), 8)
        act.dma_start(res, xt).then_inc(sem("res_in"), 16)

        def gate_b(g, more=0):
            return col[:, ds(g + (COL["gate_b"] + more), 1)]
        stage("gate_a", lambda g, b, i: act.activation(gate[:, ds(g, 1), :], bank[b][:, :], ACT.Sigmoid, bias=gate_b(g)).then_inc(ev_act, 1))
        stage("w_pa", None)
        act.wait_ge(ev_dve, LEAD + EV["gate_m"][1]["dve"])

        def merged_hi(i):
            for b in range(4):
                act.wait_ge(sem("mrg"), 4 * i + b + 1)
                act.activation(yz_hi[:, ds(4 * i + b, 1), :], merged[:, ds(4 * i + b, 1), :], ACT.Copy).then_inc(sem("mrg_hi"), 1)
        stage("gate_m", lambda g, b, i: act.activation(gate[:, ds(g, 1), :], bank[b][:, :], ACT.Sigmoid, bias=gate_b(g, 8)).then_inc(ev_act, 1),
              merged_hi)
        act.wait_ge(sem("mrg_lo"), 8)
        act.dma_start(c_in, ctxt).then_inc(sem("ctx_in"), 16)
        stage("w_out", squares_with("w_out", "out"))
        act.wait_ge(sem("ada_sum2"), 1 + ADA)
        root_of("out")
        act.wait_ge(sem("mod_ready"), 1)
        act.dma_start(rope_t[:, :, :], rope_x).then_inc(sem("rope_in"), 16)
        act.dma_start(rope_u[:, :, :], rope_c).then_inc(sem("rope_in"), 16)
        act.dma_start(diff_t[:, :], diff).then_inc(sem("diff_in"), 16)

        def shift(m0, who=0):
            return lambda k: (mod_c if who else mod)[:, m0 + k:m0 + k + 1]
        root_of("even", lambda k: res[:, k, :], ready=sem("x1_ready"), before="a_e")
        upper(shift=shift(0))
        act.wait_ge(sem("pad2_ready"), 1)
        stage("a_e", lambda g, b, i: act.activation(conv_u[:, b, 15:15 + S], bank[b][:, :], ACT.Copy).then_inc(ev_act, 1),
              has_two=True)
        act.wait_ge(sem("ctx_in"), 16)
        root_of("ctx", lambda k: c_in[:, k, :], n=CTX, var=k_x[:, 1, :], root=root_c, before="b_e")
        upper(n=CTX, shift=shift(0, 1), dst=c_hi)

        def b_free(g, b, i):
            if b >= 2:
                act.wait_ge(sem("u_made"), b - 1)
            act.activation(sq[:, b % 2, :], bank[b][:, :], ACT.Sigmoid).then_inc(ev_act, 1)
        stage("b_e", b_free, has_two=True)

        def swapped(scale):
            def free(src, to, other):
                act.activation(to, src, ACT.Copy, scale=scale)
                act.activation(other[0:64], src[64:P], ACT.Copy, scale=scale)
                return act.activation(other[64:P], src[0:64], ACT.Copy, scale=scale)
            return free
        q_swap = swapped(P ** -0.5)
        stage("q_r", lambda g, b, i: q_swap(bank[b][:, :], q_r[:, g, :], g_r[:, g, :]).then_inc(ev_act, 1))
        k_swap = swapped(1.0)

        def k_free(g, b, i):
            h = g // 2
            if g % 2 == 0:
                k_swap(bank[b][:, :], k_r[:, h, :], v_r[:, h, :]).then_inc(ev_act, 1)
            else:
                swap = v_x[:, :, :].rearrange("p a (b n) -> p (a b) n", n=CTX)[:, h, :]
                k_swap(bank[b][:, :CTX], k_x[:, h, :], swap).then_inc(ev_act, 1)
        stage("k_r", k_free)

        def v_free(g, b, i):
            if g == 0:
                act.wait_ge(sem("roped"), 12)
            s, t = g // 6, g % 6
            dst = v_r[:, t, 256 * s:256 * s + 256] if t < 4 else v_x[:, t - 4, 256 * s:256 * s + 256]
            act.activation(dst, bank[b][:, 0:256], ACT.Copy).then_inc(ev_act, 1)
        stage("v_r", v_free)
        own(act.activation(lg[:, 8:16], col[:, COL["decay"]:COL["decay"] + 8], ACT.Abs))
        own(act.activation(lg[:, 16:24], lg[:, 8:16], ACT.Exp, scale=-1.0))
        act.activation(lg[:, 8:16], lg[:, 16:24], ACT.Ln, bias=1.0).then_inc(sem("lg_ln"), 1)
        stage("g_r", lambda g, b, i: act.activation(g_r[:, g, :], bank[b][:, :], ACT.Silu).then_inc(ev_act, 1))
        for c in range(4):
            act.wait_ge(sem("conv_made"), 4)
            if c >= 2:
                act.wait_ge(sem("csq_mm"), c - 1)
            act.activation(sq[:, c % 2, :], conv_c[:, c, :], ACT.Square).then_inc(sem("csq"), 1)

        def decays(h):
            act.wait_ge(sem("decay_arg"), h + 1)
            own(act.activation(DECAY[h % 2], DECAY[h % 2], ACT.Exp))
            for j in range(2):
                own(act.activation(DECAY_X[h % 2][:, j, :], diff_t[:, S - P:], ACT.Exp, scale=lg[:, h:h + 1],
                                   bias=lg[:, 24 + 4 * j + h:25 + 4 * j + h]))
                if h:
                    act.wait_ge(sem("dx_used"), 2 * h + j - 1)
                act.activation(BACK[j], diff_t[:, S - P:], ACT.Exp, scale=lg[:, 40 + h:41 + h], bias=lg[:, 32 + 4 * j + h:33 + 4 * j + h])\
                   .then_inc(sem("dx_ready"), 1)

        def mix_upper(h):
            act.wait_ge(sem("mix_f"), h + 1)
            act.activation(x_hi[:, h, :], tt[:, 1, :], ACT.Copy).then_inc(sem("mix_hi"), 1)
        decays(0)
        act.wait_ge(sem("cvar"), 1)
        own(act.activation(c_root, c_root, ACT.Ln, bias=EPS))
        act.activation(c_root, c_root, ACT.Exp, scale=-0.5).then_inc(sem("croot"), 1)
        decays(1)
        for h in range(4):
            if h < 2:
                decays(h + 2)
            act.wait_ge(sem("y_out"), h + 1)
            if h == 0:
                act.wait_ge(sem("csq_mm"), 4)
            act.activation(sq[:, h % 2, :], q_r[:, h, :], ACT.Square).then_inc(sem("ysq"), 1)
            act.wait_ge(sem("c_norm"), h + 1)
            own(act.activation(conv_c[:, h, :], conv_c[:, h, :], ACT.Silu, bias=c1("ln_b", h)))
            act.activation(x_hi[:, 4 + h, :], conv_c[:, h, :], ACT.Copy).then_inc(sem("cmix_hi"), 1)
            if h:
                mix_upper(h - 1)
            act.wait_ge(sem("ysq_mm"), h + 1)
            act.activation(var[:, :], bank[7][:, :], ACT.Ln, scale=1.0 / P, bias=EPS).then_inc(sem("yvar"), 1)
            act.wait_ge(sem("yvar"), h + 1)
            act.activation(root[:, :], var[:, :], ACT.Exp, scale=-0.5).then_inc(sem("yroot"), 1)
        mix_upper(3)
        stage("even_out", squares_with("even_out", "ffn0"))

        def ffn(i):
            root_of(f"ffn{i}")
            upper(shift=shift(48 * i + 24), before=f"up{i}")
            before = EV[f"up{i}"][1]["dve"]

            n0, g0 = FIRST[f"up{i}"], GROUP0[f"up{i}"]

            def up(j, first=False):
                for s in range(2):
                    n = 2 * j + s
                    if not (first and s == 0):
                        split(n0 // 2 + j + (s + 1) // 2, 1 - s, 1 + g0 + 2 * n)
                    act.wait_ge(mm_done, 2 + g0 + 2 * n)
                    act.wait_ge(ev_dve, LEAD + before + n - 1)
                    act.activation(sq[:, s, :], bank[2 * s][:, :], ACT.Silu).then_inc(ev_act, 1)
                    act.wait_ge(ev_dve, LEAD + before + n + 1)
                    act.activation(hid_hi[:, ds(n, 1), :], tt[:, s, :], ACT.Copy).then_inc(sem("hid_h"), 1)
            up(0, first=True)
            with act.Fori(1, FF // 2) as j:
                up(j)
            stage(f"down{i}", None, late=squares_down(i, ("pool", "final")[i]))
        ffn(0)

        act.wait_ge(mm_done, 1 + GROUP0["pool"])
        act.dma_start(inv_t[:, :, :], inv).then_inc(sem("odd_in"), 16)
        act.dma_start(sg_r[:, :, :], sg_rows).then_inc(sem("odd_in"), 16)
        act.dma_start(pool_ws[:, :, :], pool_w).then_inc(sem("odd_in"), 16)
        act.dma_start(sg_ws[:, :, :], sg_w).then_inc(sem("odd_in"), 16)
        root_of("pool")
        upper(shift=shift(48), before="pool")
        act.wait_ge(sem("pad3_ready"), 1)
        stage("pool", lambda g, b, i: act.activation(pc[:, g, 8:8 + S], bank[b][:, :], ACT.Copy).then_inc(ev_act, 1), has_two=True)
        stage("u_s", lambda g, b, i: act.activation(u_s[:, g, :], bank[b][:, :], ACT.Gelu).then_inc(ev_act, 1))
        stage("v_s", lambda g, b, i: act.activation(v_s[:, b, 256 * (g // 4):256 * (g // 4) + 256], bank[b][:, 0:256], ACT.Gelu)
              .then_inc(ev_act, 1))
        for g in range(4):
            act.wait_ge(sem("pool_mm"), g + 1)
            act.activation(x_hi[:, g, :], bank[4 + g % 2][:, :], ACT.Copy, scale=c1("pool_scale", g)).then_inc(sem("omix_hi"), 1)
        act.wait_ge(sem("sg_var"), 1)
        act.activation(bn[:, :, 8:9], bn[:, :, 7:8], ACT.Sqrt).then_inc(sem("sg_root"), 1)
        for g in range(4):
            act.wait_ge(sem("omix_f"), g + 1)
            act.activation(x_hi[:, 4 + g, :], tt[:, g % 2, :], ACT.Copy).then_inc(sem("omix_hi"), 1)
        stage("odd_out", squares_with("odd_out", "ffn1"))
        ffn(1)
        root_of("final")

    @block.vector
    def _(dve):
        own = Tally(dve, sem("dve_own"))
        norms = [0, 0]

        def ada_sums(name, i, s):
            n, early = 2 * i + (ADA_AT[name] + s), ADA_AT[name] < 8
            dve.wait_ge(sem("ada_kept"), n + 1)
            for r in range(2 if early else 0):
                dve.wait_ge(sem(f"ada_in{r}"), 16 * n + 16)
                dve.wait_ge(sem("ada_ctx"), 2 * n + r + 1)
                dve.tensor_tensor_reduce(spare, ada_w[:, r, :], c_ctx, 1.0, 0.0, ALU.mult, ALU.add,
                                         ada_col[:, 3 + r:4 + r]).then_inc(sem("ada_ctx"), 1)
            for r in range(3):
                if early:
                    dve.wait_ge(sem("ada_ctx"), 2 * n + 3)
                dve.wait_ge(sem(f"ada_in{r}"), 16 * n + 16)
                dve.tensor_tensor_reduce(ada_w[:, r, :], ada_w[:, r, :], c_x, 1.0, 0.0, ALU.mult, ALU.add,
                                         ada_col[:, r:r + 1]).then_inc(sem(f"ada_sum{r}"), 1)
            for r in range(3):
                dve.wait_ge(sem(f"ada_sum{r}"), n + 2)
            if early:
                dve.tensor_copy(mod[:, ds(2 * n, 2)], ada_col[:, 0:2])
                dve.tensor_copy(mod_c[:, ds(2 * n, 2)], ada_col[:, 3:5])
                last = dve.tensor_copy(mod[:, ds(n + 16, 1)], ada_col[:, 2:3])
            else:
                last = dve.tensor_copy(mod[:, ds(3 * n, 3)], ada_col[:, 0:3])
            last.then_inc(sem("ada_kept"), 1)

        def stage(name, free):
            g0, per = GROUP0[name], PER[name]
            blocks_ = COUNT[name]

            def pair(i):
                for s in range(2):
                    if name in ADA_AT:
                        ada_sums(name, i, s)
                    if free:
                        for m in range(per):
                            dve.wait_ge(mm_done, 2 + g0 + per * (2 * i + s) + m)
                            free(per * (2 * i + s) + m, (per * s + m) % 4, i)

            if blocks_ > 2:
                n0 = own.n
                with dve.Fori(0, blocks_ // 2) as i:
                    pair(i)
                assert own.n == n0, "no own waits in this loop"
            else:
                pair(0)

        def norm(src, scale, n=S, shift=None, dst=(x_hi, x_lo), into=None, into_ready=None, root=root):
            v, w = norms
            dve.wait_ge(sem("root_ready"), v + 1)
            norms[0] += 1
            for k in range(KT + 1):
                if k < KT:
                    if into is not None:
                        dve.scalar_tensor_tensor(into(k), src(k), scale(k), root[:, :n], ALU.mult, ALU.mult)\
                           .then_inc(sem(into_ready), 1)
                        continue
                    if w or k >= 2:
                        dve.wait_ge(sem("xl_ready"), 8 * w + k - 1)
                    dve.scalar_tensor_tensor(tt[:, k % 2, :n], src(k), scale(k), root[:, :n], ALU.mult, ALU.mult)\
                       .then_inc(sem("t_ready"), 1)
                if k and into is None:
                    dve.wait_ge(sem("xh_ready"), 8 * w + k)
                    if shift is None:
                        dve.tensor_tensor(dst[1][:, k - 1, :n], tt[:, (k - 1) % 2, :n], dst[0][:, k - 1, :n].bitcast(F32), ALU.subtract)\
                           .then_inc(sem("xl_ready"), 1)
                    else:
                        dve.scalar_tensor_tensor(dst[1][:, k - 1, :n], tt[:, (k - 1) % 2, :n], shift(k - 1),
                                                 dst[0][:, k - 1, :n].bitcast(F32), ALU.add, ALU.subtract)\
                           .then_inc(sem("xl_ready"), 1)
            if into is None:
                norms[1] += 1

        total = tt[:, 0, :]

        def add_square(what, k, slot):
            dve.wait_ge(sem("sq_ready"), k + (8 * NORM[what] + 1))
            dve.wait_ge(sem("sq_used"), k + SQ_AT[what])
            dve.tensor_tensor(total, total, sq[:, slot, :], ALU.add).then_inc(sem("sq_used"), 1)

        dve.sem_inc(ev_dve, LEAD)
        dve.sem_inc(sem("conv_done"), 4)
        dve.memset(ones[:, :], 1.0).then_inc(sem("ones_ready"), 1)
        dve.wait_ge(sem("consts"), 48)
        norm(lambda k: pb[:, k, :], lambda k: c1("g_in", k))
        dve.wait_ge(sem("fold_in"), 32)
        for j in range(3):
            part = fold[:, j, :, :].rearrange("p (k g) c -> p k g c", g=8)
            last = dve.tensor_tensor(part, part, fold_b[:, j, :, :].unsqueeze(2).to_broadcast([P, 16, 8, 4]), ALU.mult)
        own(last)
        own(dve.tensor_reduce(fold_s[:, :, :], fold[:, :, :, :], AX.X, ALU.add))
        k_g = lambda j: fold_s[:, j, :].rearrange("p (k g) -> p k g", g=8)
        own(dve.tensor_tensor(w_g, k_g(0), k_g(1), ALU.add))
        dve.tensor_copy(v_w[:, :, P:136], k_g(2)).then_inc(sem("fold_ready"), 1)
        own(dve.memset(g_tok, 0.0))
        dve.memset(conv_in[:, :, 0:3], 0.0).then_inc(sem("pad_ready"), 1)

        def cw(g, tap):
            return col[:, ds(g * 4 + (COL["conv_w"] + tap), 1)]

        def values_out(i, b):
            g = 4 * i + b
            dve.wait_ge(sem("vg_mm"), 4 + g + 1)
            for half in range(2):
                src = bank[4 + 2 * (b % 2) + half]
                part = src[:, 0:272].rearrange("p (t n) -> p t n", n=136)
                dst = v_m[:, 2 * half:2 * half + 2, ds(g * P, P)]
                dve.tensor_copy(dst, part[:, :, 0:P])
                acc = g_tok[:, 2 * half:2 * half + 2, :]
                step = dve.tensor_tensor(acc, acc, part[:, :, P:136], ALU.add)
                if half == 0:
                    own(step)
            own(step)
            dve.sem_inc(sem("vg_done"), 1)

        n0 = own.n
        with dve.Fori(0, 4) as i:
            own.n = n0 + 20 * i
            for b in range(5):
                if b:
                    values_out(i, b - 1)
                if b == 4:
                    break
                g = 4 * i + b
                dve.wait_ge(ev_act, LEAD + g + 1)
                dve.wait_ge(sem("xc_ready"), g + 1)
                y = conv_out[:, b, :]
                own(dve.tensor_scalar(y, conv_in[:, b, 0:S], cw(g, 0), col[:, ds(g + COL["conv_b"], 1)], ALU.mult, ALU.add))
                for tap in range(1, 4):
                    step = dve.scalar_tensor_tensor(y, conv_in[:, b, tap:tap + S], cw(g, tap), y, ALU.mult, ALU.add)
                    if tap < 3:
                        own(step)
                step.then_inc(sem("conv_done"), 1)
        own.n = n0 + 20 * 4

        dve.wait_ge(sem("grow_mm"), 1)
        dve.tensor_copy(sq[0:8, 0, :], bank[0][0:8, :]).then_inc(sem("grow_out"), 1)
        dve.wait_ge(sem("gates_mm"), 1)
        own(dve.tensor_tensor(gs, bank[7][:, 0:32].rearrange("p (t g) -> p t g", g=8), g_tok, ALU.add))
        for t in range(4):
            last = dve.tensor_tensor(gs[:, t, :], gs[:, t, :], col[:, COL["b_if"]:COL["b_if"] + 8], ALU.add)
        own(last)
        dve.sem_inc(sem("g_ready"), 1)
        dve.wait_ge(sem("ln_ready"), 1)
        own(dve.tensor_scalar(lf, gs[:, :, 4:8], 0.0, None, ALU.min))
        dve.tensor_tensor(lf, lf, ga, ALU.subtract).then_inc(sem("lf_ready"), 1)
        dve.wait_ge(sem("b_mm"), 1)
        own(dve.tensor_copy(b_c, bank[6][:, 64:80].rearrange("p (t g) -> p t g", g=4)))
        dve.tensor_tensor(u_c, gs[:, :, 0:4], b_c, ALU.subtract).then_inc(sem("u_ready"), 1)
        dve.wait_ge(sem("rows_mm"), 1)
        own(dve.tensor_copy(sq[0:4, 0, :], bank[6][0:4, :]))
        own(dve.tensor_tensor_scan(sq[0:4, 1, :], sq[0:4, 0, :], sq[0:4, 0, :], 0.0, ALU.max, ALU.max))
        own(dve.tensor_scalar(rows[0:4, :], sq[0:4, 1, :], -1.0, None, ALU.mult))
        own(dve.tensor_tensor(root[0:4, :], bank[7][0:4, :], sq[0:4, 1, :], ALU.add))
        dve.tensor_copy(root[32:36, :], root[0:4, :]).then_inc(sem("bm_ready"), 1)

        for h in range(4):
            dve.wait_ge(sem("bc_mm"), h + 1)
            if h:
                dve.wait_ge(sem("y_done"), 4 * h)
            dve.tensor_copy(tt[:, 0, :], bank[6][:, :])
            for j in range(4):
                last = dve.tensor_tensor(tt[:, 1, P * j:P * j + P], bank[6][:, P * j:P * j + P], neg, ALU.add)
            own(last)
            own(dve.tensor_copy(var[:, :], bank[7][:, :]))
            dve.sem_inc(sem("nm_ready"), 1)
            for j in range(4):
                dve.wait_ge(sem("s_mm"), 4 * h + j + 1)
                dve.wait_ge(sem("e_done"), 4 * h + j + 1)
                n = S - P * j
                dve.tensor_tensor(p_t[:, j, :n], bank[4 + j % 2][:, :n], p_t[:, j, :n], ALU.mult).then_inc(sem("pt_done"), 1)
            dve.wait_ge(sem("abs_done"), h + 1)
            own(dve.tensor_tensor(var[:, :], var[:, :], root[:, :], ALU.max))
            dve.wait_ge(ev_act, LEAD + EV[f"o_m{h}"][1]["act"] + 4)
            for e in range(4):
                dve.wait_ge(sem("h_mm"), 4 * h + e + 1)
                dve.tensor_tensor(q_t[:, e, :], bank[HB[e]][:, :], q_t[:, e, :], ALU.mult).then_inc(sem("h_done"), 1)
                dve.wait_ge(sem("h_done"), 4 * h + e + 1)
                if e == 0:
                    continue
                first = q_t[:, 0, :] if e == 1 else tt[:, 0, :]
                own(dve.tensor_tensor(tt[:, 0, :], first, q_t[:, e, :], ALU.add))
                dve.wait_ge(sem("hsq_ready"), 4 * h + e + 1)
                first = sq[:, 0, :] if e == 1 else tt[:, 1, :]
                own(dve.tensor_tensor(tt[:, 1, :], first, sq[:, e % 2, :], ALU.add))
                if e == 1:
                    dve.sem_inc(sem("pair_added"), 1)
            dve.sem_inc(sem("h_added"), 1)
            own(dve.reciprocal(var[:, :], var[:, :]))
            dve.wait_ge(sem("sum_mm"), h + 1)
            own(dve.tensor_scalar(tt[:, 0, :], bank[4][:, :], 1.0 / 512, None, ALU.mult))
            own(dve.tensor_tensor(tt[:, 1, :], tt[:, 0, :], tt[:, 0, :], ALU.mult))
            own(dve.scalar_tensor_tensor(root[:, :], bank[5][:, :], 1.0 / 512, tt[:, 1, :], ALU.mult, ALU.subtract))
            own(dve.tensor_tensor(root[:, :], root[:, :], var[:, :], ALU.mult))
            dve.tensor_tensor(root[:, :], root[:, :], var[:, :], ALU.mult).then_inc(sem("hvar_ready"), 1)
            dve.wait_ge(sem("hroot_ready"), h + 1)
            own(dve.tensor_tensor(root[:, :], root[:, :], var[:, :], ALU.mult))

            def lower(e):
                dve.wait_ge(sem("yh_done"), 4 * h + e + 1)
                dve.tensor_tensor(y_lo[:, e, :], q_t[:, e, :], y_hi[:, e, :].bitcast(F32), ALU.subtract).then_inc(sem("y_done"), 1)
            for e in range(4):
                own(dve.tensor_tensor(q_t[:, e, :], q_t[:, e, :], tt[:, 0, :], ALU.subtract))
                own(dve.scalar_tensor_tensor(q_t[:, e, :], q_t[:, e, :], c1("g_head", 4 * h + e), root[:, :], ALU.mult, ALU.mult))
                own(dve.scalar_tensor_tensor(q_t[:, e, :], x_c[:, 4 * h + e, :], c1("skip", 4 * h + e), q_t[:, e, :], ALU.mult, ALU.add))
                if e:
                    lower(e - 1)
                dve.wait_ge(ev_act, LEAD + EV[f"z_m{h}"][1]["act"] + e + 1)
                dve.tensor_tensor(q_t[:, e, :], q_t[:, e, :], sq[:, e % 2, :], ALU.mult).then_inc(sem("prod_done"), 1)
            lower(3)

            def pb_free(g, b, i):
                if h == 0:
                    dve.tensor_copy(pb[:, g, :], bank[b][:, :]).then_inc(ev_dve, 1)
                else:
                    dve.tensor_tensor(pb[:, g, :], bank[b][:, :], pb[:, g, :], ALU.add).then_inc(ev_dve, 1)
            stage(f"w_pb{h}", pb_free)

        own(dve.memset(rel_sb[32:33, :], 1.0))
        dve.sem_inc(sem("rel_one"), 1)
        dve.wait_ge(mm_done, 1 + GROUP0["w_pb3"] + 8)
        for r in range(3):
            dve.sem_inc(sem(f"ada_sum{r}"), 1)
        dve.sem_inc(sem("ada_ctx"), 1)
        dve.sem_inc(sem("ada_kept"), 1)
        dve.wait_ge(sem("silu_c"), 1)
        stage("q_a", None)
        stage("k_a", None)

        def v_a_free(g, b, i):
            dve.tensor_copy(v_a[:, b, ds((g - b) * 64, 256)], bank[b][:, 0:256]).then_inc(ev_dve, 1)
        stage("v_a", v_a_free)

        def finish(h):
            own(dve.reciprocal(stat(h, 3), stat(h, 2)))
            dve.wait_ge(sem("pv_mm"), h + 1)
            dve.tensor_tensor(y_a[:, :, 64 * h:64 * h + 64], bank[7][:, 0:256].rearrange("p (t n) -> p t n", n=64),
                              stat(h, 3).unsqueeze(2).to_broadcast([P, 4, 64]), ALU.mult).then_inc(sem("ya_done"), 1)

        def weights(h):
            dve.wait_ge(sem("t_mm"), 3 * h + 3)
            if h:
                dve.wait_ge(sem("pv_mm"), h)
            dve.tensor_copy(p_c[:, S:S + 384], bank[5][:, 0:384])
            dve.tensor_copy(p_c[:, S + 384:TRI], bank[6][:, 0:384]).then_inc(sem("pc_dve"), 1)

        for h in range(16):
            dve.wait_ge(sem("qk_a_mm"), h + 1)
            dve.wait_ge(sem(f"strip_in{h % 2}"), 16 * (h // 2) + 16)
            if h:
                dve.wait_ge(sem("p_done"), h)
            for i in range(4):
                o, n = TRI_AT[i], P * (i + 1)
                src = bank[SB[i]][:, SO[i]:SO[i] + n]
                last = dve.tensor_tensor_reduce(s_r[:, o:o + n], src, strip[:, h % 2, S - n:S], 1.0, -3e38,
                                                ALU.add, ALU.max, stat(h, 0)[:, i:i + 1])
            own(last)
            dve.tensor_scalar(stat(h, 1), stat(h, 0), -1.0, None, ALU.mult).then_inc(sem("max_ready"), 1)
            if h > 1:
                finish(h - 2)
            if h:
                weights(h - 1)
        finish(14)
        weights(15)
        finish(15)
        stage("z_a", None)
        for c in range(9):
            if c < 8:
                dve.wait_ge(ev_act, LEAD + EV["gate_a"][1]["act"])
                dve.wait_ge(sem("yt_mm"), c + 1)
                if c >= 2:
                    dve.wait_ge(sem("yz_l"), c - 1)
                dve.tensor_tensor(tt[:, c % 2, :].rearrange("p (t n) -> p t n", n=P), backward(4 + c % 3),
                                  z_a[:, c, :].rearrange("p (t n) -> p t n", n=P), ALU.mult).then_inc(sem("yz_f"), 1)
            if c:
                dve.wait_ge(sem("yz_h"), c)
                dve.tensor_tensor(yz_lo[:, c - 1, :], tt[:, (c - 1) % 2, :], yz_hi[:, c - 1, :].bitcast(F32), ALU.subtract)\
                   .then_inc(sem("yz_l"), 1)
        stage("gate_a", None)
        stage("w_pa", lambda g, b, i: dve.tensor_tensor(merged[:, ds(g, 1), :], bank[b][:, :], gate[:, ds(g, 1), :], ALU.mult)
              .then_inc(ev_dve, 1))
        dve.wait_ge(ev_dve, LEAD + EV["gate_m"][1]["dve"])
        n0 = own.n
        with dve.Fori(0, 2) as i:
            own.n = n0 + 4 * i
            for b in range(4):
                if b % 2 == 0:
                    ada_sums("gate_m", i, b // 2)
                g = 4 * i + b
                dve.wait_ge(ev_act, LEAD + EV["gate_m"][1]["act"] + g + 1)
                own(dve.tensor_tensor(tt[:, b % 2, :], gate[:, ds(g, 1), :], pb[:, ds(g, 1), :], ALU.mult))
                dve.tensor_tensor(merged[:, ds(g, 1), :], merged[:, ds(g, 1), :], tt[:, b % 2, :], ALU.add).then_inc(sem("mrg"), 1)
            for b in range(4):
                g = 4 * i + b
                dve.wait_ge(sem("mrg_hi"), g + 1)
                dve.tensor_tensor(yz_lo[:, ds(g, 1), :], merged[:, ds(g, 1), :], yz_hi[:, ds(g, 1), :].bitcast(F32), ALU.subtract)\
                   .then_inc(sem("mrg_lo"), 1)
        own.n = n0 + 8
        dve.wait_ge(sem("res_in"), 16)
        own(dve.memset(total, 0.0))

        def w_out_free(g, b, i):
            dve.tensor_tensor(res[:, ds(g, 1), :], bank[b][:, :], res[:, ds(g, 1), :], ALU.add).then_inc(ev_dve, 1)
            add_square("out", g, b % 2)
        stage("w_out", w_out_free)
        dve.wait_ge(ev_dve, LEAD + EV["a_e"][1]["dve"])
        dve.wait_ge(sem("ada_kept"), 1 + ADA)
        b0 = COL["ada_b"]
        own(dve.tensor_tensor(mod[:, :], mod[:, :], col[:, b0:b0 + 96], ALU.add))
        own(dve.tensor_tensor(mod_c[:, :], mod_c[:, :], col[:, b0:b0 + 16], ALU.add))
        for j, (m0, w0, who) in enumerate(((8, 0, 0), (32, 8, 0), (56, 16, 0), (80, 24, 0), (8, 0, 1))):
            w0 += COL["norm_w"]
            last = dve.scalar_tensor_tensor(coef[:, j, :], (mod_c if who else mod)[:, m0:m0 + 8], 1.0, col[:, w0:w0 + 8], ALU.add, ALU.mult)
        own(last)
        dve.sem_inc(sem("mod_ready"), 1)

        def shift(m0, who=0):
            return lambda k: (mod_c if who else mod)[:, m0 + k:m0 + k + 1]
        own(dve.memset(conv_u[:, :, 0:15], 0.0))
        own(dve.memset(conv_u[:, :, 15 + S:CW], 0.0))
        dve.sem_inc(sem("pad2_ready"), 1)
        norm(lambda k: res[:, k, :], lambda k: c1("g_out", k), into=lambda k: res[:, k, :], into_ready="x1_ready")
        norm(lambda k: res[:, k, :], lambda k: coef[:, 0, k:k + 1], shift=shift(0))
        norm(lambda k: c_in[:, k, :], lambda k: coef[:, 4, k:k + 1], n=CTX, shift=shift(0, 1), dst=(c_hi, c_lo), root=root_c)
        for b in range(4):
            dve.wait_ge(ev_act, LEAD + EV["b_e"][1]["act"] + b + 1)
            last = dve.tensor_tensor(conv_u[:, b, 15:15 + S], conv_u[:, b, 15:15 + S], sq[:, b % 2, :], ALU.mult)
            last.then_inc(sem("u_made"), 1)

        def convolve(c0):
            w = COL["conv2_w"]
            dve.wait_ge(sem("u_made"), c0 + 2)
            for c in (c0, c0 + 1):
                last = dve.tensor_scalar(conv_c[:, c, :], conv_u[:, c, 0:S], col[:, w + 31 * c:w + 31 * c + 1], None, ALU.mult)
                last.then_inc(sem("tap"), 1)
            n = 60 * (c0 // 2) + 2 * (c0 // 2)
            with dve.Fori(0, 10) as i:
                for tap in range(3):
                    for k, c in enumerate((c0, c0 + 1)):
                        dve.wait_ge(sem("tap"), 6 * i + (n + 2 * tap + k + 1))
                        dve.scalar_tensor_tensor(conv_c[:, c, :], conv_u[:, c, ds(3 * i + (tap + 1), S)],
                                                 col[:, ds(3 * i + (w + 31 * c + tap + 1), 1)], conv_c[:, c, :], ALU.mult, ALU.add)\
                           .then_inc(sem("tap"), 1)
            dve.wait_ge(sem("tap"), n + 62)
            dve.sem_inc(sem("conv_made"), 2)

        def rope(x, other, table):
            own(dve.tensor_tensor(x, x, table[:, 0, :], ALU.mult))
            own(dve.tensor_tensor(other, other, table[:, 1, :], ALU.mult))
            dve.tensor_tensor(x, x, other, ALU.add).then_inc(sem("roped"), 1)
        convolve(0)
        dve.wait_ge(sem("rope_in"), 32)
        for h in range(4):
            dve.wait_ge(ev_act, LEAD + EV["q_r"][1]["act"] + h + 1)
            rope(q_r[:, h, :], g_r[:, h, :], rope_t)
        for h in range(4):
            dve.wait_ge(ev_act, LEAD + EV["k_r"][1]["act"] + 2 * h + 2)
            rope(k_r[:, h, :], v_r[:, h, :], rope_t)
            swap = v_x[:, :, :].rearrange("p a (b n) -> p (a b) n", n=CTX)[:, h, :]
            rope(k_x[:, h, :], swap, rope_u)
        convolve(2)
        dve.wait_ge(sem("lg_ln"), 1)
        own(dve.tensor_scalar(lg[:, 0:8], col[:, COL["decay"]:COL["decay"] + 8], 0.0, None, ALU.min))
        own(dve.tensor_tensor(lg[:, 0:8], lg[:, 0:8], lg[:, 8:16], ALU.subtract))
        for j in range(2):
            dve.tensor_scalar(lg[:, 24 + 4 * j:28 + 4 * j], lg[:, 0:4], float(CTX - P * j), None, ALU.mult)
            dve.tensor_scalar(lg[:, 32 + 4 * j:36 + 4 * j], lg[:, 4:8], float(S - 1 + P * j), None, ALU.mult)
        own(dve.tensor_scalar(lg[:, 40:44], lg[:, 4:8], -1.0, None, ALU.mult))
        dve.wait_ge(sem("diff_in"), 16)
        dve.tensor_scalar(ahead[:, :], diff_t[:, :], 0.0, None, ALU.max)
        own(dve.tensor_scalar(behind[:, :], diff_t[:, :], 1.0, 0.0, ALU.add, ALU.min))
        dve.wait_ge(mm_done, 1 + GROUP0["g_r"])

        def arguments(h):
            d = DECAY[h % 2]
            own(dve.tensor_scalar(d, ahead[:, :], lg[:, h:h + 1], None, ALU.mult))
            own(dve.scalar_tensor_tensor(d, behind[:, :], lg[:, 40 + h:41 + h], d, ALU.mult, ALU.add))
            dve.sem_inc(sem("decay_arg"), 1)

        def head_out(h):
            dve.wait_ge(sem("wr_used"), 6 * h + 6)
            dve.tensor_copy(q_r[:, h, :], bank[6][:, :]).then_inc(sem("y_out"), 1)

        def head_norm(h):
            dve.wait_ge(sem("ysq"), h + 1)
            own(dve.tensor_tensor(q_r[:, h, :], q_r[:, h, :], g_r[:, h, :], ALU.mult))
            dve.wait_ge(sem("yroot"), h + 1)
            if h:
                dve.wait_ge(sem("mix_lo"), h)
            dve.tensor_tensor(tt[:, 1, :], q_r[:, h, :], root[:, :], ALU.mult).then_inc(sem("mix_f"), 1)
            dve.wait_ge(sem("mix_hi"), h + 1)
            dve.tensor_tensor(x_lo[:, h, :], tt[:, 1, :], x_hi[:, h, :].bitcast(F32), ALU.subtract).then_inc(sem("mix_lo"), 1)

        def conv_lower(c):
            dve.wait_ge(sem("cmix_hi"), 1 + c)
            dve.tensor_tensor(x_lo[:, 4 + c, :], conv_c[:, c, :], x_hi[:, 4 + c, :].bitcast(F32), ALU.subtract).then_inc(sem("cmix_lo"), 1)
        arguments(0)
        dve.wait_ge(sem("csq_mm"), 4)
        own(dve.tensor_scalar(c_mean, bank[6][:, :], 1.0 / 512, None, ALU.mult))
        own(dve.tensor_tensor(tt[:, 1, :], c_mean, c_mean, ALU.mult))
        dve.scalar_tensor_tensor(c_root, bank[7][:, :], 1.0 / 512, tt[:, 1, :], ALU.mult, ALU.subtract).then_inc(sem("cvar"), 1)
        arguments(1)
        dve.wait_ge(ev_act, LEAD + EV["g_r"][1]["act"] + 4)

        def context_decays(h):
            for j in range(2):
                dve.wait_ge(sem("dx_ready"), 2 * h + j + 1)
                own(dve.tensor_tensor(DECAY_X[h % 2][:, j, :], DECAY_X[h % 2][:, j, :], BACK[j], ALU.add))
                dve.sem_inc(sem("dx_used"), 1)
        context_decays(0)
        for h in range(4):
            if h:
                head_out(h - 1)
            for j in range(6):
                dve.wait_ge(sem("sr_mm"), 6 * h + j + 1)
                if h:
                    dve.wait_ge(sem("wr_used"), 6 * (h - 1) + j + 1)
                m = DECAY[h % 2][:, S - P - P * j:TOEP - P * j] if j < 4 else DECAY_X[h % 2][:, j - 4, :]
                dve.tensor_tensor(w_r[:, j, :], bank[j][:, :], m, ALU.mult).then_inc(sem("wr_done"), 1)
            if h < 3:
                context_decays(h + 1)
            if h < 2:
                dve.wait_ge(sem("wr_done"), 6 * h + 6)
                arguments(h + 2)
            if h == 0:
                dve.wait_ge(sem("croot"), 1)
            own(dve.tensor_tensor(conv_c[:, h, :], conv_c[:, h, :], c_mean, ALU.subtract))
            dve.scalar_tensor_tensor(conv_c[:, h, :], conv_c[:, h, :], c1("ln_w", h), c_root, ALU.mult, ALU.mult)\
               .then_inc(sem("c_norm"), 1)
            if h >= 1:
                conv_lower(h - 1)
            if h >= 2:
                head_norm(h - 2)
        head_out(3)
        conv_lower(3)
        head_norm(2)
        head_norm(3)

        def add_gated(name, m0, what):
            def free(g, b, i):
                r = res[:, ds(g, 1), :]
                dve.scalar_tensor_tensor(r, bank[b][:, :], mod[:, ds(g + m0, 1)], r, ALU.mult, ALU.add).then_inc(ev_dve, 1)
                add_square(what, g, b % 2)
            own(dve.memset(total, 0.0))
            stage(name, free)
        add_gated("even_out", 16, "ffn0")

        def ffn(i):
            dve.wait_ge(ev_dve, LEAD + EV[f"up{i}"][1]["dve"])
            norm(lambda k: res[:, k, :], lambda k: coef[:, 2 * i + 1, k:k + 1], shift=shift(48 * i + 24))
            g0, before = GROUP0[f"up{i}"], EV[f"up{i}"][1]
            with dve.Fori(0, FF // 2) as j:
                for s in range(2):
                    n = 2 * j + s
                    dve.wait_ge(mm_done, 3 + g0 + 2 * n)
                    dve.wait_ge(ev_act, LEAD + before["act"] + n + 1)
                    dve.wait_ge(sem("hid_l"), FF * i + n + 1)
                    dve.tensor_tensor(tt[:, s, :], bank[2 * s + 1][:, :], sq[:, s, :], ALU.mult).then_inc(ev_dve, 1)
                    dve.wait_ge(sem("hid_h"), FF * i + n + 1)
                    dve.tensor_tensor(hid_lo[:, ds(n, 1), :], tt[:, s, :], hid_hi[:, ds(n, 1), :].bitcast(F32), ALU.subtract)\
                       .then_inc(sem("hid_l"), 1)
            g0 = GROUP0[f"down{i}"]
            m0 = 48 * i + 40
            own(dve.memset(total, 0.0))
            with dve.Fori(0, 4) as j:
                for b in range(2):
                    dve.wait_ge(mm_done, 4 * j + (g0 + 2 * b + 3))
                    r = res[:, ds(2 * j + b, 1), :]
                    dve.scalar_tensor_tensor(r, bank[b][:, :], mod[:, ds(2 * j + (b + m0), 1)], r, ALU.mult, ALU.add)\
                       .then_inc(ev_dve, 1)
                    add_square(("pool", "final")[i], 2 * j + b, 0)
        dve.sem_inc(sem("hid_l"), 2)
        ffn(0)

        own(dve.memset(pc[:, :, 0:8], 0.0))
        own(dve.memset(pc[:, :, 8 + S:PW], 0.0))
        dve.sem_inc(sem("pad3_ready"), 1)
        dve.wait_ge(ev_dve, LEAD + EV["pool"][1]["dve"])
        norm(lambda k: res[:, k, :], lambda k: coef[:, 2, k:k + 1], shift=shift(48))
        dve.wait_ge(sem("odd_in"), 64)
        for g, w in enumerate((2, 4, 8, 16)):
            dve.wait_ge(ev_act, LEAD + EV["pool"][1]["act"] + g + 1)
            src, n = pc[:, g, :], PW
            for step in range(g + 1):
                dst = (pool_a, pool_b)[step % 2][:, g, :]
                n -= 1 << step
                own(dve.tensor_tensor(dst[:, 0:n], src[:, 0:n], src[:, (1 << step):(1 << step) + n], ALU.add))
                src = dst
            own(dve.tensor_tensor(src[:, 8 - w // 2:8 - w // 2 + S], src[:, 8 - w // 2:8 - w // 2 + S], inv_t[:, g, :], ALU.mult))
            dve.tensor_tensor(pc[:, g, 8:8 + S], src[:, 8 - w // 2:8 - w // 2 + S], pc[:, g, 8:8 + S], ALU.subtract).then_inc(sem("m_ready"), 1)
        for t in range(4):
            dve.wait_ge(ev_act, LEAD + EV["v_s"][1]["act"] + 5 + t)
            own(dve.bn_stats(bn[:, t, 0:6], v_s[:, t, :]))
            own(dve.bn_aggr(bn[:, t, 6:8], bn[:, t, 0:6]))
            v = v_s[:, t, :]
            own(dve.scalar_tensor_tensor(v, v, bn[:, t, 6:7], sg_r[:, 0, :], ALU.subtract, ALU.mult))
        own(dve.tensor_scalar(bn[:, :, 7:8], bn[:, :, 7:8], EPS, None, ALU.add))
        dve.sem_inc(sem("sg_var"), 1)
        for g in range(4):
            dve.wait_ge(sem("omix_hi"), g + 1)
            dve.scalar_tensor_tensor(x_lo[:, g, :], bank[4 + g % 2][:, :], c1("pool_scale", g), x_hi[:, g, :].bitcast(F32), ALU.mult, ALU.subtract)\
               .then_inc(sem("omix_lo"), 1)
        dve.wait_ge(sem("sg_root"), 1)
        own(dve.reciprocal(bn[:, :, 9:10], bn[:, :, 8:9]))
        for t in range(4):
            v = v_s[:, t, :]
            dve.scalar_tensor_tensor(v, v, bn[:, t, 9:10], sg_r[:, 1, :], ALU.mult, ALU.add).then_inc(sem("v_norm"), 1)
        for g in range(4):
            dve.wait_ge(sem("sg_mm"), g + 1)
            if g >= 2:
                dve.wait_ge(sem("omix_lo"), 4 + g - 1)
            t3 = tt[:, g % 2, :].rearrange("p (n q) -> p n q", q=P)
            own(dve.tensor_tensor(t3, bank[6 + g % 2][:, :].rearrange("p (n q) -> p n q", q=P),
                                  sg_r[:, 2, P * g:P * g + P].unsqueeze(1).to_broadcast([P, 4, P]), ALU.add))
            dve.tensor_tensor(tt[:, g % 2, :], tt[:, g % 2, :], u_s[:, g, :], ALU.mult).then_inc(sem("omix_f"), 1)
            dve.wait_ge(sem("omix_hi"), 5 + g)
            dve.tensor_tensor(x_lo[:, 4 + g, :], tt[:, g % 2, :], x_hi[:, 4 + g, :].bitcast(F32), ALU.subtract).then_inc(sem("omix_lo"), 1)
        add_gated("odd_out", 64, "ffn1")
        ffn(1)
        norm(lambda k: res[:, k, :], lambda k: c1("g_final", k), into=lambda k: res[:, k, :], into_ready="out_ready")

    @block.tensor
    def _(pe):
        pe.sem_inc(mm_done, 1)
        pe.sem_inc(sem("vg_mm"), 4)

        def three(dst, wh, wl, xh, xl, first, last):
            pe.matmul(dst, wh, xh, start=first, stop=False)
            pe.matmul(dst, wh, xl, start=False, stop=False)
            return pe.matmul(dst, wl, xh, start=False, stop=last)

        def bank_free(name, g, q):
            by, before = EV[name]
            own_, other = (ev_act, ev_dve) if by == "act" else (ev_dve, ev_act)
            pe.wait_ge(own_, LEAD + before[by] + g - 3)
            pe.wait_ge(other, LEAD + before["dve" if by == "act" else "act"] - max(3 - q, 0))

        def begin(name):
            pe.wait_ge(ev_act, LEAD + EV[name][1]["act"])
            pe.wait_ge(ev_dve, LEAD + EV[name][1]["dve"])

        def stage(name, xh=x_hi, xl=x_lo, kts=KT, behind_by_one=None, ready=None, first=0):
            n0, per = FIRST[name], PER[name]
            blocks_ = COUNT[name]

            order = [(first + k) % kts for k in range(kts)]

            def group(m, s, wh, wl, ks):
                for k in ks:
                    last = three(bank[(per * s + m) % 4][:, :], wh[:, k, P * m:P * m + P], wl[:, k, P * m:P * m + P],
                                 xh[:, k, :], xl[:, k, :], k == order[0], k == order[-1])
                if k == order[-1]:
                    last.then_inc(mm_done, 1)

            def pair(i):
                for s in range(2):
                    pe.wait_ge(lo_done, n0 + 2 * i + s + 1)
                    wh = w_hi[:, s, :].rearrange("p (k n) -> p k n", k=kts)
                    wl = w_lo[:, s, :].rearrange("p (k n) -> p k n", k=kts)
                    together = ready is not None and s == 0
                    for m in range(per):
                        bank_free(name, per * (2 * i + s) + m, per * s + m)
                        if not together:
                            group(m, s, wh, wl, order)
                            if behind_by_one:
                                behind_by_one(i, m + 1)
                    if together:
                        for k in order:
                            if k < (ready + (KT,))[2]:
                                pe.wait_ge(ready[0], ready[1] + k + 1)
                            for m in range(per):
                                group(m, s, wh, wl, (k,))
                    if behind_by_one:
                        behind_by_one(i, 3 * s)
            if blocks_ > 2:
                with pe.Fori(0, blocks_ // 2) as i:
                    pair(i)
            else:
                pair(0)

        def norm(what, n=S):
            v, at = NORM[what], SQ_AT[what]
            if v:
                pe.wait_ge(sem("var_ready"), v)
            if SUMMED[what]:
                pe.wait_ge(sem("sq_used"), at + 8)
                pe.matmul(bank[4][:, :n], ones[:, :], tt[:, 0, :n], start=True, stop=True).then_inc(sem("sq_used"), 1)
                return
            for k in range(KT):
                pe.wait_ge(sem("sq_ready"), 8 * v + k + 1)
                pe.matmul(bank[4][:, :n], ones[:, :], sq[:, k % 2, :n], start=(k == 0), stop=(k == KT - 1))\
                  .then_inc(sem("sq_used"), 1)

        pe.wait_ge(sem("ones_ready"), 1)
        norm("first")

        def x_m_values(i, b):
            g = 4 * i + b
            pe.wait_ge(sem("fold_ready"), 1)
            pe.wait_ge(sem("bd_in"), 16)
            pe.wait_ge(ev_act, LEAD + g + 1)
            pe.wait_ge(sem("vg_done"), g - 1 + 2)
            for t in range(4):
                last = pe.matmul(bank[4 + 2 * (b % 2) + t // 2][:, 136 * (t % 2):136 * (t % 2) + 136],
                                 conv_in[:, b, 3 + P * t:3 + P * t + P], v_w[:, ds(g, 1), :], start=True, stop=True)
            last.then_inc(sem("vg_mm"), 1)
        pe.sem_inc(sem("vg_done"), 2)
        stage("x_m", behind_by_one=x_m_values, ready=(sem("xl_ready"), 0))

        def query_key(h, parts):
            for j in parts:
                if j == 0:
                    pe.wait_ge(sem("bd_ready"), 16 * h + 16)
                    if h:
                        pe.wait_ge(sem("hvar_ready"), h)
                if j >= 2:
                    pe.wait_ge(sem("qk_ev"), 8 * h + j - 1)
                last = pe.matmul(bank[4 + j % 2][:, :], bd[:, j % 4, j // 4, :], x_c[:, 4 * h + j % 4, :], start=True, stop=True)
                last.then_inc(sem("qk_mm"), 1)

        pe.wait_ge(ev_act, LEAD + EV["o_m0"][1]["act"])
        for g in range(16):
            pe.wait_ge(sem("xc_ready"), 4 + g + 1)
            last = pe.matmul(bank[0][0:8, :], w_g[:, g, :], x_c[:, g, :], start=(g == 0), stop=(g == 15))
        last.then_inc(sem("grow_mm"), 1)
        pe.wait_ge(sem("vg_done"), 2 + 16)
        query_key(0, range(4))
        pe.wait_ge(sem("grow_out"), 1)
        for t in range(4):
            last = pe.transpose(bank[7][:, 8 * t:8 * t + 8], sq[0:8, 0, P * t:P * t + P], ident[0:8, 0:8])
        last.then_inc(sem("gates_mm"), 1)
        query_key(0, range(4, 8))
        pe.wait_ge(sem("lf_ready"), 1)
        for t in range(4):
            for s in range(t + 1):
                last = pe.matmul(bank[6][:, 64 + 4 * t:68 + 4 * t], (tri if s == t else ones[:, :]), lf[:, s, :],
                                 start=(s == 0), stop=(s == t))
        last.then_inc(sem("b_mm"), 1)
        pe.wait_ge(sem("u_ready"), 1)
        for t in range(4):
            pe.transpose(bank[6][0:4, P * t:P * t + P], u_c[:, t, :], ident)
            last = pe.transpose(bank[7][0:4, P * t:P * t + P], b_c[:, t, :], ident)
        last.then_inc(sem("rows_mm"), 1)

        for h in range(4):
            if h:
                query_key(h, range(8))
            if h == 0:
                pe.wait_ge(sem("rows_ready"), 1)
            pe.matmul(bank[6][:, :], ident[0:4, h:h + 1].to_broadcast([4, P]), rows[0:4, :], start=True, stop=True)
            pe.matmul(bank[7][:, :], ident[32:36, 32 + h:33 + h].to_broadcast([4, P]), rows[32:36, :], start=True, stop=True)\
              .then_inc(sem("bc_mm"), 1)
            pe.wait_ge(sem("qk_ev"), 8 * h + 8)
            for j in range(4):
                if j >= 2:
                    pe.wait_ge(sem("pt_done"), 4 * h + j - 1)
                for c in range(4):
                    last = pe.matmul(bank[4 + j % 2][:, :S - P * j], k_t[:, c, P * j:P * j + P], q_t[:, c, P * j:S],
                                     start=(c == 0), stop=(c == 3))
                last.then_inc(sem("s_mm"), 1)
            stage(f"o_m{h}")
            pe.wait_ge(sem("nm_ready"), h + 1)
            pe.wait_ge(sem("pt_done"), 4 * h + 4)
            for j in range(4):
                last = pe.matmul(bank[6][:, P * j:S], ones[:, :], p_t[:, j, :S - P * j], start=(j == 0), stop=(j == 3))
            last.then_inc(sem("den_mm"), 1)
            for e in range(4):
                if e == 3:
                    pe.wait_ge(sem("abs_done"), h + 1)
                for j in range(4):
                    last = pe.matmul(bank[HB[e]][:, P * j:S], v_m[:, j, P * (4 * h + e):P * (4 * h + e) + P],
                                     p_t[:, j, :S - P * j], start=(j == 0), stop=(j == 3))
                last.then_inc(sem("h_mm"), 1)
            pe.wait_ge(sem("h_added"), h + 1)
            pe.matmul(bank[4][:, :], ones[:, :], tt[:, 0, :], start=True, stop=True)
            pe.matmul(bank[5][:, :], ones[:, :], tt[:, 1, :], start=True, stop=True).then_inc(sem("sum_mm"), 1)
            stage(f"z_m{h}")
            stage(f"w_pb{h}", y_hi, y_lo, kts=4, ready=(sem("y_done"), 4 * h))

        pe.wait_ge(sem("rel_in"), 32)
        pe.wait_ge(sem("rel_one"), 1)
        pe.matmul(bank[4][0:16, :], rel_sb[:, :], hot_sb[:, 0:S], start=True, stop=True)
        pe.matmul(bank[5][0:16, 0:P], rel_sb[:, :], hot_sb[:, S:], start=True, stop=True).then_inc(sem("bias_mm"), 1)
        stage("q_a")
        stage("k_a")

        def stage_tokens(name):
            n0 = FIRST[name]

            def pair(i):
                for s in range(2):
                    pe.wait_ge(lo_done, n0 + 2 * i + s + 1)
                    wh = w_hi[:, s, :].rearrange("p (k n) -> p k n", k=KT)
                    wl = w_lo[:, s, :].rearrange("p (k n) -> p k n", k=KT)
                    for t in range(4):
                        bank_free(name, 4 * (2 * i + s) + t, 4 * s + t)
                        for k in range(KT):
                            c = slice(P * t, P * t + P)
                            d = bank[t][:, 0:256]
                            pe.matmul(d, x_hi[:, k, c], wh[:, k, :], start=(k == 0), stop=False)
                            pe.matmul(d, x_hi[:, k, c], wl[:, k, :], start=False, stop=False)
                            last = pe.matmul(d, x_lo[:, k, c], wh[:, k, :], start=False, stop=(k == KT - 1))
                        last.then_inc(mm_done, 1)
            if COUNT[name] > 2:
                with pe.Fori(0, COUNT[name] // 2) as i:
                    pair(i)
            else:
                pair(0)
        stage_tokens("v_a")
        begin("z_a")

        def head(h):
            return slice(64 * (h % 2), 64 * (h % 2) + 64), h // 2
        def values(h):
            pe.wait_ge(sem("pc_act"), h + 1)
            pe.wait_ge(sem("pc_dve"), h + 1)
            if h:
                pe.wait_ge(sem("ya_done"), h)
            for i in range(4):
                for j in range(i + 1):
                    o = PC_AT[j] + P * (i - j)
                    last = pe.matmul(bank[7][:, 64 * i:64 * i + 64], p_c[:, o:o + P], v_a[:, j, 64 * h:64 * h + 64],
                                     start=(j == 0), stop=(j == i))
            last.then_inc(sem("pv_mm"), 1)

        pe.wait_ge(sem("bias_ready"), 1)
        for h in range(-1, 16):
            if h + 1 < 16:
                r, c = head(h + 1)
                if h >= 0:
                    pe.wait_ge(sem("max_ready"), h + 1)
                for i in range(4):
                    n = P * (i + 1)
                    last = pe.matmul(bank[SB[i]][:, SO[i]:SO[i] + n], q_a[r, c, P * i:P * i + P], k_a[r, c, 0:n], start=True, stop=True)
                last.then_inc(sem("qk_a_mm"), 1)
            if h >= 1:
                values(h - 1)
            if h >= 0:
                pe.wait_ge(sem("p_done"), h + 1)
                for j, (b, o) in enumerate(((4, 0), (5, 0), (6, 0), (6, 256))):
                    for i in range(j, 4):
                        last = pe.transpose(bank[b][:, o + P * (i - j):o + P * (i - j) + P],
                                            p_r[:, TRI_AT[i] + P * j:TRI_AT[i] + P * j + P], ident)
                    if j != 2:
                        last.then_inc(sem("t_mm"), 1)
        values(15)
        pe.wait_ge(sem("ya_done"), 16)
        stage("z_a")
        for c in range(8):
            if c >= 3:
                pe.wait_ge(sem("yz_f"), c - 2)
            for t in range(4):
                last = pe.transpose(bank[4 + c % 3][:, P * t:P * t + P], y_a[:, t, P * c:P * c + P], ident)
            last.then_inc(sem("yt_mm"), 1)
        stage("gate_a")
        pe.wait_ge(sem("yz_l"), 8)
        stage("w_pa", yz_hi, yz_lo)
        stage("gate_m")
        stage("w_out", yz_hi, yz_lo, ready=(sem("mrg_lo"), 0))
        begin("a_e")
        norm("out")

        norm("even")
        stage("a_e", ready=(sem("xl_ready"), 8))
        norm("ctx", CTX)
        stage("b_e")
        stage("q_r")

        pe.wait_ge(sem("xl_ready"), 24)
        for s in range(2):
            pe.wait_ge(lo_done, FIRST["k_r"] + s + 1)
            wh = w_hi[:, s, :].rearrange("p (k n) -> p k n", k=KT)
            wl = w_lo[:, s, :].rearrange("p (k n) -> p k n", k=KT)
            for m in range(2):
                for j, (xh, xl, n) in enumerate(((x_hi, x_lo, S), (c_hi, c_lo, CTX))):
                    bank_free("k_r", 4 * s + 2 * m + j, 4 * s + 2 * m + j)
                    for k in range(KT):
                        last = three(bank[2 * m + j][:, :n], wh[:, k, P * m:P * m + P], wl[:, k, P * m:P * m + P],
                                     xh[:, k, :], xl[:, k, :], k == 0, k == KT - 1)
                    last.then_inc(mm_done, 1)
        for s in range(2):
            pe.wait_ge(lo_done, FIRST["v_r"] + s + 1)
            wh = w_hi[:, s, :].rearrange("p (k n) -> p k n", k=KT)
            wl = w_lo[:, s, :].rearrange("p (k n) -> p k n", k=KT)
            for t in range(6):
                bank_free("v_r", 6 * s + t, 6 * s + t)
                d = bank[(6 * s + t) % 4][:, 0:256]
                ah, al = (x_hi, x_lo) if t < 4 else (c_hi, c_lo)
                c = slice(P * (t % 4), P * (t % 4) + P)
                for k in range(KT):
                    last = three(d, ah[:, k, c], al[:, k, c], wh[:, k, :], wl[:, k, :], k == 0, k == KT - 1)
                last.then_inc(mm_done, 1)
        stage("g_r")
        pe.wait_ge(sem("conv_made"), 4)
        for c in range(4):
            pe.matmul(bank[6][:, :], ones[:, :], conv_c[:, c, :], start=(c == 0), stop=(c == 3))
        for c in range(4):
            pe.wait_ge(sem("csq"), c + 1)
            pe.matmul(bank[7][:, :], ones[:, :], sq[:, c % 2, :], start=(c == 0), stop=(c == 3)).then_inc(sem("csq_mm"), 1)

        def scores(h, j):
            key = k_r[:, h, P * j:P * j + P] if j < 4 else k_x[:, h, P * (j - 4):P * (j - 4) + P]
            pe.matmul(bank[j][:, :], key, q_r[:, h, :], start=True, stop=True).then_inc(sem("sr_mm"), 1)

        def square_sum(h):
            pe.wait_ge(sem("ysq"), h + 1)
            if h:
                pe.wait_ge(sem("yvar"), h)
            pe.matmul(bank[7][:, :], ones[:, :], sq[:, h % 2, :], start=True, stop=True).then_inc(sem("ysq_mm"), 1)
        pe.wait_ge(sem("roped"), 12)
        begin("even_out")
        for j in range(6):
            scores(0, j)
        pe.wait_ge(sem("cvar"), 1)
        for h in range(4):
            for j in range(6):
                pe.wait_ge(sem("wr_done"), 6 * h + j + 1)
                if h < 3:
                    scores(h + 1, j)
                if h and j == 0:
                    pe.wait_ge(sem("y_out"), h)
                v = v_r[:, j, P * h:P * h + P] if j < 4 else v_x[:, j - 4, P * h:P * h + P]
                last = pe.matmul(bank[6][:, :], v, w_r[:, j, :], start=(j == 0), stop=(j == 5))
                last.then_inc(sem("wr_used"), 1)
                if h and j == 2:
                    square_sum(h - 1)
        square_sum(3)
        pe.wait_ge(sem("cmix_lo"), 4)
        stage("even_out", ready=(sem("mix_lo"), 0, 4), first=4)

        def ffn(i):
            norm(f"ffn{i}")
            name = f"up{i}"
            begin(name)
            n0, before = FIRST[name], EV[name][1]
            with pe.Fori(0, FF // 2) as j:
                for s in range(2):
                    n = 2 * j + s
                    pe.wait_ge(lo_done, n + (n0 + 1))
                    pe.wait_ge(ev_act, n + (LEAD + before["act"] - 1))
                    pe.wait_ge(ev_dve, n + (LEAD + before["dve"] - 1))
                    for part in range(KT if s == 0 else 2):
                        if s == 0:
                            pe.wait_ge(sem("xl_ready"), 8 * (3, 5)[i] + part + 1)
                        for k, m in ([(part, 0), (part, 1)] if s == 0 else [(k, part) for k in range(KT)]):
                            o = 256 * k + P * m
                            last = three(bank[2 * s + m][:, :], w_hi[:, s, o:o + P], w_lo[:, s, o:o + P],
                                         x_hi[:, k, :], x_lo[:, k, :], k == 0, k == KT - 1)
                            if k == KT - 1:
                                last.then_inc(mm_done, 1)
            name = f"down{i}"
            pe.wait_ge(ev_act, LEAD + EV[name][1]["act"] - 1)
            pe.wait_ge(ev_dve, LEAD + EV[name][1]["dve"] - 1)
            n0, before = FIRST[name], EV[name][1]["dve"]
            with pe.Fori(0, 4) as j:
                for b in range(2):
                    pe.wait_ge(ev_dve, 2 * j + (LEAD + before + b - 1))
                    for s in range(2):
                        pe.wait_ge(lo_done, 4 * j + (n0 + 2 * b + s + 1))
                        pe.wait_ge(sem("hid_l"), 2 + FF * i + FF // 2 * (s + 1))
                        for k in range(FF // 2):
                            last = three(bank[b][:, :], w_hi[:, s, P * k:P * k + P], w_lo[:, s, P * k:P * k + P],
                                         hid_hi[:, FF // 2 * s + k, :], hid_lo[:, FF // 2 * s + k, :],
                                         s == 0 and k == 0, s == 1 and k == FF // 2 - 1)
                        last.then_inc(mm_done, 1)
        ffn(0)

        norm("pool")
        begin("pool")
        stage("pool", ready=(sem("xl_ready"), 32))
        stage("u_s")
        stage_tokens("v_s")
        pe.wait_ge(sem("odd_in"), 64)
        for g in range(4):
            pe.wait_ge(sem("m_ready"), g + 1)
            if g >= 2:
                pe.wait_ge(sem("omix_lo"), g - 1)
            pe.matmul(bank[4 + g % 2][:, :], pool_ws[:, g, :], pc[:, g, 8:8 + S], start=True, stop=True).then_inc(sem("pool_mm"), 1)
        for g in range(4):
            if g >= 2:
                pe.wait_ge(sem("omix_f"), g - 1)
            for n in range(4):
                if g == 0:
                    pe.wait_ge(sem("v_norm"), n + 1)
                last = pe.matmul(bank[6 + g % 2][:, P * n:P * n + P], v_s[:, n, P * g:P * g + P], sg_ws[:, g, :], start=True, stop=True)
            last.then_inc(sem("sg_mm"), 1)
        stage("odd_out", ready=(sem("omix_lo"), 0))
        ffn(1)
        norm("final")
def rope_table(seq, row, col):
    parts = []
    for p, n in zip((seq, row, col), ROPE_PAIRS):
        freq = np.float32(10000.0) ** (-np.arange(n, dtype=np.float32) / np.float32(n))
        parts.append(freq[:, None] * p[None, :].astype(np.float32))
    ang = np.concatenate(parts, 0)
    return np.concatenate([np.cos(ang), np.cos(ang)], 0), np.concatenate([-np.sin(ang), np.sin(ang)], 0)


def shape_tables():
    f = np.float32
    p = np.arange(P)
    dist = S - 1 - np.arange(S + P)
    d0 = np.maximum(dist, 0)
    large = 16 + (np.log(np.maximum(d0, 16).astype(f) / f(16)) / f(math.log(128.0)) * f(16)).astype(np.int32)
    bucket = np.where(d0 < 16, d0, np.minimum(large, 31))
    times = 1 * (d0 <= 128) + 1 * (d0 % 4 == 0) + 1 * (d0 % 16 == 0)
    hot = np.zeros((33, S + P), f)
    hot[bucket, np.arange(S + P)] = 1.0
    hot[32] = np.where((dist >= 0) & (times > 0), np.log(np.maximum(times, 1)), -1e30)
    t = np.arange(S)
    x_cos, x_sin = rope_table(np.full(S, float(CTX), f), t // 64, t % 64)
    c_cos, c_sin = rope_table(np.arange(CTX), np.zeros(CTX), np.zeros(CTX))
    inv = np.zeros((4, S), f)
    for g, w in enumerate((2, 4, 8, 16)):
        lo, hi = np.clip(t - w // 2, 0, S - 1), np.clip(t + w - 1 - w // 2, 0, S - 1)
        inv[g] = 1.0 / (hi - lo + 1)
    square = np.stack([np.eye(P, dtype=f), (p[:, None] <= p[None, :]).astype(f),
                       np.where(p[None, :] >= p[:, None], 0.0, -1e30).astype(f)], 1)
    diff = (np.arange(TOEP)[None, :] - (S - P) - p[:, None]).astype(f)
    return dict(square=square, hot=hot, diff=diff,
                rope_x=np.stack([x_cos, x_sin], 1).astype(f), rope_c=np.stack([c_cos, c_sin], 1).astype(f),
                inv=np.ascontiguousarray(np.broadcast_to(inv[None], (P, 4, S))))


def column_pack(v):
    col = lambda a: np.asarray(a).reshape(-1, P).T
    row = lambda a: np.broadcast_to(np.asarray(a).reshape(1, -1), (P, np.asarray(a).size))
    parts = {
        "g_in": col(v["norm_in_g"]), "g_out": col(v["norm_out_g"]), "gate_b": col(v["gate_b"]),
        "conv_w": v["conv_w"][0].reshape(4, 16, P).transpose(2, 1, 0).reshape(P, 64),
        "conv_b": col(v["conv_b"]), "g_head": col(v["head_norm_g"]), "skip": col(v["skip_m"]),
        "b_if": row(v["b_if"]),
        "ada_b": col(v["ada_b_2"]), "norm_w": col(v["norm_w_2"]), "decay": row(v["ret_decay_logit_2"]),
        "conv2_w": v["conv_dw_w_2"][0].reshape(31, 4, P).transpose(2, 1, 0).reshape(P, 124),
        "ln_w": col(v["conv_ln_w_2"]), "ln_b": col(v["conv_ln_b_2"]),
        "pool_scale": col(v["pool_scale_2"]), "g_final": col(v["final_norm_w_2"]),
    }
    assert {k: a.shape[1] for k, a in parts.items()} == WIDTHS
    return np.ascontiguousarray(np.concatenate(list(parts.values()), 1))


def weight_blocks(v):
    def cols(w, lo, hi, k=8):
        n = 2048 // k
        w = w[:, lo:hi].reshape(k, P, (hi - lo) // n, n)
        return w.transpose(2, 1, 0, 3).reshape(-1, P, 2048)
    w_in, even, odd = v["w_in"][0], v["even_w_in_2"][0], v["odd_w_in_2"][0]
    out = [cols(w_in, 4096, 6144)]
    for h in range(4):
        o = 512 * h
        out += [cols(w_in, 8192 + o, 8704 + o), cols(w_in, 6144 + o, 6656 + o), cols(v["w_pb"][0][o:o + 512], 0, 1024, 4)]
    out += [cols(w_in, 0, 3072), cols(w_in, 3072, 4096), cols(w_in, 10240, 11264), cols(v["w_pa"][0], 0, 1024),
            cols(w_in, 11264, 12288), cols(v["w_out"][0], 0, 1024)]
    out += [cols(even, 2048, 3072), cols(even, 0, 2048), cols(v["even_w_out_2"][0], 0, 1024)]

    def ffn(i):
        gate, up, down = v["ffn_w_gate_2"][i], v["ffn_w_up_2"][i], v["ffn_w_down_2"][i]
        both = np.stack([gate.reshape(8, P, 22, P), up.reshape(8, P, 22, P)], 3)
        d = down.reshape(2, 11, P, 8, P).transpose(3, 0, 2, 1, 4).reshape(16, P, 1408)
        full = np.zeros((16, P, 2048), d.dtype)
        full[:, :, :1408] = d
        return [both.transpose(2, 1, 0, 3, 4).reshape(22, P, 2048), full]
    out += ffn(0)
    out += [cols(odd, 0, 1536), cols(v["odd_w_out_2"][0], 0, 1024)]
    out += ffn(1)
    return np.concatenate(out, 0)


def block_diagonal(w):
    out = np.zeros((16, 32, 4, 32, 4), w.dtype)
    b = np.arange(32)
    out[:, b, :, b, :] = w.reshape(16, 32, 4, 4).transpose(1, 0, 2, 3)
    return out.reshape(16, P, P)


def lay_out(v):
    tiles = lambda a, n: np.ascontiguousarray(a.T.reshape(8, P, n).transpose(1, 0, 2))
    q, k, w = (block_diagonal(v[n][0]) for n in ("wq_m", "wk_m", "wv_m"))
    qk = np.stack([q, k], 1).reshape(4, 4, 2, P, P).transpose(3, 0, 1, 2, 4).reshape(P, 4, 1024)
    four = np.stack([v[n][0].reshape(16, P, 4) for n in ("wq_m", "wk_m", "wv_m")])
    fold = np.repeat(v["w_if"][0].reshape(3, 16, 32, 1, 4, 8), 4, 3).reshape(3, 16, P, 4, 8)
    ada = v["ada_w_2"].transpose(0, 2, 1).reshape(96, P, D)
    order = [m for n in range(8) for m in (2 * n, 2 * n + 1, 16 + n)] + list(range(24, 96))
    ada = ada[order]
    return dict(
        xt=tiles(v["x"][0], S), ctxt=tiles(v["ctx_2"][0], CTX), cols=column_pack(v), blocks=weight_blocks(v),
        bd_qk=np.ascontiguousarray(qk), bd_v=np.ascontiguousarray(w.transpose(1, 0, 2)),
        fold_w=np.ascontiguousarray(fold.transpose(2, 0, 1, 4, 3)).reshape(P, 3, P, 4),
        fold_c=np.ascontiguousarray(four.transpose(2, 0, 1, 3)),
        c_rows=np.ascontiguousarray(np.broadcast_to(np.stack([v["c_2"].reshape(-1), v["c_ctx_2"].reshape(-1)])[None], (P, 2, D))),
        sg_rows=np.ascontiguousarray(np.broadcast_to(np.stack([v["sg_ln_w_2"].reshape(-1), v["sg_ln_b_2"].reshape(-1),
                                                               v["sg_b_2"].reshape(-1)])[None], (P, 3, 512))),
        rel=np.ascontiguousarray(v["rel_bias"]), ada=np.ascontiguousarray(ada),
        pool_w=np.ascontiguousarray(v["pool_w_2"][0].transpose(1, 0, 2)),
        sg_w=np.ascontiguousarray(v["sg_w_2"][0].transpose(2, 0, 1)), **shape_tables())


def kernel(**inputs):
    import concourse.bacc as bacc
    from concourse.bass_utils import run_bass_kernel_spmd

    nc = bacc.Bacc("TRN2", target_bir_lowering=False, num_devices=1)
    arrays = lay_out({k: np.asarray(v) for k, v in inputs.items()})
    aps = {k: nc.dram_tensor(k, a.shape, F32, kind="ExternalInput").ap() for k, a in arrays.items()}
    aps["out"] = nc.dram_tensor("out", (D, S), F32, kind="ExternalOutput").ap()
    program(nc, **aps)
    r = run_bass_kernel_spmd(nc, [arrays], core_ids=[0])
    return np.ascontiguousarray(r.results[0]["out"].T)[None]
```
